# Optimizing a Trainium2 kernel written in Bass

```python
import math
import jax
import jax.numpy as jnp
from jax import lax
import numpy as np

D_MODEL = 1024
BATCH = 1
SEQ = 1024
DEPTH = 2

GRID_W = 64
CTX_LEN = 256
MIX_WIDTH = 2 * D_MODEL
S5_WIDTH = MIX_WIDTH // 2
RG_WIDTH = MIX_WIDTH - S5_WIDTH
IN_WIDTH_EVEN = 2 * S5_WIDTH + 2 * RG_WIDTH
S5_GROUP = 16
S5_GROUPS = S5_WIDTH // S5_GROUP
S5_STATE = 64
S5_CHUNK = 128
RG_HEADS = 4
RG_HEAD_DIM = RG_WIDTH // RG_HEADS
RG_C = 8.0
CONV_W = 4
ML_WIDTH = MIX_WIDTH
IN_WIDTH_ODD = 2 * ML_WIDTH
ML_HEADS = 4
ML_HEAD_DIM = ML_WIDTH // ML_HEADS
ML_QKV_BLOCK = 4
ML_CHUNK = 64
EPS = 1e-6

kernel_name = 'hybrid_s5_rglru_mlstm_prefix_dit'

def rms_norm(x, g):
    xf = x.astype(jnp.float32)
    y = xf * lax.rsqrt(jnp.mean(xf * xf, axis=-1, keepdims=True) + EPS)
    return (y * g.astype(jnp.float32)).astype(x.dtype)

def centred_dwconv(x, w, b):
    L = x.shape[1]
    left = (CONV_W - 1) // 2
    xp = jnp.pad(x, ((0, 0), (left, CONV_W - 1 - left), (0, 0)))
    y = b + xp[:, 0:L] * w[0]
    for j in range(1, CONV_W):
        y = y + xp[:, j:j + L] * w[j]
    return y

def headwise(x, w):
    nb, bi, bo = w.shape
    y = jnp.einsum('blgi,gio->blgo', x.reshape(x.shape[0], x.shape[1], nb, bi), w)
    return y.reshape(x.shape[0], x.shape[1], nb * bo)

def to_col_major(h, rows):
    bt, L, dm = h.shape
    return h.reshape(bt, rows, GRID_W, dm).transpose(0, 2, 1, 3).reshape(bt, L, dm)

def from_col_major(h, rows):
    bt, L, dm = h.shape
    return h.reshape(bt, GRID_W, rows, dm).transpose(0, 2, 1, 3).reshape(bt, L, dm)

def cmul(ar, ai, br, bi):
    return ar * br - ai * bi, ar * bi + ai * br

def prefix_bidir(scan_fn, ctx_seqs, lat_seqs, p_fwd, p_bwd):
    n_ctx = ctx_seqs[0].shape[1]
    fwd = scan_fn(*[jnp.concatenate([cs, ls], axis=1) for cs, ls in zip(ctx_seqs, lat_seqs)], *p_fwd)
    bwd = scan_fn(*[jnp.concatenate([jnp.flip(cs, 1), jnp.flip(ls, 1)], axis=1) for cs, ls in zip(ctx_seqs, lat_seqs)], *p_bwd)
    y_ctx = fwd[:, :n_ctx] + jnp.flip(bwd[:, :n_ctx], 1)
    y_lat = fwd[:, n_ctx:] + jnp.flip(bwd[:, n_ctx:], 1)
    return y_ctx, y_lat

def s5_scan(u, a_re, a_im, log_dt, b_re, b_im, c_re, c_im):
    f32 = jnp.float32
    bt, L, G, H = u.shape
    a_re, a_im = a_re.astype(f32), a_im.astype(f32)
    b_re, b_im = b_re.astype(f32), b_im.astype(f32)
    c_re, c_im = c_re.astype(f32), c_im.astype(f32)
    P = a_re.shape[-1]
    dt = jnp.exp(log_dt.astype(f32))[:, None]
    dar, dai = dt * a_re, dt * a_im
    mag = jnp.exp(dar)
    ab_re, ab_im = mag * jnp.cos(dai), mag * jnp.sin(dai)
    den = a_re * a_re + a_im * a_im
    nr, ni = ab_re - 1.0, ab_im
    co_re = (nr * a_re + ni * a_im) / den
    co_im = (ni * a_re - nr * a_im) / den
    bb_re = co_re[..., None] * b_re - co_im[..., None] * b_im
    bb_im = co_re[..., None] * b_im + co_im[..., None] * b_re
    k = jnp.arange(1, S5_CHUNK + 1, dtype=f32)[:, None, None]
    pmag = jnp.exp(k * dar)
    pw_re, pw_im = pmag * jnp.cos(k * dai), pmag * jnp.sin(k * dai)
    a_blk_re = jnp.broadcast_to(ab_re, (bt, S5_CHUNK, G, P))
    a_blk_im = jnp.broadcast_to(ab_im, (bt, S5_CHUNK, G, P))
    nc = L // S5_CHUNK
    uc = u.reshape(bt, nc, S5_CHUNK, G, H).transpose(1, 0, 2, 3, 4)

    def combine(e1, e2):
        a1r, a1i, b1r, b1i = e1
        a2r, a2i, b2r, b2i = e2
        ar, ai = cmul(a2r, a2i, a1r, a1i)
        br, bi = cmul(a2r, a2i, b1r, b1i)
        return ar, ai, br + b2r, bi + b2i

    def step(h, u_blk):
        hr, hi = h
        bur = jnp.einsum('btgh,gph->btgp', u_blk, bb_re)
        bui = jnp.einsum('btgh,gph->btgp', u_blk, bb_im)
        _, _, sr, si = lax.associative_scan(combine, (a_blk_re, a_blk_im, bur, bui), axis=1)
        cr, ci = cmul(pw_re, pw_im, hr[:, None], hi[:, None])
        sr, si = sr + cr, si + ci
        y = jnp.einsum('btgp,ghp->btgh', sr, c_re) - jnp.einsum('btgp,ghp->btgh', si, c_im)
        return (sr[:, -1], si[:, -1]), y

    h0 = jnp.zeros((bt, G, P), f32)
    _, y = lax.scan(step, (h0, h0), uc)
    return y.transpose(1, 0, 2, 3, 4).reshape(bt, L, G, H)

def rglru_scan(xc, wa, ba, wx, bx, lam):
    f32 = jnp.float32
    bt, L, W = xc.shape
    xf = xc.astype(f32)
    xh = xf.reshape(bt, L, RG_HEADS, RG_HEAD_DIM)
    r = jax.nn.sigmoid(jnp.einsum('blhi,hij->blhj', xh, wa.astype(f32)).reshape(bt, L, W) + ba.astype(f32))
    ig = jax.nn.sigmoid(jnp.einsum('blhi,hij->blhj', xh, wx.astype(f32)).reshape(bt, L, W) + bx.astype(f32))
    log_a = -RG_C * r * jax.nn.softplus(-lam.astype(f32))
    a = jnp.exp(log_a)
    bterm = jnp.sqrt(-jnp.expm1(2.0 * log_a)) * (ig * xf)

    def combine(e1, e2):
        return e1[0] * e2[0], e2[0] * e1[1] + e2[1]

    _, h = lax.associative_scan(combine, (a, bterm), axis=1)
    return h

def mlstm_scan(q, k, v, w_if, b_if):
    f32 = jnp.float32
    bt, L, nh, dh = q.shape
    e = nh * dh
    q, k, v = q.astype(f32), k.astype(f32), v.astype(f32)
    w_if = w_if.astype(f32)
    g = (q.reshape(bt, L, e) @ w_if[0] + k.reshape(bt, L, e) @ w_if[1]
         + v.reshape(bt, L, e) @ w_if[2] + b_if.astype(f32))
    log_i = g[..., :nh]
    log_f = jax.nn.log_sigmoid(g[..., nh:])
    k = k * (dh ** -0.5)
    nc = L // ML_CHUNK
    chunk = lambda t: t.reshape(bt, nc, ML_CHUNK, nh, dh).transpose(1, 0, 3, 2, 4)
    gchunk = lambda t: t.reshape(bt, nc, ML_CHUNK, nh).transpose(1, 0, 3, 2)
    mask = jnp.tril(jnp.ones((ML_CHUNK, ML_CHUNK), dtype=bool))

    def step(carry, xs):
        cmat, nvec, m = carry
        qc, kc, vc, li, lf = xs
        b = jnp.cumsum(lf, axis=-1)
        dmat = jnp.where(mask, b[..., :, None] - b[..., None, :] + li[..., None, :], -jnp.inf)
        inter = b + m[..., None]
        m_t = jnp.maximum(inter, jnp.max(dmat, axis=-1))
        s = jnp.einsum('bntd,bnsd->bnts', qc, kc) * jnp.exp(dmat - m_t[..., None])
        sc = jnp.exp(inter - m_t)
        num = jnp.einsum('bnts,bnse->bnte', s, vc) + sc[..., None] * jnp.einsum('bntd,bnde->bnte', qc, cmat)
        den = jnp.sum(s, axis=-1) + sc * jnp.einsum('bntd,bnd->bnt', qc, nvec)
        h = num / jnp.maximum(jnp.abs(den), jnp.exp(-m_t))[..., None]
        b_end = b[..., -1]
        g_s = b_end[..., None] - b + li
        m_new = jnp.maximum(b_end + m, jnp.max(g_s, axis=-1))
        decay = jnp.exp(b_end + m - m_new)
        kw = kc * jnp.exp(g_s - m_new[..., None])[..., None]
        c_new = decay[..., None, None] * cmat + jnp.einsum('bnsd,bnse->bnde', kw, vc)
        n_new = decay[..., None] * nvec + jnp.sum(kw, axis=2)
        return (c_new, n_new, m_new), h

    init = (jnp.zeros((bt, nh, dh, dh), f32), jnp.zeros((bt, nh, dh), f32), jnp.zeros((bt, nh), f32))
    _, h = lax.scan(step, init, (chunk(q), chunk(k), chunk(v), gchunk(log_i), gchunk(log_f)))
    return h.transpose(1, 0, 3, 2, 4).reshape(bt, L, nh, dh)

def head_norm(h, g):
    mu = jnp.mean(h, axis=-1, keepdims=True)
    var = jnp.mean(jnp.square(h - mu), axis=-1, keepdims=True)
    y = (h - mu) * lax.rsqrt(var + EPS)
    return y.reshape(h.shape[0], h.shape[1], -1) * g.astype(jnp.float32)

def even_mixer(h_ctx, h_lat, w_in, w_out, a_re, a_im, log_dt, b_re, b_im, c_re, c_im,
               s5_d, glu_w, glu_b, conv_w, conv_b, wa, ba, wx, bx, lam):
    def split_proj(h):
        return jnp.split(h @ w_in, [S5_WIDTH, 2 * S5_WIDTH, 2 * S5_WIDTH + RG_WIDTH], axis=-1)

    u_c, gs_c, xr_c, gr_c = split_proj(h_ctx)
    u_l, gs_l, xr_l, gr_l = split_proj(h_lat)
    grp = lambda u: u.astype(jnp.float32).reshape(u.shape[0], u.shape[1], S5_GROUPS, S5_GROUP)
    s5p = lambda d: (a_re[d], a_im[d], log_dt[d], b_re[d], b_im[d], c_re[d], c_im[d])
    ys_c, ys_l = prefix_bidir(s5_scan, (grp(u_c),), (grp(u_l),), s5p(0), s5p(1))
    rgp = lambda d: (wa[d], ba[d], wx[d], bx[d], lam[d])
    yr_c, yr_l = prefix_bidir(rglru_scan, (centred_dwconv(xr_c, conv_w, conv_b),),
                              (centred_dwconv(xr_l, conv_w, conv_b),), rgp(0), rgp(1))

    def post(ys, u, gs, yr, gr):
        y = ys.reshape(u.shape).astype(u.dtype) + s5_d * u
        y = jax.nn.gelu(y)
        y = y * jax.nn.sigmoid(y @ glu_w + glu_b)
        a_out = y * jax.nn.silu(gs)
        b_out = yr.astype(gr.dtype) * jax.nn.silu(gr)
        return jnp.concatenate([a_out, b_out], axis=-1) @ w_out

    return post(ys_c, u_c, gs_c, yr_c, gr_c), post(ys_l, u_l, gs_l, yr_l, gr_l)

def odd_mixer(h_ctx, h_lat, w_in, w_out, conv_w, conv_b, wq, wk, wv, w_if, b_if, norm_g, skip):
    def pre(h):
        xm, zg = jnp.split(h @ w_in, [ML_WIDTH], axis=-1)
        xcv = jax.nn.silu(centred_dwconv(xm, conv_w, conv_b))
        heads = lambda t: t.reshape(t.shape[0], t.shape[1], ML_HEADS, ML_HEAD_DIM)
        return xcv, zg, heads(headwise(xcv, wq)), heads(headwise(xcv, wk)), heads(headwise(xm, wv))

    xcv_c, z_c, q_c, k_c, v_c = pre(h_ctx)
    xcv_l, z_l, q_l, k_l, v_l = pre(h_lat)
    hm_c, hm_l = prefix_bidir(mlstm_scan, (q_c, k_c, v_c), (q_l, k_l, v_l),
                              (w_if[0], b_if[0]), (w_if[1], b_if[1]))

    def post(hm, xcv, zg):
        hn = head_norm(hm, norm_g).astype(xcv.dtype)
        return ((hn + skip * xcv) * jax.nn.silu(zg)) @ w_out

    return post(hm_c, xcv_c, z_c), post(hm_l, xcv_l, z_l)

def setup_inputs(seed: int = 0) -> dict:
    key = jax.random.key(seed)
    ks = iter(jax.random.split(key, 64))
    f32 = jnp.float32
    ne, no = (DEPTH + 1) // 2, DEPTH // 2
    dm = D_MODEL
    G, P, H = S5_GROUPS, S5_STATE, S5_GROUP

    def nrm(shape, scale):
        return scale * jax.random.normal(next(ks), shape, f32)

    lru_u = jax.random.uniform(next(ks), (ne, 2, RG_WIDTH), f32, 0.9, 0.999)
    lru_s = lru_u ** (1.0 / RG_C)
    f_bias = jnp.linspace(3.0, 6.0, ML_HEADS, dtype=f32)
    b_if = jnp.concatenate([nrm((no, 2, ML_HEADS), 0.1), f_bias + nrm((no, 2, ML_HEADS), 0.1)], axis=-1)
    return {
        'x': nrm((BATCH, SEQ, dm), 1.0),
        'c': nrm((BATCH, dm), 1.0),
        'ctx': nrm((BATCH, CTX_LEN, dm), 1.0),
        'c_ctx': nrm((dm,), 1.0),
        'norm_g': 1.0 + nrm((DEPTH, dm), 0.02),
        'mod_w': nrm((DEPTH, dm, 3 * dm), 0.5 * dm ** -0.5),
        'mod_b': nrm((DEPTH, 3 * dm), 0.02),
        'final_g': 1.0 + nrm((dm,), 0.02),
        'e_w_in': nrm((ne, dm, IN_WIDTH_EVEN), dm ** -0.5),
        'e_w_out': nrm((ne, MIX_WIDTH, dm), MIX_WIDTH ** -0.5),
        's5_a_re': -0.5 + nrm((ne, 2, G, P), 0.01),
        's5_a_im': math.pi * jnp.arange(P, dtype=f32) + nrm((ne, 2, G, P), 0.01),
        's5_log_dt': jax.random.uniform(next(ks), (ne, 2, G), f32, math.log(1e-3), math.log(1e-1)),
        's5_b_re': nrm((ne, 2, G, P, H), (2 * H) ** -0.5),
        's5_b_im': nrm((ne, 2, G, P, H), (2 * H) ** -0.5),
        's5_c_re': nrm((ne, 2, G, H, P), P ** -0.5),
        's5_c_im': nrm((ne, 2, G, H, P), P ** -0.5),
        's5_d': nrm((ne, S5_WIDTH), 1.0),
        's5_glu_w': nrm((ne, S5_WIDTH, S5_WIDTH), S5_WIDTH ** -0.5),
        's5_glu_b': nrm((ne, S5_WIDTH), 0.02),
        'rg_conv_w': nrm((ne, CONV_W, RG_WIDTH), CONV_W ** -0.5),
        'rg_conv_b': nrm((ne, RG_WIDTH), 0.02),
        'rg_wa': nrm((ne, 2, RG_HEADS, RG_HEAD_DIM, RG_HEAD_DIM), RG_HEAD_DIM ** -0.5),
        'rg_ba': nrm((ne, 2, RG_WIDTH), 0.02),
        'rg_wx': nrm((ne, 2, RG_HEADS, RG_HEAD_DIM, RG_HEAD_DIM), RG_HEAD_DIM ** -0.5),
        'rg_bx': nrm((ne, 2, RG_WIDTH), 0.02),
        'rg_lam': jnp.log(lru_s) - jnp.log1p(-lru_s),
        'o_w_in': nrm((no, dm, IN_WIDTH_ODD), dm ** -0.5),
        'o_w_out': nrm((no, ML_WIDTH, dm), ML_WIDTH ** -0.5),
        'ml_conv_w': nrm((no, CONV_W, ML_WIDTH), CONV_W ** -0.5),
        'ml_conv_b': nrm((no, ML_WIDTH), 0.02),
        'ml_wq': nrm((no, ML_WIDTH // ML_QKV_BLOCK, ML_QKV_BLOCK, ML_QKV_BLOCK), ML_QKV_BLOCK ** -0.5),
        'ml_wk': nrm((no, ML_WIDTH // ML_QKV_BLOCK, ML_QKV_BLOCK, ML_QKV_BLOCK), ML_QKV_BLOCK ** -0.5),
        'ml_wv': nrm((no, ML_WIDTH // ML_QKV_BLOCK, ML_QKV_BLOCK, ML_QKV_BLOCK), ML_QKV_BLOCK ** -0.5),
        'ml_w_if': nrm((no, 2, 3, ML_WIDTH, 2 * ML_HEADS), (3 * ML_WIDTH) ** -0.5),
        'ml_b_if': b_if,
        'ml_norm_g': 1.0 + nrm((no, ML_WIDTH), 0.02),
        'ml_skip': 1.0 + nrm((no, ML_WIDTH), 0.02),
    }

def reference(x, c, ctx, c_ctx, norm_g, mod_w, mod_b, final_g, e_w_in, e_w_out,
              s5_a_re, s5_a_im, s5_log_dt, s5_b_re, s5_b_im, s5_c_re, s5_c_im, s5_d, s5_glu_w, s5_glu_b,
              rg_conv_w, rg_conv_b, rg_wa, rg_ba, rg_wx, rg_bx, rg_lam,
              o_w_in, o_w_out, ml_conv_w, ml_conv_b, ml_wq, ml_wk, ml_wv, ml_w_if, ml_b_if,
              ml_norm_g, ml_skip):
    rows = x.shape[1] // GRID_W
    s_lat = jax.nn.silu(c)
    s_ctx = jax.nn.silu(c_ctx)
    for l in range(DEPTH):
        j = l // 2
        sh, sc, gt = jnp.split(s_lat @ mod_w[l] + mod_b[l], 3, axis=-1)
        shc, scc, gtc = jnp.split(s_ctx @ mod_w[l] + mod_b[l], 3, axis=-1)
        h_lat = rms_norm(x, norm_g[l]) * (1.0 + sc[:, None]) + sh[:, None]
        h_ctx = rms_norm(ctx, norm_g[l]) * (1.0 + scc) + shc
        if l % 2 == 0:
            o_ctx, o_lat = even_mixer(h_ctx, h_lat, e_w_in[j], e_w_out[j],
                                      s5_a_re[j], s5_a_im[j], s5_log_dt[j], s5_b_re[j], s5_b_im[j],
                                      s5_c_re[j], s5_c_im[j], s5_d[j], s5_glu_w[j], s5_glu_b[j],
                                      rg_conv_w[j], rg_conv_b[j], rg_wa[j], rg_ba[j], rg_wx[j],
                                      rg_bx[j], rg_lam[j])
        else:
            o_ctx, o_lat = odd_mixer(h_ctx, to_col_major(h_lat, rows), o_w_in[j], o_w_out[j],
                                     ml_conv_w[j], ml_conv_b[j], ml_wq[j], ml_wk[j], ml_wv[j],
                                     ml_w_if[j], ml_b_if[j], ml_norm_g[j], ml_skip[j])
            o_lat = from_col_major(o_lat, rows)
        x = x + gt[:, None] * o_lat
        if l < DEPTH - 1:
            ctx = ctx + gtc * o_ctx
    return rms_norm(x, final_g)


_drawn_inputs = setup_inputs


def setup_inputs(seed=0):
    import zlib

    import numpy as np

    out = dict(_drawn_inputs(seed))
    spreads = {}
    factors = {'norm_g': 4.485,
     'final_g': 8.132,
     's5_a_re': 64.0,
     's5_a_im': 63.168,
     's5_log_dt': 64.0,
     's5_b_re': 64.0,
     's5_b_im': 64.0,
     's5_c_re': 64.0,
     's5_c_im': 64.0,
     's5_glu_w': 3.991,
     's5_glu_b': 28.747,
     'rg_ba': 8.0,
     'rg_bx': 8.0,
     'ml_conv_b': 5.074,
     'ml_norm_g': 64.0,
     'ml_skip': 24.407}
    for name, (base, spread) in spreads.items():
        noise = np.random.default_rng([zlib.crc32(name.encode()), seed]).standard_normal(out[name].shape)
        drawn = base * np.exp(spread * noise) if base else spread * noise
        out[name] = jnp.asarray(drawn.astype(out[name].dtype))
    for name, factor in factors.items():
        out[name] = (out[name] * factor).astype(out[name].dtype)
    return out
```

```python
import math
from contextlib import ExitStack

import concourse.bass as bass
import concourse.mybir as mybir

F32 = mybir.dt.float32
ALU = mybir.AluOpType
ACT = mybir.ActivationFunctionType
AX = mybir.AxisListType

P = 128
BANK = 512
D = 1024
DT = D // P
CTX, LAT = 256, 1024
TOK = CTX + LAT
SEGS = [(0, 512), (512, 512), (1024, 256)]
GRID_W = 64
ROWS = LAT // GRID_W
EPS = 1e-6

G, ST, HC = 64, 64, 16
T = 8
NJ = TOK // T
NJC = CTX // T
GB = 4
NB = G // GB
SL = T + 2
LAG = 2 * T - 1

RH, RD = 4, 256
MW = 2048
MT = MW // P
MH, MD = 4, 512
HT_ = MD // P
NBLK = TOK // P
CBLK = CTX // P
LBLK = LAT // P
PAD = 1 + CTX + 2 + 1 + LAT + 2
LOFF = CTX + 3
CV = LOFF + LAT

C_MODB, C_NG, C_FG, C_GLUB, C_RCW, C_RCB, C_C = 0, 48, 64, 72, 80, 112, 120
C_CC, C_BA, C_BX, C_LAM, C_MCB, C_MG, C_SK = 128, 136, 152, 168, 184, 200, 216
C_MCW = 256

HEAD_SIGNALS = ("xc_in", "xm_in0", "xm_in1", "xr_stored", "xb_in", "zt_in", "out_stored0", "out_stored1",
    "rows_t", "mix", "v_mmx0", "v_mmx1", "xb_used", "out_ready", "rows_ready", "em_ready", "yr_ready",
    "tr_ready", "xo", "h_ev", "bdkv_ready", "k_ev", "k_mm", "vt_ev", "bdq_ready", "ht_ev", "q_mm", "q_ev", "p_ready",
    "s_mm", "pv_mm", "hn_ready", "h_t", "wo_mm0", "wo_mm1", "sqf_ready", "ssf_mm", "yf_ready", "yf_t", "lf_abs",
    "lf_exp", "m_ready", "em_free", "xr_ready", "ybh_ready", "d_ready", "xmask", "rd_ready", "hf_ready", "mv_ready",
    "sd_ready", "sx_ready", "rf_ready")
DONE_SIGNALS = (("u_w0", 64), ("u_w1", 64), ("glu_w0", 16 * DT), ("glu_w1", 16 * DT), ("eo_w0", 64), ("eo_w1", 64),
    ("rows_in", 16 * 15), ("x_in", 16 * 5), ("par_t", 3), ("cs_ready", 1),
    ("csig", 1), ("par_ready", 2), ("s5_nat", 1), ("s5_at", 1), ("s5_bct", 2), ("s5_bt", 16), ("s5_ct", 16),
    ("s5_dt", 1), ("s5_dar", 1), ("s5_mag", 1), ("s5_ang", 1), ("s5_sin", 1), ("lam_abs", 1), ("lam_exp", 1),
    ("lam_ready", 1), ("u_mm0", 4), ("u_mm1", 4), ("u_ev0", 4), ("u_ev1", 4), ("xt_t", 3 * DT), ("xt_ready", 3 * DT),
    ("ss_mm0", DT), ("ht_ready", 2 * DT), ("glu_mm0", DT), ("glu_mm1", DT), ("glu_sg", DT), ("glu_ev0", DT),
    ("glu_ev1", DT), ("eo_mm0", 4), ("eo_mm1", 4), ("mod0_mm0", 4), ("mod0_mm1", 4), ("mod1_mm0", DT), ("mod1_mm1", DT),
    ("mod1_mm2", DT), ("f_mm0", NB // 2), ("f_mm1", NB // 2), ("x_t0", NB // 2), ("x_t1", NB // 2),
    ("x_ready0", NB // 2), ("x_ready1", NB // 2), ("v_mm0", NB // 2), ("v_mm1", NB // 2))


def build(nc, A, out):
    with ExitStack() as ctx:
        sems = {}

        TAKES_OVER = {}
        for new, (old, total) in zip(HEAD_SIGNALS, DONE_SIGNALS):
            TAKES_OVER[new] = (old, total)

        def sem(name):
            name = TAKES_OVER.get(name, (name, 0))[0]
            if name not in sems:
                sems[name] = ctx.enter_context(nc.semaphore(name))
            return sems[name]

        def past(name, n):
            return sem(name), n + TAKES_OVER.get(name, (name, 0))[1]

        def sb(name, n):
            return ctx.enter_context(nc.sbuf_tensor(name, [P, n], F32))

        def dram(name, shape):
            return nc.dram_tensor(name, shape, F32).ap()

        def mm(o, lhsT, rhs, k, n):
            return nc.tensor.matmul(o, lhsT, rhs, start=(k == 0), stop=(k == n - 1))

        AR = sb("arena", 47520)
        ps = ctx.enter_context(nc.psum_tensor("ps", [P, 8, BANK], F32))

        psf = ps[:, :, :].rearrange("p b c -> p (b c)")
        ps3 = [psf[:, 3 * s * BANK:3 * s * BANK + TOK] for s in range(2)]

        def at(o, n):
            return AR[:, o:o + n]

        HTo, XTo, WZo, YTo, RB = 0, 10240, 10240, 20480, 30848
        HT = at(HTo, DT * TOK).rearrange("p (k t) -> p k t", k=DT)
        XT = at(XTo, DT * TOK).rearrange("p (k t) -> p k t", k=DT)
        xin = at(HTo, NBLK * D).rearrange("p (b d) -> p b d", b=NBLK)
        WZ = at(WZo, (NJ + 1) * 2 * G).rearrange("p (j r g) -> p j r g", r=2, g=G)
        PV = sb("param_cols", 384)
        MOD = sb("modulation", 2 * 48)
        MODv = MOD[:, :].rearrange("p (l n w) -> p l n w", l=2, w=2)
        ACf = sb("norm_scale", 32)
        ACv = ACf[:, :].rearrange("p (l k w) -> p l k w", l=2, w=2)
        cs = sb("silu_c", 16)
        csv = cs[:, :].rearrange("p (k w) -> p k w", w=2)
        cst = sb("silu_tmp", 16)
        ident = sb("ident", 128)
        ones = sb("ones", 128)
        cols = sb("const_cols", 4)
        lamc = sb("rg_decay", 32)
        W = sb("weights", 2048)
        Wv = W[:, :].rearrange("p (s k n) -> p s k n", s=2, k=DT)
        GW = sb("weights2", 2048)
        sq = [at(RB + 8192, 2 * TOK).rearrange("p (s t) -> p s t", s=2), at(YTo, DT * TOK).rearrange("p (s t) -> p s t", s=DT)]
        SQN = [2, DT]
        rstd = [at(RB + 8192 + 2 * TOK, TOK), at(RB, TOK)]
        ntmp = [at(o, 2 * TOK).rearrange("p (s t) -> p s t", s=2) for o in (RB + 8192 + 3 * TOK, RB + TOK)]
        modw1 = at(44400, 3 * 1024).rearrange("p (s k n) -> p s k n", s=3, k=DT)
        modw = at(RB, 2 * 3072).rearrange("p (s k n) -> p s k n", s=2, k=DT)
        rows = at(RB + 6144, 384).rearrange("p (v c) -> p v c", v=3)

        xt_d = dram("xt_spill", [P, DT * TOK])
        u_d = dram("u_chunks", [DT, P, TOK])
        y_d = dram("y_chunks", [DT, P, TOK])
        v_d = dram("s5_lags", [G, HC, LAG * HC])
        g_d = dram("s5_out_maps", [NB, P, GB * 2 * SL * HC])
        bo_d = dram("rg_out", [DT, P, TOK])
        xm_d = dram("ml_xm", [MT, P, TOK])
        xc_d = dram("ml_xcv", [MT, P, TOK])
        z_d = dram("ml_z", [MT, P, LAT])
        xr_d = dram("ml_rows", [2 * MH, LAT])

        xr_ = A["x"][0].rearrange("(b p) d -> p b d", p=P)
        cx_ = A["ctx"][0].rearrange("(b p) d -> p b d", p=P)
        rr = lambda ap, pat, **k: ap.rearrange(pat, **k)
        VP = [
            (0, 0, rr(A["mod_b"], "l (n c) -> (l n) c", c=P)),
            (0, 48, rr(A["norm_g"], "l (n c) -> (l n) c", c=P)),
            (0, 64, rr(A["final_g"], "(n c) -> n c", c=P)),
            (0, 72, rr(A["s5_glu_b"], "l (n c) -> (l n) c", c=P)),
            (0, 80, rr(A["rg_conv_w"][0], "j (n c) -> (j n) c", c=P)),
            (0, 112, rr(A["rg_conv_b"], "l (n c) -> (l n) c", c=P)),
            (0, 120, rr(A["c"], "l (n c) -> (l n) c", c=P)),
            (1, 0, rr(A["c_ctx"], "(n c) -> n c", c=P)),
            (1, 8, rr(A["rg_ba"][0], "l (n c) -> (l n) c", c=P)),
            (1, 24, rr(A["rg_bx"][0], "l (n c) -> (l n) c", c=P)),
            (1, 40, rr(A["rg_lam"][0], "l (n c) -> (l n) c", c=P)),
            (1, 56, rr(A["ml_conv_b"], "l (n c) -> (l n) c", c=P)),
            (1, 72, rr(A["ml_norm_g"], "l (n c) -> (l n) c", c=P)),
            (1, 88, rr(A["ml_skip"], "l (n c) -> (l n) c", c=P)),
            (2, 0, rr(A["ml_conv_w"][0], "j (n c) -> (j n) c", c=P)),
        ]
        NVP = len(VP)
        mod_v = [A["mod_w"][l].rearrange("(k p) n -> p k n", p=P) for l in range(2)]
        ew_in = A["e_w_in"][0].rearrange("(k p) (m n) -> m p k n", p=P, n=P)
        glu_v = A["s5_glu_w"][0].rearrange("(k p) (m n) -> m p k n", p=P, n=P)
        ew_out = A["e_w_out"][0].rearrange("(k p) (m n) -> m p k n", p=P, n=P)

        def rb(o, n):
            return at(RB + o, n)

        bn = rb(0, 2048).rearrange("p (r q h) -> p r q h", r=2, h=HC)
        cn = rb(2048, 2048).rearrange("p (h r q) -> p h r q", r=2, h=HC)
        X = rb(0, 2048).rearrange("p (s r g c) -> p s r g c", s=2, r=2, g=GB)
        Gb = [rb(2048, 1280), rb(14336, 1280)]
        Gv = [g.rearrange("p (g r k h) -> p g r k h", g=GB, r=2, h=HC) for g in Gb]
        BT = rb(4096, 2048).rearrange("p (r h g) -> p r h g", r=2, h=HC)
        t1 = rb(4096, 1280)
        CT = rb(6144, 2048).rearrange("p (r h g) -> p r h g", r=2, h=HC)
        BB = rb(8192, 2048).rearrange("p (r h g) -> p r h g", r=2, h=HC)
        Q = rb(10240, 1280).rearrange("p (k r g) -> p k r g", r=2, g=G)
        t2 = rb(10240, 1280)
        PWE = rb(11520, 1024).rearrange("p (k r g) -> p k r g", r=2, g=G)
        PWF = rb(12544, 1280).rearrange("p (k r g) -> p k r g", r=2, g=G)
        AL = rb(13824, 256).rearrange("p (v g) -> p v g", v=4)
        A12 = sb("s5_decay", 256)
        A1 = A12[:, 0:128].rearrange("p (r g) -> p r g", r=2)
        A2 = A12[:, 128:256].rearrange("p (r g) -> p r g", r=2)
        scanP = sb("s5_scan_tmp", 256)
        SP1 = scanP[:, 0:128].rearrange("p (r g) -> p r g", r=2)
        SP2 = scanP[:, 128:256].rearrange("p (r g) -> p r g", r=2)
        nat = rb(14336, 1280).rearrange("p (v q) -> p v q", q=64)
        Eg = rb(15616, 1024).rearrange("p (r g c) -> p r g c", r=2, g=GB)
        Ub = GW[:, 0:1280].rearrange("p (s g j) -> p s g j", s=2, g=GB)
        Vs = W[0:HC, 0:GB * LAG * HC].rearrange("p (g i h) -> p g i h", g=GB, h=HC)
        Dg = W[0:HC, 960:960 + G * HC].rearrange("p (g h) -> p g h", h=HC)
        dcol = W[0:HC, 1984:1984 + G]
        u_b = u_d.rearrange("k (g h) (s j) -> (k g) (h s) j", h=HC, s=T)
        y_b = y_d.rearrange("k (g h) (t j) -> (k g) t h j", h=HC, t=T)
        u_stage = rb(0, 2 * TOK).rearrange("p (z s j) -> p z s j", z=2, s=T)

        Fg = rb(0, 2560).rearrange("p (s n) -> p s n", s=2)
        Fgv = [Fg[:, s].rearrange("p (g r k h) -> p g r k h", g=GB, r=2, h=HC) for s in range(2)]
        Mb = rb(2560, 1024).rearrange("p (s g c) -> p s g c", s=2, g=GB)
        Fu = rb(3584, 1280).rearrange("p (s g j) -> p s g j", s=2, g=GB)
        Zb = rb(4864, 2560).rearrange("p (s r g j) -> p s r g j", s=2, r=2, g=GB)
        Yb = rb(7424, 1280).rearrange("p (s g j) -> p s g j", s=2, g=GB)

        xrp = rb(0, 2 * PAD).rearrange("p (s t) -> p s t", s=2)
        xcb = rb(2572, 2 * TOK).rearrange("p (s t) -> p s t", s=2)
        RT = rb(5132, 2 * TOK).rearrange("p (s t) -> p s t", s=2)
        IT = rb(7692, 2 * TOK).rearrange("p (s t) -> p s t", s=2)
        AT = rb(10252, 2 * TOK).rearrange("p (s t) -> p s t", s=2)
        TT = rb(12812, CV)
        HH = rb(14095, 2 * TOK).rearrange("p (s t) -> p s t", s=2)
        SG = rb(0, 2 * TOK).rearrange("p (s t) -> p s t", s=2)
        lt = scanP[:, 0:96].rearrange("p (v c) -> p v c", v=6)
        BBs = GW[:, 1280:1536]
        BBv = BBs.rearrange("p (s r h g) -> p s r h g", s=2, r=2, h=HC)
        sa = rb(0, 384).rearrange("p (v r g) -> p v r g", v=3, r=2)
        tB = rb(512, 2048).rearrange("p (r h g) -> p r h g", r=2, h=HC)
        pg1 = rb(4096, 640)
        pg2 = rb(10240, 640)
        xt1 = rb(4096 + 640, 512)
        xt2 = rb(10240 + 640, 512)
        AO = rb(0, DT * TOK).rearrange("p (k t) -> p k t", k=DT)
        YT = at(YTo, DT * TOK).rearrange("p (k t) -> p k t", k=DT)
        SZ = rb(10240, TOK)
        SGs = rb(10240 + TOK, TOK)
        WO = [w[:, :].rearrange("p (k n) -> p k n", k=2 * DT) for w in (W, GW)]
        m_d = bass.AP(v_d.tensor, 0, [[HC * LAG * HC, G], [LAG * HC, HC], [HC, T], [1, P]])
        vtmp = GW[0:HC, 1536:1536 + GB * HC].rearrange("p (g h) -> p g h", g=GB)
        GWv = GW[:, :].rearrange("p (d m k n) -> p d m k n", d=2, m=2, k=2)

        K1 = 41088
        W4 = at(K1, 192).rearrange("p (m t o) -> p m t o", m=3, o=4)
        WIF = at(K1 + 192, 768).rearrange("p (m t d n) -> p m t d n", m=3, t=MT, d=2)
        WFc = at(K1 + 960, 512).rearrange("p (t w n) -> p t w n", t=MT, w=2)
        WFs = at(K1 + 1472, 512).rearrange("p (s w n) -> p s w n", s=2, w=2)
        bmask = at(K1 + 1984, P).rearrange("p (b o) -> p b o", o=4)
        BD = at(K1 + 2112, 384).rearrange("p (m c) -> p m c", m=3)
        BDT = at(K1 + 2496, 384).rearrange("p (m c) -> p m c", m=3)
        BI = sb("gate_bias", 1)
        xmp = at(YTo, 2 * PAD).rearrange("p (s t) -> p s t", s=2)
        mcv = at(YTo + 2572, CV)
        mcs = at(YTo + 2572 + CV, CV)
        xco = at(YTo + 5140, 2 * TOK).rearrange("p (s t) -> p s t", s=2)
        zo = at(YTo + 7700, 2 * LAT).rearrange("p (s t) -> p s t", s=2)
        psG = psf[:, 5 * BANK:5 * BANK + TOK]
        GZ = GW[:, :].rearrange("p (s k n) -> p s k n", s=2, k=DT)
        ow_in = A["o_w_in"][0].rearrange("(k p) (m n) -> m p k n", p=P, n=P)
        ow_out = A["o_w_out"][0].rearrange("(h k p) (m n) -> h m p k n", p=P, n=P, h=MH)
        row = [at(1280 * n, TOK)[0:64] for n in range(8)]
        rLI, rLF, rA, rB, rC, rM, rRes, rO = row
        NPC = 52 * P
        Pm = at(0, NPC)
        Xb = at(NPC, 2 * LAT).rearrange("p (d t) -> p d t", d=2)
        Dt = at(8704, 1024).rearrange("p (s t) -> p s t", s=2)
        XM = at(9728, 256).rearrange("p (s t) -> p s t", s=2)
        Xc = at(YTo, 4 * TOK).rearrange("p (k t) -> p k t", k=4)
        Kt = at(YTo + 5120, 4 * TOK).rearrange("p (k t) -> p k t", k=4)
        Vt = at(YTo + 10240, 4 * TOK).rearrange("p (b e) -> p b e", b=NBLK)
        Qt = at(YTo + 15360, 2048).rearrange("p (k t) -> p k t", k=4)
        MX = at(YTo + 17408, 2048).rearrange("p (k t) -> p k t", k=4)
        WOo = at(YTo + 19456, 1024).rearrange("p (s k n) -> p s k n", s=2, k=4)
        Xm = at(43968, 2 * TOK).rearrange("p (s t) -> p s t", s=2)
        BDq = at(46528, 512).rearrange("p (k c) -> p k c", k=4)
        BDkv = [at(47040, 256).rearrange("p (m c) -> p m c", m=2), A12[:, :].rearrange("p (m c) -> p m c", m=2)]
        Zt = W[:, :].rearrange("p (k t) -> p k t", k=4)
        Hb = GW[:, :].rearrange("p (j e) -> p j e", j=4)
        YB = at(K1 + 192, 800).rearrange("p (d j i h) -> p d j i h", d=2, j=NBLK, i=NBLK)
        TB = at(K1 + 992, 80).rearrange("p (d h j) -> p d h j", d=2, h=4)
        TR = at(K1 + 1072, 80)[0:64].rearrange("p (d h j) -> p d h j", d=2, h=4)
        EMT = at(K1 + 1152, 64).rearrange("p (j d h) -> p j d h", j=LBLK, d=2)
        cmask = at(K1 + 1216, 256).rearrange("p (d c) -> p d c", d=2)
        YBh = at(K1 + 1472, 200).rearrange("p (d j i) -> p d j i", d=2, j=NBLK)
        EMh = at(K1 + 1672, 16).rearrange("p (j d) -> p j d", d=2)
        rden = at(K1 + 1688, 16).rearrange("p (j d) -> p j d", d=2)
        bst = at(K1 + 1704, 48).rearrange("p (s n) -> p s n", s=8)
        mv = at(K1 + 1752, 16).rearrange("p (s n) -> p s n", n=2)
        gs1 = MODv[:, 1, 16:24]
        HALF = LAT // 2
        HB_ = HALF // P

        def blocks_of(d, I, th):
            js = range(CBLK + HB_ * th, CBLK + HB_ * (th + 1))
            return [J for J in js if I < CBLK or (J >= I if d == 0 else J <= I)]

        PIECES = [[(I, d, blocks_of(d, I, th)) for I in range(NBLK) for d in range(2) if blocks_of(d, I, th)] for th in range(2)]
        NPI = len(PIECES[0])
        assert len(PIECES[1]) == NPI
        POFF = [{}, {}]
        for th in range(2):
            o = 0
            for I, d, js in PIECES[th]:
                POFF[th][I, d] = o
                o += P * len(js)
            assert o <= NPC

        def p_of(th, I, d, J):
            js = blocks_of(d, I, th)
            o = POFF[th][I, d] + P * (J - js[0])
            return Pm[:, o:o + P]

        def pieces_before(th, I):
            return sum(1 for x in PIECES[th] if x[0] < I)

        def step_of(d, I):
            return I if d == 0 else (CBLK - 1 - I if I < CBLK else NBLK + CBLK - 1 - I)

        xr_rows = bass.AP(xr_d.tensor, 0, [[0, P], [LAT, 2 * MH], [1, LAT]])

        def bcast_row(n):
            return xr_rows[:, bass.ds(n, 1)].rearrange("p o t -> p (o t)")

        SQf = at(0, DT * LAT).rearrange("p (k t) -> p k t", k=DT)
        YF = at(YTo, DT * LAT).rearrange("p (k t) -> p k t", k=DT)
        rfin = at(8192, LAT)
        YO = at(30720, 2 * D).rearrange("p (s c) -> p s c", s=2)

        def natural(ap, rw):
            return [ap[rw, 0:CTX][:, ::-1], ap[rw, CTX:TOK][:, ::-1]]

        block = ctx.enter_context(nc.Block())
        MAGIC = 12582912.0
        TWO_PI = (6.28125, 0.0019350051879882812, 3.019916050561733e-07)

        def wz_moves(r, b):
            src = ps[:, 2 + 2 * r:4 + 2 * r, 0:2 * NJ].rearrange("p a (g j) -> p a g j", g=2)

            def put(rw, steps):
                w = WZ[rw, steps, r, bass.ds(GB * b, GB)]
                return w.rearrange("p j (a g) -> p a g j", a=2)

            f, bk = slice(0, 64), slice(64, 128)
            return [
                (put(f, slice(1, NJ + 1)), src[f]),
                (put(bk, slice(1, NJC + 1)), src[bk, :, :, 0:NJC][:, :, :, ::-1]),
                (put(bk, slice(NJC + 1, NJ + 1)), src[bk, :, :, NJC:NJ][:, :, :, ::-1]),
            ]

        def log1p(link, y, z, z2, o, n=9):
            V = nc.vector
            link(V.tensor_scalar(z, y, 2.0, None, ALU.add))
            link(V.reciprocal(z, z))
            link(V.tensor_tensor(z, z, y, ALU.mult))
            link(V.tensor_tensor(z2, z, z, ALU.mult))
            link(V.tensor_scalar(o, z2, 1.0 / (2 * n - 1), None, ALU.mult))
            for c in range(n - 2, 0, -1):
                link(V.scalar_tensor_tensor(out=o, in0=o, scalar=1.0 / (2 * c + 1), in1=z2, op0=ALU.add, op1=ALU.mult))
            link(V.scalar_tensor_tensor(out=o, in0=o, scalar=1.0, in1=z, op0=ALU.add, op1=ALU.mult))
            link(V.tensor_scalar(o, o, 2.0, None, ALU.mult))

        @block.sync
        def _(sp):
            for v, r, src in VP:
                sp.dma_start(rows[r:r + src.shape[0], v, :], src).then_inc(sem("rows_in"), 16)
            sp.dma_start(xin[:, 0:CBLK, :], cx_).then_inc(sem("x_in"), 16)
            for b in range(0, LBLK, 2):
                sp.dma_start(xin[:, CBLK + b:CBLK + b + 2, :], xr_[:, b:b + 2, :]).then_inc(sem("x_in"), 16)
            with sp.Fori(0, 4) as i:
                for s in range(2):
                    sp.wait_ge(*past(f"mod0_mm{s}", i))
                    sp.dma_start(modw[:, s], mod_v[0][:, :, bass.ds((2 * i + s) * 384, 384)]).then_inc(sem(f"mod0_in{s}"), 16)
            sp.wait_ge(*past("xt_ready", 24))
            sp.dma_start(xt_d, at(XTo, DT * TOK)).then_inc(sem("xt_spilled"), 16)
            with sp.Fori(0, 4) as i:
                for s in range(2):
                    sp.wait_ge(*past(f"u_mm{s}", i))
                    sp.dma_start(Wv[:, s], ew_in[bass.ds(2 * i + s, 1)].rearrange("m p k n -> p (m k) n")).then_inc(sem(f"u_w{s}"), 16)
            sp.wait_ge(*past("u_stored0", 64))
            sp.wait_ge(*past("u_stored1", 64))
            sp.wait_ge(*past("ht_ready", 16))
            for dst, src in (
                (nat[:, 0], A["s5_a_re"][0].rearrange("d g q -> (d g) q")),
                (nat[:, 1], A["s5_a_im"][0].rearrange("d g q -> (d g) q")),
                (nat[:, 2, 0:1], A["s5_log_dt"][0].rearrange("d (g o) -> (d g) o", o=1)),
                (bn[:, 0], A["s5_b_re"][0].rearrange("d g q h -> (d g) q h")),
                (bn[:, 1], A["s5_b_im"][0].rearrange("d g q h -> (d g) q h")),
                (cn[:, :, 0], A["s5_c_re"][0].rearrange("d g h q -> (d g) h q")),
                (cn[:, :, 1], A["s5_c_im"][0].rearrange("d g h q -> (d g) h q")),
            ):
                sp.dma_start(dst, src).then_inc(sem("s5_in"), 16)
            with nc.allow_non_contiguous_dma(reason="a thousand skip coefficients"):
                sp.dma_start(dcol, A["s5_d"][0].rearrange("(g h) -> h g", h=HC)).then_inc(sem("s5_in"), 16)
            with sp.Fori(0, NB // 2) as i:
                for s in range(2):
                    sp.wait_ge(*past(f"e_mm{s}", i))
                    sp.dma_start(Ub[:, s], u_b[bass.ds(GB * (2 * i + s), GB)].rearrange("g q j -> q g j")).then_inc(sem(f"ub_in{s}"), 16)
            sp.wait_ge(*past("v_stored", 16 * NB))
            sp.wait_ge(*past("e_mm0", NB // 2))
            sp.wait_ge(*past("e_mm1", NB // 2))
            with sp.Fori(0, RH) as i:
                for s in range(2):
                    sp.wait_ge(*past(f"rg_pmm{s}", 2 * i))
                    sp.dma_start(Wv[:, s], ew_in[bass.ds(2 * i + 16 + s, 1)].rearrange("m p k n -> p (m k) n")).then_inc(sem(f"rg_w{s}"), 16)
                for s in range(2):
                    sp.wait_ge(*past(f"rg_gmm{s}", 4 * i))
                for d in range(2):
                    for m, name in enumerate(("rg_wa", "rg_wx")):
                        sp.dma_start(GWv[:, d, m], A[name][0, d, bass.ds(i, 1)].rearrange("o (k p) n -> p (o k) n", p=P)).then_inc(sem("rg_gw"), 16)
                for s in range(2):
                    sp.wait_ge(*past(f"rg_pmm{s}", 2 * i + 1))
                    sp.dma_start(Wv[:, s], ew_in[bass.ds(2 * i + 24 + s, 1)].rearrange("m p k n -> p (m k) n")).then_inc(sem(f"rg_w{s}"), 16)
            sp.wait_ge(*past("bo_stored", 16 * RH))
            sp.wait_ge(*past("g_stored0", 16 * NB // 2))
            sp.wait_ge(*past("g_stored1", 16 * NB // 2))
            with sp.Fori(0, NB // 2) as i:
                for s in range(2):
                    sp.wait_ge(*past(f"f_mm{s}", i))
                    sp.dma_start(Fg[:, s], g_d[bass.ds(2 * i + s, 1)].rearrange("b p n -> p (b n)")).then_inc(sem(f"f_in{s}"), 16)
                    sp.dma_start(Fu[:, s], u_b[bass.ds(GB * (2 * i + s), GB)].rearrange("g q j -> q g j")).then_inc(sem(f"f_in{s}"), 16)
                    for g in range(GB):
                        sp.dma_start(Mb[:, s, g], m_d[bass.ds(GB * (2 * i + s) + g, 1)]).then_inc(sem(f"f_in{s}"), 16)
            sp.wait_ge(*past("y_stored0", 16 * GB * (NB // 2)))
            sp.wait_ge(*past("y_stored1", 16 * GB * (NB // 2)))
            sp.dma_start(YT, y_d.rearrange("k p t -> p k t")).then_inc(sem("y_in"), 16)
            sp.dma_start(XT, xt_d.rearrange("p (k t) -> p k t", k=DT)).then_inc(sem("mix_in"), 16)
            with sp.Fori(0, DT) as i:
                for s, src in enumerate((glu_v[bass.ds(i, 1)], ew_in[bass.ds(i + 8, 1)])):
                    sp.wait_ge(*past(f"glu_mm{s}", i))
                    sp.dma_start(Wv[:, s], src.rearrange("m p k n -> p (m k) n")).then_inc(sem(f"glu_w{s}"), 16)
            sp.wait_ge(*past("glu_mm0", DT))
            sp.wait_ge(*past("glu_mm1", DT))
            sp.dma_start(HT, bo_d.rearrange("k p t -> p k t")).then_inc(sem("mix_in"), 16)
            with sp.Fori(0, 4) as i:
                for s in range(2):
                    sp.wait_ge(*past(f"eo_mm{s}", i))
                    sp.dma_start(WO[s], ew_out[bass.ds(2 * i + s, 1)].rearrange("m p k n -> p (m k) n")).then_inc(sem(f"eo_w{s}"), 16)
            sp.wait_ge(*past("glu_ao", DT))
            for m, name in enumerate(("ml_wq", "ml_wk", "ml_wv")):
                sp.dma_start(W4[:, m], A[name][0].rearrange("(t b) i o -> (b i) t o", b=32)).then_inc(sem("ml_in"), 16)
            for m in range(3):
                for d in range(2):
                    sp.dma_start(WIF[:, m, :, d], A["ml_w_if"][0, d, m].rearrange("(t p) n -> p t n", p=P)).then_inc(sem("ml_in"), 16)
            sp.wait_ge(*past("bi_zero", 1))
            for d in range(2):
                for n in range(2):
                    sp.dma_start(BI[64 * n + 32 * d:64 * n + 32 * d + MH, :], A["ml_b_if"][0, d, MH * n:MH * n + MH].rearrange("(h o) -> h o", o=1)).then_inc(sem("ml_in"), 16)
            sp.wait_ge(*past("eo_mm0", 4))
            sp.wait_ge(*past("eo_mm1", 4))
            with sp.Fori(0, MT // 2) as i:
                for s in range(2):
                    sp.wait_ge(*past(f"xm_mm{s}", i))
                    sp.dma_start(Wv[:, s], ow_in[bass.ds(2 * i + s, 1)].rearrange("m p k n -> p (m k) n")).then_inc(sem(f"xm_w{s}"), 16)
                    sp.wait_ge(*past(f"z_mm{s}", i))
                    sp.dma_start(GZ[:, s], ow_in[bass.ds(2 * i + MT + s, 1)].rearrange("m p k n -> p (m k) n")).then_inc(sem(f"z_w{s}"), 16)
            for s in range(2):
                sp.wait_ge(*past(f"xm_mm{s}", MT // 2))
                sp.wait_ge(*past(f"z_mm{s}", MT // 2))
                for nm, n in (("xm", 32), ("xcv", 16), ("z", 16)):
                    sp.wait_ge(*past(f"{nm}_stored{s}", n * MT // 2))
            sp.wait_ge(*past("rows_t", 1))
            with sp.Fori(0, MH) as i:
                sp.wait_ge(*past("mix", 2 * i))
                sp.dma_start(Xc, xc_d[bass.ds(4 * i, 4)].rearrange("k p t -> p k t")).then_inc(sem("xc_in"), 16)
                for k in range(4):
                    s = k % 2
                    sp.wait_ge(*past(f"v_mmx{s}", 2 * i + k // 2))
                    sp.dma_start(Xm[:, s], xm_d[bass.ds(4 * i + k, 1)].rearrange("k p t -> p (k t)")).then_inc(sem(f"xm_in{s}"), 16)
                sp.wait_ge(*past("xr_stored", 32))
                sp.wait_ge(*past("xb_used", i))
                for d in range(2):
                    sp.dma_start(Xb[:, d], bcast_row(i + MH * d)).then_inc(sem("xb_in"), 16)
                for th in range(2):
                    sp.wait_ge(*past("mix", 2 * i + th))
                    sp.dma_start(Zt, z_d[bass.ds(4 * i, 4), :, HALF * th:HALF * th + HALF].rearrange("k p t -> p k t")).then_inc(sem("zt_in"), 16)
                    for n in range(DT):
                        sp.wait_ge(*past(f"wo_mm{n % 2}", 8 * i + 4 * th + n // 2))
                        sp.dma_start(WOo[:, n % 2], ow_out[bass.ds(i, 1), n].rearrange("o p k n -> p (o k) n")).then_inc(sem(f"wo_in{n % 2}"), 16)
            for b in range(LBLK):
                sp.wait_ge(*past("out_ready", b + 1))
                sp.dma_start(out[0, P * b:P * b + P, :], YO[:, b % 2]).then_inc(sem(f"out_stored{b % 2}"), 16)
            for s in range(2):
                sp.wait_ge(*past(f"out_stored{s}", 16 * LBLK // 2))

        @block.tensor
        def _(pe):
            pe.wait_ge(*past("rows_in", 16 * NVP))
            pe.wait_ge(*past("consts", 4))
            for v, n in enumerate((128, 104, 64)):
                nc.tensor.transpose(ps[:, 7, P * v:P * v + n], rows[0:n, v, :], ident[0:n, 0:n]).then_inc(sem("par_t"), 1)

            def square_sums(l, k):
                pe.wait_ge(*past(f"sq_ready{l}", k + 1))
                for j, (t0, n) in enumerate(SEGS):
                    last = mm(ps[:, 4 + j, 0:n], ones[:, :], sq[l][:, k % SQN[l], t0:t0 + n], k, DT)
                last.then_inc(sem(f"ss_mm{l}"), 1)

            pe.wait_ge(*past("x_in", 16 * 5))
            for k in range(DT):
                for j, (t0, n) in enumerate(SEGS):
                    q = 3 * k + j
                    if q >= 4:
                        pe.wait_ge(*past("xt_ready", q - 3))
                    for b in range(n // P):
                        last = nc.tensor.transpose(ps[:, q % 4, P * b:P * b + P], xin[:, t0 // P + b, P * k:P * k + P], ident[:, :])
                    last.then_inc(sem("xt_t"), 1)
                if k:
                    square_sums(0, k - 1)
            square_sums(0, DT - 1)

            def modulate(l):
                pe.wait_ge(*past("cs_ready", 1))
                with pe.Fori(0, 4) as i:
                    for s in range(2):
                        pe.wait_ge(*past(f"mod{l}_in{s}", 16 * i + 16))
                        for n in range(3):
                            for k in range(DT):
                                last = mm(ps[:, 7, bass.ds(12 * i + 6 * s + 2 * n, 2)], modw[:, s, k, P * n:P * n + P], csv[:, k, :], k, DT)
                        last.then_inc(sem(f"mod{l}_mm{s}"), 1)

            modulate(0)
            pe.wait_ge(*past("ht_ready", 16))
            with pe.Fori(0, 4) as i:
                for s in range(2):
                    pe.wait_ge(*past(f"u_w{s}", 16 * i + 16))
                    pe.wait_ge(*past(f"u_ev{s}", i))
                    for t0, n in SEGS:
                        for k in range(DT):
                            last = mm(ps3[s][:, t0:t0 + n], Wv[:, s, k], HT[:, k, t0:t0 + n], k, DT)
                    last.then_inc(sem(f"u_mm{s}"), 1)
            pe.wait_ge(*past("s5_nat", 1))
            pe.wait_ge(*past("u_ev0", 4))
            pe.wait_ge(*past("u_ev1", 4))
            nc.tensor.transpose(ps[:, 6, 0:P], nat[:, 11:13].rearrange("p v q -> p (v q)"), ident[:, :])
            nc.tensor.transpose(ps[:, 6, P:2 * P], nat[:, 17:19].rearrange("p v q -> p (v q)"), ident[:, :]).then_inc(sem("s5_at"), 1)
            for w in range(2):
                if w == 1:
                    pe.wait_ge(*past("s5_bt", 16))
                for h in range(HC):
                    src = (bn.rearrange("p r q h -> p h (r q)") if w == 0 else cn.rearrange("p h r q -> p h (r q)"))[:, h]
                    last = nc.tensor.transpose(ps[:, h // 4, P * (h % 4):P * (h % 4) + P], src, ident[:, :])
                last.then_inc(sem("s5_bct"), 1)
            pe.wait_ge(*past("s5_ct", 16))
            with pe.Fori(0, NB // 2) as i:
                for s in range(2):
                    b = 2 * i + s
                    pe.wait_ge(*past(f"x_ready{s}", i + 1))
                    pe.wait_ge(*past(f"g_ready{s}", i + 1))
                    pe.wait_ge(*past("v_ev", b))
                    pe.wait_ge(*past("eg_ready", 2 * b))
                    for r in range(2):
                        for g in range(GB):
                            last = nc.tensor.transpose(ps[:, r, P * g:P * g + P], X[:, s, r, g], ident[:, :])
                    last.then_inc(sem(f"x_t{s}"), 1)
                    for g in range(GB):
                        for d in range(2):
                            rw = slice(64 * d, 64 * d + 64)
                            for r in range(2):
                                last = mm(ps[0:HC, 6 + d, P * g:P * g + P], BBv[rw, s, r, :, g],
                                          Gv[s][rw, g, r, 2 * d:2 * d + T, :], r, 2)
                    last.then_inc(sem(f"v_mm{s}"), 1)
                    pe.wait_ge(*past("eg_ready", 2 * b + 2))
                    pe.wait_ge(*past(f"ub_in{s}", 16 * i + 16))
                    pe.wait_ge(*past("wz_a", b))
                    pe.wait_ge(*past("wz_v", b))
                    for r in range(2):
                        for g in range(GB):
                            last = mm(ps[:, 2 + 2 * r + g // 2, NJ * (g % 2):NJ * (g % 2) + NJ], Eg[:, r, g], Ub[:, s, g], 0, 1)
                    last.then_inc(sem(f"e_mm{s}"), 1)
            pe.wait_ge(*past("wz_a", NB))
            pe.wait_ge(*past("wz_v", NB))
            pe.wait_ge(*past("v_ev", NB))
            with pe.Fori(0, RH) as i:
                for kind in range(2):
                    for s in range(2):
                        pe.wait_ge(*past(f"rg_w{s}", 32 * i + 16 * kind + 16))
                        pe.wait_ge(*past(f"rg_ev{s}", 6 * i + kind))
                        for t0, n in SEGS:
                            for k in range(DT):
                                last = mm(ps3[s][:, t0:t0 + n], Wv[:, s, k], HT[:, k, t0:t0 + n], k, DT)
                        last.then_inc(sem(f"rg_pmm{s}"), 1)
                pe.wait_ge(*past("rg_gw", 64 * i + 64))
                pe.wait_ge(*past("xc_ready", 2 * i + 2))
                for d in range(2):
                    for m in range(2):
                        for s in range(2):
                            pe.wait_ge(*past(f"rg_ev{s}", 6 * i + 2 + 2 * d + m))
                            for t0, n in SEGS:
                                for k in range(2):
                                    last = mm(ps3[s][:, t0:t0 + n], GWv[:, d, m, k, P * s:P * s + P], xcb[:, k, t0:t0 + n], k, 2)
                            last.then_inc(sem(f"rg_gmm{s}"), 1)
            pe.wait_ge(*past("rg_ev0", 6 * RH))
            pe.wait_ge(*past("rg_ev1", 6 * RH))
            with pe.Fori(0, NB // 2) as i:
                for s in range(2):
                    pe.wait_ge(*past(f"f_in{s}", 96 * i + 96))
                    pe.wait_ge(*past(f"z_ready{s}", i + 1))
                    pe.wait_ge(*past(f"y_ev{s}", i))
                    for g in range(GB):
                        o = ps[:, 2 * s + g // 2, NJ * (g % 2):NJ * (g % 2) + NJ]
                        mm(o, Mb[:, s, g], Fu[:, s, g], 0, 3)
                        for r in range(2):
                            last = mm(o, Fgv[s][:, g, r, 1:1 + T, :].rearrange("p k h -> p (k h)"), Zb[:, s, r, g], 1 + r, 3)
                    last.then_inc(sem(f"f_mm{s}"), 1)
            pe.wait_ge(*past("y_in", 16))
            pe.wait_ge(*past("y_ev0", NB // 2))
            pe.wait_ge(*past("y_ev1", NB // 2))
            with pe.Fori(0, DT) as i:
                for s, src in enumerate((YT, HT)):
                    pe.wait_ge(*past(f"glu_w{s}", 16 * i + 16))
                    pe.wait_ge(*past(f"glu_ev{s}", i))
                    for t0, n in SEGS:
                        for k in range(DT):
                            last = mm(ps3[s][:, t0:t0 + n], Wv[:, s, k], src[:, k, t0:t0 + n], k, DT)
                    last.then_inc(sem(f"glu_mm{s}"), 1)
                for q in range(3):
                    pe.wait_ge(*past(f"mod1_in{q}", 16 * i + 16))
                    for k in range(DT):
                        last = mm(ps[:, 7, bass.ds(6 * i + 2 * q, 2)], modw1[:, q, k], csv[:, k, :], k, DT)
                    last.then_inc(sem(f"mod1_mm{q}"), 1)
            pe.wait_ge(*past("mix_in", 32))
            pe.wait_ge(*past("glu_ao", DT))
            with pe.Fori(0, 4) as i:
                for s in range(2):
                    pe.wait_ge(*past(f"eo_w{s}", 16 * i + 16))
                    pe.wait_ge(*past(f"eo_ev{s}", 2 * i))
                    for t0, n in SEGS:
                        for k in range(2 * DT):
                            src = AO[:, k] if k < DT else HT[:, k - DT]
                            last = mm(ps3[s][:, t0:t0 + n], WO[s][:, k], src[:, t0:t0 + n], k, 2 * DT)
                    last.then_inc(sem(f"eo_mm{s}"), 1)
            for s in range(2):
                pe.wait_ge(*past(f"eo_ev{s}", 8))
            for k in range(DT):
                square_sums(1, k)
            pe.wait_ge(*past("ml_in", 16 * 13))
            with pe.Fori(0, MT) as i:
                pe.wait_ge(*past("bd_ready", i + 1))
                pe.wait_ge(*past("fold_ev", i))
                for m in range(3):
                    last = nc.tensor.transpose(ps[:, 0, P * m:P * m + P], BD[:, m], ident[:, :])
                last.then_inc(sem("bd_t"), 1)
                pe.wait_ge(*past("bdt_ready", i + 1))
                for m in range(3):
                    last = mm(ps[:, 1, 16 * (m // 2):16 * (m // 2) + 16], BDT[:, m],
                              WIF[:, m, bass.ds(i, 1)].rearrange("p o d n -> p (o d n)"), m % 2, 2 - m // 2)
                last.then_inc(sem("fold_mm"), 1)
            pe.wait_ge(*past("ht1_ready", 16))
            pe.wait_ge(*past("fold_ev", MT))
            pe.wait_ge(*past("wf_zero", 1))
            for t0, n in SEGS:
                nc.tensor.matmul(psG[:, t0:t0 + n], WFs[:, 0, 0], XT[:, 0, t0:t0 + n], start=True, stop=False, skip_group_check=True).then_inc(sem("gates_open"), 1)
            with pe.Fori(0, MT // 2) as i:
                for s in range(2):
                    m = 2 * i + s
                    pe.wait_ge(*past(f"xm_w{s}", 16 * i + 16))
                    pe.wait_ge(*past("xm_ev", m))
                    for t0, n in SEGS:
                        for k in range(DT):
                            last = mm(ps3[0][:, t0:t0 + n], Wv[:, s, k], HT[:, k, t0:t0 + n], k, DT)
                    last.then_inc(sem(f"xm_mm{s}"), 1)
                    pe.wait_ge(*past(f"z_w{s}", 16 * i + 16))
                    pe.wait_ge(*past("z_ev", m))
                    for t0 in (0, BANK):
                        for k in range(DT):
                            last = mm(psf[:, 3 * BANK + t0:4 * BANK + t0], GZ[:, s, k], HT[:, k, CTX + t0:CTX + t0 + BANK], k, DT)
                    last.then_inc(sem(f"z_mm{s}"), 1)
                    pe.wait_ge(*past("wf_ready", m + 1))
                    pe.wait_ge(*past("xcv_ready", m + 1))
                    for t0, n in SEGS:
                        nc.tensor.matmul(psG[:, t0:t0 + n], WFs[:, s, 0], xco[:, s, t0:t0 + n], start=False, stop=False, skip_group_check=True)
                        if t0 == 0:
                            x = [(xmp[:, s, 1:1 + CTX], 0), (xmp[:, s, LOFF + 1:LOFF + 1 + CTX], CTX)]
                        else:
                            x = [(xmp[:, s, LOFF + 1 + t0 - CTX:LOFF + 1 + t0 - CTX + n], 0)]
                        for r, o in x:
                            last = nc.tensor.matmul(psG[:, t0 + o:t0 + o + r.shape[1]], WFs[:, s, 1], r, start=False, stop=False, skip_group_check=True)
                    last.then_inc(sem("gates_mm"), 1)
            pe.wait_ge(*past("rows_ready", 2))
            pe.wait_ge(*past("z_ev", MT))
            pe.wait_ge(*past("xm_ev", MT))
            pe.wait_ge(*past("em_ready", 1))
            for j in range(LBLK):
                nc.tensor.transpose(ps[:, 5, 64 * j:64 * j + 64], rA[0:64, P * j:P * j + P], ident[0:64, 0:64])
            pe.wait_ge(*past("yr_ready", 1))
            for b in range(NBLK):
                nc.tensor.transpose(psf[:, 2 * BANK + 64 * b:2 * BANK + 64 * b + 64], rB[0:64, P * b:P * b + P], ident[0:64, 0:64])
            pe.wait_ge(*past("tr_ready", 1))
            mm(ps[:, 4, 0:80], ones[0:64, :], TR.rearrange("p d h j -> p (d h j)"), 0, 1).then_inc(sem("rows_t"), 1)
            with pe.Fori(0, MH) as i:
                pe.wait_ge(*past("xc_in", 16 * i + 16))
                pe.wait_ge(*past("xo", 16 * i))
                pe.wait_ge(*past("h_ev", 8 * i))
                pe.wait_ge(*past("ybh_ready", i + 1))
                for k in range(4):
                    pe.wait_ge(*past("bdkv_ready", 4 * i + k + 1))
                    pe.wait_ge(*past("k_ev", 4 * i + k))
                    for t0, n in SEGS:
                        last = mm(ps3[0][:, t0:t0 + n], BDkv[k % 2][:, 0], Xc[:, k, t0:t0 + n], 0, 1)
                    last.then_inc(sem("k_mm"), 1)
                    pe.wait_ge(*past(f"xm_in{k % 2}", 32 * i + 16 * (k // 2) + 16))
                    pe.wait_ge(*past("vt_ev", 4 * i + k))
                    for b in range(NBLK):
                        last = mm(ps3[1][:, P * b:P * b + P], Xm[:, k % 2, P * b:P * b + P], BDkv[k % 2][:, 1], 0, 1)
                    last.then_inc(sem(f"v_mmx{k % 2}"), 1)

                def queries(th):
                    for k in range(4):
                        if k == 0:
                            pe.wait_ge(*past("ht_ev", 8 * i))
                            pe.wait_ge(*past("h_ev", 8 * i + 4 * th))
                        else:
                            pe.wait_ge(*past("q_ev", 8 * i + 4 * th + k - 1))
                        mm(ps[:, 6 + k % 2], BDq[:, k], Xc[:, k, CTX + HALF * th:CTX + HALF * th + HALF], 0, 1).then_inc(sem("q_mm"), 1)

                def scores(th):
                    pe.wait_ge(*past("q_ev", 8 * i + 4 * th + 4))
                    pe.wait_ge(*past("k_ev", 4 * i + 4))
                    for I in range(NBLK):
                        done = pieces_before(th, max(I - 1, 0))
                        pe.wait_ge(*past("p_ready", 2 * NPI * i + (NPI * th + done)))
                        for k in range(4):
                            last = mm(ps[:, I % 2], Kt[:, k, P * I:P * I + P], Qt[:, k, :], k, 4)
                        last.then_inc(sem("s_mm"), 1)

                def values(th):
                    pe.wait_ge(*past("p_ready", 2 * NPI * i + NPI * (th + 1)))
                    pe.wait_ge(*past("vt_ev", 4 * i + 4))
                    for j in range(HB_):
                        J = CBLK + HB_ * th + j
                        b0 = 2 + 2 * (j % 2)
                        pe.wait_ge(*past("h_ev", 8 * i + 4 * th + max(j - 1, 0)))
                        for d in range(2):
                            Is = [I for I in range(NBLK) if J in blocks_of(d, I, th)]
                            for n, I in enumerate(Is):
                                p = p_of(th, I, d, J)
                                mm(ps[:, b0 + d], p, Vt[:, I], n, len(Is))
                                last = mm(ps[:, 6 + j % 2, d:d + 1], p, ones[:, 0:1], n, len(Is))
                        last.then_inc(sem("pv_mm"), 1)

                def outputs(th):
                    for j in range(HB_):
                        pe.wait_ge(*past("hn_ready", 8 * i + 4 * th + j + 1))
                        pe.wait_ge(*past("ht_ev", 8 * i + 4 * th + max(j - 1, 0)))
                        for k in range(4):
                            last = nc.tensor.transpose(ps[:, 6 + j % 2, P * k:P * k + P], Hb[:, j, P * k:P * k + P], ident[:, :])
                        last.then_inc(sem("h_t"), 1)
                    pe.wait_ge(*past("mix", 2 * i + th + 1))
                    for n in range(DT):
                        pe.wait_ge(*past(f"wo_in{n % 2}", 16 * (8 * i + 4 * th + n // 2 + 1)))
                        pe.wait_ge(*past("xo", 16 * i + 8 * th + max(n - 1, 0)))
                        for k in range(4):
                            last = mm(ps[:, n % 2], WOo[:, n % 2, k], MX[:, k, :], k, 4)
                        last.then_inc(sem(f"wo_mm{n % 2}"), 1)

                pe.wait_ge(*past("bdq_ready", 4 * i + 4))
                queries(0)
                scores(0)
                values(0)
                queries(1)
                scores(1)
                outputs(0)
                values(1)
                outputs(1)
            pe.wait_ge(*past("xo", 16 * MH))
            for k in range(DT):
                pe.wait_ge(*past("sqf_ready", k + 1))
                for t in range(2):
                    last = mm(ps[:, 2 + t], ones[:, :], SQf[:, k, BANK * t:BANK * t + BANK], k, DT)
            last.then_inc(sem("ssf_mm"), 1)
            pe.wait_ge(*past("yf_ready", DT))
            for b in range(LBLK):
                if b >= 2:
                    pe.wait_ge(*past("out_ready", b - 1))
                for k in range(DT):
                    o = 4 + 2 * (b % 2) + k // 4
                    last = nc.tensor.transpose(ps[:, o, P * (k % 4):P * (k % 4) + P], YF[:, k, P * b:P * b + P], ident[:, :])
                last.then_inc(sem("yf_t"), 1)

        @block.scalar
        def _(act):
            act.wait_ge(*past("par_ready", 2))
            nc.scalar.activation(cst[:, :], PV[:, C_C:C_C + 16], ACT.Sigmoid).then_inc(sem("csig"), 1)

            def square(l, k):
                if k >= SQN[l]:
                    act.wait_ge(*past(f"ss_mm{l}", k + 1 - SQN[l]))
                nc.scalar.activation(sq[l][:, k % SQN[l]], XT[:, k], ACT.Square).then_inc(sem(f"sq_ready{l}"), 1)

            def norm(l):
                act.wait_ge(*past(f"ss_mm{l}", DT))
                for j, (t0, n) in enumerate(SEGS):
                    nc.scalar.activation(rstd[l][:, t0:t0 + n], ps[:, 4 + j, 0:n], ACT.Sqrt, bias=cols[:, 0:1], scale=1.0 / D).then_inc(sem(f"rms{l}"), 1)
                for k in range(DT):
                    for w, (t0, n) in ((1, (0, CTX)), (0, (CTX, LAT))):
                        act.wait_ge(*past(f"nt_ready{l}", 2 * k + 2 - w))
                        o, i_ = HT[:, k, t0:t0 + n], ntmp[l][:, k % 2, t0:t0 + n]
                        if l == 1 and w == 0:
                            o = o.rearrange("p (c r) -> p r c", r=ROWS)
                            i_ = i_.rearrange("p (r c) -> p r c", r=ROWS)
                        nc.scalar.activation(o, i_, ACT.Identity, bias=MODv[:, l, k, w:w + 1]).then_inc(sem(["ht_ready", "ht1_ready"][l]), 1)

            for k in range(DT):
                act.wait_ge(*past("xt_ready", 3 * k + 3))
                square(0, k)
            norm(0)
            with act.Fori(0, 4) as i:
                for s in range(2):
                    act.wait_ge(*past(f"u_mm{s}", i + 1))
                    act.wait_ge(*past(f"u_stored{s}", 16 * i))
                    nc.scalar.activation(u_stage[:, s, ::-1, :].rearrange("p s j -> p j s"),
                                         ps3[s].rearrange("p (j s) -> p j s", s=T), ACT.Copy).then_inc(sem(f"u_ev{s}"), 1)
                    act.wait_ge(*past(f"u_ev{s}", i + 1))
                    act.dma_start(u_d[bass.ds(2 * i + s, 1)].rearrange("o p t -> p (o t)"),
                                  u_stage[:, s].rearrange("p s j -> p (s j)")).then_inc(sem(f"u_stored{s}"), 16)
            act.wait_ge(*past("s5_in", 128))
            nc.scalar.activation(nat[:, 2, 1:2], nat[:, 2, 0:1], ACT.Exp).then_inc(sem("s5_dt"), 1)
            act.wait_ge(*past("s5_dar", 1))
            nc.scalar.activation(nat[:, 5], nat[:, 3], ACT.Exp).then_inc(sem("s5_mag"), 1)
            act.wait_ge(*past("s5_ang", 1))
            nc.scalar.activation(nat[:, 8], nat[:, 7], ACT.Sin)
            nc.scalar.activation(nat[:, 9], nat[:, 7], ACT.Sin, scale=0.5).then_inc(sem("s5_sin"), 1)
            act.wait_ge(*past("lam_abs", 1))
            nc.scalar.activation(lt[:, 1], lt[:, 0], ACT.Exp, scale=-1.0).then_inc(sem("lam_exp"), 1)
            with act.Fori(0, NB // 2) as i:
                for s in range(2):
                    b = 2 * i + s
                    act.wait_ge(*past(f"x_t{s}", i + 1))
                    act.wait_ge(*past(f"e_mm{1 - s}", i + s))
                    for r in range(2):
                        nc.scalar.activation(Eg[:, r].rearrange("p g c -> p (g c)"), ps[:, r], ACT.Copy).then_inc(sem("eg_ready"), 1)
                    act.wait_ge(*past(f"g_ready{s}", i + 1))
                    act.dma_start(g_d[bass.ds(b, 1)].rearrange("b p n -> p (b n)"), Gb[s]).then_inc(sem(f"g_stored{s}"), 16)
                    act.wait_ge(*past(f"e_mm{s}", i + 1))
                    for o, src in wz_moves(0, b):
                        last = nc.scalar.activation(o, src, ACT.Copy)
                    last.then_inc(sem("wz_a"), 1)
                    act.wait_ge(*past("v_ev", b + 1))
                    act.dma_start(v_d[bass.ds(GB * b, GB)].rearrange("g h c -> h g c"),
                                  Vs.rearrange("p g i h -> p g (i h)")).then_inc(sem("v_stored"), 16)
            act.wait_ge(*past("g_stored0", 16 * NB // 2))
            act.wait_ge(*past("g_stored1", 16 * NB // 2))
            act.wait_ge(*past("lam_ready", 1))
            with act.Fori(0, RH) as i:
                act.wait_ge(*past("rg_bo", 2 * i))
                for s in range(2):
                    act.wait_ge(*past(f"rg_pmm{s}", 2 * i + 1))
                    nc.scalar.activation(xrp[:, s, 1:1 + CTX], ps3[s][:, 0:CTX], ACT.Copy)
                    nc.scalar.activation(xrp[:, s, LOFF + 1:LOFF + 1 + LAT], ps3[s][:, CTX:TOK], ACT.Copy).then_inc(sem(f"rg_ev{s}"), 1)
                act.wait_ge(*past("xc_ready", 2 * i + 2))
                for s in range(2):
                    act.wait_ge(*past(f"rg_pmm{s}", 2 * i + 2))
                    nc.scalar.activation(SG[:, s], ps3[s], ACT.Sigmoid).then_inc(sem("rg_sg"), 1)
                for d in range(2):
                    act.wait_ge(*past("rg_dir", 2 * i + d))
                    for m, (dst, c0) in enumerate(((RT, C_BA), (IT, C_BX))):
                        for s in range(2):
                            act.wait_ge(*past(f"rg_gmm{s}", 4 * i + 2 * d + m + 1))
                            nc.scalar.activation(dst[:, s], ps3[s], ACT.Sigmoid, bias=PV[:, bass.ds(2 * i + (c0 + 8 * d + s), 1)]).then_inc(sem(f"rg_ev{s}"), 1)
                    for s in range(2):
                        act.wait_ge(*past(f"rg_ev{s}", 6 * i + 4 + 2 * d))
                        nc.scalar.activation(AT[:, s], RT[:, s], ACT.Exp, scale=lamc[:, bass.ds(2 * i + (8 * d + s), 1)]).then_inc(sem("rg_at"), 1)
                        act.wait_ge(*past("rg_at", 8 * i + 4 * d + 2 * s + 1))
                        nc.scalar.activation(RT[:, s], RT[:, s], ACT.Tanh, scale=lamc[:, bass.ds(2 * i + (16 + 8 * d + s), 1)]).then_inc(sem("rg_at"), 1)
                    for s in range(2):
                        act.wait_ge(*past("rg_om", 4 * i + 2 * d + s + 1))
                        nc.scalar.activation(RT[:, s], RT[:, s], ACT.Sqrt).then_inc(sem("rg_sq"), 1)
                act.wait_ge(*past("rg_bo", 2 * i + 2))
                act.dma_start(bo_d[bass.ds(2 * i, 2)].rearrange("s p t -> p s t"), HH).then_inc(sem("bo_stored"), 16)
            act.wait_ge(*past("bo_stored", 16 * RH))
            with act.Fori(0, NB // 2) as i:
                for s in range(2):
                    act.wait_ge(*past(f"f_mm{s}", i + 1))
                    act.wait_ge(*past(f"y_stored{s}", 16 * GB * i))
                    nc.scalar.activation(Yb[:, s].rearrange("p (a b) j -> p a (b j)", a=2),
                                         ps[:, 2 * s:2 * s + 2, 0:2 * NJ], ACT.Gelu_apprx_tanh).then_inc(sem(f"y_ev{s}"), 1)
                    act.wait_ge(*past(f"y_ev{s}", i + 1))
                    for g in range(GB):
                        act.dma_start(y_b[bass.ds(GB * (2 * i + s) + g, 1)].rearrange("o t h j -> (o t) h j"), Yb[:, s, g]).then_inc(sem(f"y_stored{s}"), 16)
            with act.Fori(0, DT) as i:
                act.wait_ge(*past("glu_mm0", i + 1))
                act.wait_ge(*past("glu_ao", i))
                nc.scalar.activation(SZ, ps3[0], ACT.Sigmoid, bias=PV[:, bass.ds(i + C_GLUB, 1)]).then_inc(sem("glu_ev0"), 1)
                act.wait_ge(*past("glu_mm1", i + 1))
                nc.scalar.activation(SGs, ps3[1], ACT.Sigmoid).then_inc(sem("glu_sg"), 1)
            for k in range(DT):
                act.wait_ge(*past(f"eo_ev{k % 2}", 2 * (k // 2) + 2))
                square(1, k)
            norm(1)
            with act.Fori(0, MT) as i:
                act.wait_ge(*past("bd_t", i + 1))
                nc.scalar.activation(BDT.rearrange("p m c -> p (m c)"), ps[:, 0, 0:3 * P], ACT.Copy).then_inc(sem("bdt_ready"), 1)
            with act.Fori(0, MT // 2) as i:
                for s in range(2):
                    m = 2 * i + s
                    act.wait_ge(*past(f"xm_mm{s}", i + 1))
                    act.wait_ge(*past(f"xm_stored{s}", 32 * i))
                    if s:
                        act.wait_ge(*past("gates_mm", 2 * i))
                    else:
                        act.wait_ge(*past("gates_mm", 2 * i))
                    nc.scalar.activation(xmp[:, s, 1:1 + CTX], ps3[0][:, 0:CTX], ACT.Copy)
                    nc.scalar.activation(xmp[:, s, LOFF + 1:LOFF + 1 + LAT], ps3[0][:, CTX:TOK], ACT.Copy).then_inc(sem("xm_ev"), 1)
                    act.wait_ge(*past("mcv_ready", m + 1))
                    nc.scalar.activation(mcs, mcv, ACT.Sigmoid).then_inc(sem("mcs_ready"), 1)
                    act.wait_ge(*past(f"z_mm{s}", i + 1))
                    act.wait_ge(*past(f"z_stored{s}", 16 * i))
                    nc.scalar.activation(zo[:, s], psf[:, 3 * BANK:5 * BANK], ACT.Sigmoid).then_inc(sem("zs_ready"), 1)
                    act.wait_ge(*past("xm_ev", m + 1))
                    act.dma_start(xm_d[bass.ds(m, 1), :, 0:CTX].rearrange("o p t -> p (o t)"), xmp[:, s, 1:1 + CTX]).then_inc(sem(f"xm_stored{s}"), 16)
                    act.dma_start(xm_d[bass.ds(m, 1), :, CTX:TOK].rearrange("o p t -> p (o t)"), xmp[:, s, LOFF + 1:LOFF + 1 + LAT]).then_inc(sem(f"xm_stored{s}"), 16)
                    act.wait_ge(*past("xcv_ready", m + 1))
                    act.dma_start(xc_d[bass.ds(m, 1)].rearrange("o p t -> p (o t)"), xco[:, s]).then_inc(sem(f"xcv_stored{s}"), 16)
                    act.wait_ge(*past("z_ev", m + 1))
                    act.dma_start(z_d[bass.ds(m, 1)].rearrange("o p t -> p (o t)"), zo[:, s]).then_inc(sem(f"z_stored{s}"), 16)
            act.wait_ge(*past("gates_mm", MT))
            act.wait_ge(*past("ml_in", 16 * 13))
            for n, r in enumerate((rLI, rLF)):
                nc.scalar.activation(r[0:32], psG[64 * n:64 * n + 32], ACT.Identity, bias=BI[64 * n:64 * n + 32, :])
                for o, src in zip(natural(r, slice(32, 64)), (psG[64 * n + 32:64 * n + 64, 0:CTX], psG[64 * n + 32:64 * n + 64, CTX:TOK])):
                    last = nc.scalar.activation(o, src, ACT.Identity, bias=BI[64 * n + 32:64 * n + 64, :])
                last.then_inc(sem("rows_ready"), 1)
            act.wait_ge(*past("lf_abs", 1))
            nc.scalar.activation(rA, rA, ACT.Exp, scale=-1.0).then_inc(sem("lf_exp"), 1)
            act.wait_ge(*past("m_ready", 1))
            act.wait_ge(*past("em_free", 1))
            nc.scalar.activation(rA[0:32, 0:LAT], rM[0:32, CTX:TOK], ACT.Exp, scale=-1.0)
            nc.scalar.activation(rA[32:64, 0:LAT][:, ::-1], rM[32:64, CTX:TOK], ACT.Exp, scale=-1.0).then_inc(sem("em_ready"), 1)
            act.wait_ge(*past("xr_ready", 1))
            for d in range(2):
                act.dma_start(xr_d[MH * d:MH * d + MH, :], rO[32 * d:32 * d + MH, 0:LAT]).then_inc(sem("xr_stored"), 16)
            act.wait_ge(*past("xr_stored", 32))
            with act.Fori(0, MH) as i:
                for k in range(4):
                    act.wait_ge(*past("k_mm", 4 * i + k + 1))
                    if k == 0:
                        act.wait_ge(*past("s_mm", 20 * i))
                    nc.scalar.activation(Kt[:, k], ps3[0], ACT.Copy).then_inc(sem("k_ev"), 1)

                def queries(th):
                    for k in range(4):
                        act.wait_ge(*past("q_mm", 8 * i + 4 * th + k + 1))
                        if k == 0:
                            act.wait_ge(*past("s_mm", 20 * i + 10 * th))
                        nc.scalar.activation(Qt[:, k], ps[:, 6 + k % 2], ACT.Copy).then_inc(sem("q_ev"), 1)

                def decays(th):
                    for n, (I, d, js) in enumerate(PIECES[th]):
                        u = NPI * th + n
                        act.wait_ge(*past("p_ready", 2 * NPI * i + max(u - 1, 0)))
                        for J in js:
                            if J == I:
                                x = 8 * th + sum(1 for q in PIECES[th][:n] if q[0] in q[2])
                                act.wait_ge(*past("xmask", 16 * i + x + 1))
                                src = XM[:, x % 2]
                            else:
                                src = Xb[:, d, P * (J - CBLK):P * (J - CBLK) + P]
                            last = nc.scalar.activation(Dt[:, u % 2, P * (J - js[0]):P * (J - js[0]) + P], src, ACT.Exp, bias=YBh[:, d, J, I:I + 1])
                        last.then_inc(sem("d_ready"), 1)

                def heads_out(th):
                    act.wait_ge(*past("h_t", 8 * i + 4 * th))
                    for j in range(HB_):
                        act.wait_ge(*past("rd_ready", 8 * i + 4 * th + j + 1))
                        nc.scalar.activation(Hb[:, j], ps[:, 2 + 2 * (j % 2)], ACT.Copy, scale=rden[:, 4 * th + j, 0:1]).then_inc(sem("hf_ready"), 1)
                    act.wait_ge(*past("mv_ready", 2 * i + th + 1))
                    nc.scalar.activation(mv[:, 4 * th:4 * th + 4, 1], mv[:, 4 * th:4 * th + 4, 1], ACT.Sqrt, bias=cols[:, 0:1]).then_inc(sem("sd_ready"), 1)

                act.wait_ge(*past("xb_in", 32 * i + 32))
                act.wait_ge(*past("ybh_ready", i + 1))
                queries(0)
                decays(0)
                heads_out(0)
                queries(1)
                act.wait_ge(*past("q_mm", 8 * i + 8))
                for k in range(4):
                    nc.scalar.activation(Xc[:, k, CTX:TOK], Xc[:, k, CTX:TOK], ACT.Copy, scale=PV[:, bass.ds(4 * i + (C_SK + k), 1)]).then_inc(sem("sx_ready"), 1)
                decays(1)
                nc.scalar.activation(cst[:, 0:1], cols[:, 0:1], ACT.Copy).then_inc(sem("xb_used"), 1)
                heads_out(1)
            act.wait_ge(*past("xo", 16 * MH))
            for k in range(DT):
                nc.scalar.activation(SQf[:, k], XT[:, k, CTX:TOK], ACT.Square).then_inc(sem("sqf_ready"), 1)
            act.wait_ge(*past("ssf_mm", 1))
            nc.scalar.activation(rfin, psf[:, 2 * BANK:4 * BANK], ACT.Sqrt, bias=cols[:, 0:1], scale=1.0 / D).then_inc(sem("rf_ready"), 1)
            for b in range(LBLK):
                act.wait_ge(*past("yf_t", b + 1))
                if b >= 2:
                    act.wait_ge(*past(f"out_stored{b % 2}", 16 * (b // 2)))
                nc.scalar.activation(YO[:, b % 2], psf[:, (4 + 2 * (b % 2)) * BANK:(6 + 2 * (b % 2)) * BANK], ACT.Copy).then_inc(sem("out_ready"), 1)

        @block.vector
        def _(dve):
            V = nc.vector
            link_n = [0]

            def link(ins):
                link_n[0] += 1
                ins.then_inc(sem("dve_chain"), 1)
                dve.wait_ge(*past("dve_chain", link_n[0]))

            dve.wait_ge(*past("par_t", 3))
            V.tensor_copy(PV[:, 0:232], ps[:, 7, 0:232]).then_inc(sem("par_ready"), 1)
            V.tensor_copy(PV[:, 256:320], ps[:, 7, 256:320]).then_inc(sem("par_ready"), 1)
            dve.wait_ge(*past("csig", 1))
            V.tensor_tensor(csv.rearrange("p k w -> p w k"), cst[:, :].rearrange("p (w k) -> p w k", w=2),
                            PV[:, C_C:C_C + 16].rearrange("p (w k) -> p w k", w=2), ALU.mult).then_inc(sem("cs_ready"), 1)
            for q in range(24):
                t0, n = SEGS[q % 3]
                dve.wait_ge(*past("xt_t", q + 1))
                V.tensor_copy(XT[:, q // 3, t0:t0 + n], ps[:, q % 4, 0:n]).then_inc(sem("xt_ready"), 1)

            def modulation(l):
                for s in range(2 + l):
                    dve.wait_ge(*past(f"mod{l}_mm{s}", 4 + 4 * l))
                link(V.tensor_tensor(MODv[:, l], ps[:, 7, 0:48].rearrange("p (n w) -> p n w", w=2),
                                     PV[:, C_MODB + 24 * l:C_MODB + 24 * l + 24].unsqueeze(2).to_broadcast([P, 24, 2]), ALU.add))
                link(V.scalar_tensor_tensor(out=ACv[:, l], in0=MODv[:, l, DT:2 * DT], scalar=1.0,
                                            in1=PV[:, C_NG + 8 * l:C_NG + 8 * l + 8].unsqueeze(2).to_broadcast([P, DT, 2]),
                                            op0=ALU.add, op1=ALU.mult))

            def norm(l):
                dve.wait_ge(*past(f"rms{l}", 3))
                link(V.reciprocal(rstd[l], rstd[l]))
                for k in range(DT):
                    if k >= 2:
                        dve.wait_ge(*past(["ht_ready", "ht1_ready"][l], 2 * k - 2))
                    for w, (t0, n) in ((1, (0, CTX)), (0, (CTX, LAT))):
                        V.scalar_tensor_tensor(out=ntmp[l][:, k % 2, t0:t0 + n], in0=XT[:, k, t0:t0 + n], scalar=ACv[:, l, k, w:w + 1],
                                               in1=rstd[l][:, t0:t0 + n], op0=ALU.mult, op1=ALU.mult).then_inc(sem(f"nt_ready{l}"), 1)

            modulation(0)
            norm(0)
            dve.wait_ge(*past("s5_dt", 1))
            V.tensor_scalar(nat[:, 3], nat[:, 0], nat[:, 2, 1:2], None, ALU.mult).then_inc(sem("s5_dar"), 1)
            link(V.tensor_scalar(nat[:, 4], nat[:, 1], nat[:, 2, 1:2], None, ALU.mult))
            link(V.tensor_scalar(nat[:, 6], nat[:, 4], 1.0 / (2 * math.pi), MAGIC, ALU.mult, ALU.add))
            link(V.tensor_scalar(nat[:, 6], nat[:, 6], MAGIC, None, ALU.subtract))
            src = 4
            for c in TWO_PI:
                link(V.scalar_tensor_tensor(out=nat[:, 7], in0=nat[:, 6], scalar=-c, in1=nat[:, src], op0=ALU.mult, op1=ALU.add))
                src = 7
            V.tensor_scalar(nat[:, 7], nat[:, 7], 3.1415925, -3.1415925, ALU.min, ALU.max).then_inc(sem("s5_ang"), 1)
            link(V.tensor_tensor(nat[:, 13], nat[:, 0], nat[:, 0], ALU.mult))
            link(V.tensor_tensor(nat[:, 14], nat[:, 1], nat[:, 1], ALU.mult))
            link(V.tensor_tensor(nat[:, 13], nat[:, 13], nat[:, 14], ALU.add))
            link(V.reciprocal(nat[:, 13], nat[:, 13]))
            dve.wait_ge(*past("s5_mag", 1))
            dve.wait_ge(*past("s5_sin", 1))
            link(V.tensor_tensor(nat[:, 10], nat[:, 9], nat[:, 9], ALU.mult))
            link(V.tensor_scalar(nat[:, 10], nat[:, 10], -2.0, 1.0, ALU.mult, ALU.add))
            link(V.tensor_tensor(nat[:, 11], nat[:, 5], nat[:, 10], ALU.mult))
            link(V.tensor_tensor(nat[:, 12], nat[:, 5], nat[:, 8], ALU.mult))
            link(V.tensor_scalar(nat[:, 15], nat[:, 11], 1.0, None, ALU.subtract))
            link(V.tensor_tensor(nat[:, 14], nat[:, 15], nat[:, 0], ALU.mult))
            link(V.tensor_tensor(nat[:, 16], nat[:, 12], nat[:, 1], ALU.mult))
            link(V.tensor_tensor(nat[:, 14], nat[:, 14], nat[:, 16], ALU.add))
            link(V.tensor_tensor(nat[:, 17], nat[:, 14], nat[:, 13], ALU.mult))
            link(V.tensor_tensor(nat[:, 16], nat[:, 12], nat[:, 0], ALU.mult))
            link(V.tensor_tensor(nat[:, 19], nat[:, 15], nat[:, 1], ALU.mult))
            link(V.tensor_tensor(nat[:, 16], nat[:, 16], nat[:, 19], ALU.subtract))
            V.tensor_tensor(nat[:, 18], nat[:, 16], nat[:, 13], ALU.mult).then_inc(sem("s5_nat"), 1)
            link(V.tensor_scalar(lt[:, 0], PV[:, C_LAM:C_LAM + 16], -1.0, None, ALU.mult))
            link(V.tensor_scalar(lt[:, 4], lt[:, 0], 0.0, None, ALU.max))
            V.tensor_tensor(lt[:, 0], lt[:, 0], PV[:, C_LAM:C_LAM + 16], ALU.max).then_inc(sem("lam_abs"), 1)
            dve.wait_ge(*past("lam_exp", 1))
            log1p(link, lt[:, 1], lt[:, 2], lt[:, 3], lt[:, 5])
            link(V.tensor_tensor(lt[:, 4], lt[:, 4], lt[:, 5], ALU.add))
            link(V.tensor_scalar(lamc[:, 0:16], lt[:, 4], -8.0, None, ALU.mult))
            V.tensor_scalar(lamc[:, 16:32], lt[:, 4], 8.0, None, ALU.mult).then_inc(sem("lam_ready"), 1)
            dve.wait_ge(*past("s5_at", 1))
            for v in range(4):
                for d in range(2):
                    last = V.tensor_copy(AL[64 * d:64 * d + 64, v], ps[64 * (v % 2):64 * (v % 2) + 64, 6, P * (v // 2) + 64 * d:P * (v // 2) + 64 * d + 64])
            link(last)
            for w, dst in enumerate((BT, CT)):
                dve.wait_ge(*past("s5_bct", w + 1))
                for q in range(4):
                    for r in range(2):
                        for d in range(2):
                            V.tensor_copy(dst[64 * d:64 * d + 64, r, 4 * q:4 * q + 4, :],
                                          ps[64 * r:64 * r + 64, q].rearrange("p (h c) -> p h c", h=4)[:, :, 64 * d:64 * d + 64]).then_inc(sem(("s5_bt", "s5_ct")[w]), 1)
            dve.wait_ge(*past("s5_ct", 16))
            V.tensor_copy(sa[:, 0, 0], AL[:, 0])
            V.tensor_copy(sa[:, 0, 1], AL[:, 0])
            V.tensor_scalar(sa[:, 1, 0], AL[:, 1], -1.0, None, ALU.mult)
            V.tensor_copy(sa[:, 1, 1], AL[:, 1])
            V.memset(Q[:, 0, 0], 1.0)
            V.memset(Q[:, 0, 1], 0.0)
            link(V.tensor_copy(Q[:, 1], AL[:, 0:2]))
            for k in range(2, SL):
                V.tensor_tensor(Q[:, k], Q[:, k - 1], sa[:, 0], ALU.mult)
                link(V.tensor_tensor(sa[:, 2], Q[:, k - 1, ::-1], sa[:, 1], ALU.mult))
                link(V.tensor_tensor(Q[:, k], Q[:, k], sa[:, 2], ALU.add))
            V.tensor_copy(A1[:, 0], Q[:, T, 0])
            V.tensor_copy(A1[:, 1], Q[:, T, 0])
            V.tensor_scalar(A2[:, 1], Q[:, T, 1], -1.0, None, ALU.mult)
            V.tensor_copy(A2[:, 0], Q[:, T, 1])
            f, bk = slice(0, 64), slice(64, 128)
            V.tensor_copy(PWE[f], Q[f, 0:T])
            V.tensor_copy(PWE[bk], Q[bk, T - 1::-1])
            V.tensor_copy(PWF[f, :, 0], Q[f, :, 0])
            V.tensor_copy(PWF[bk, :, 0], Q[bk, ::-1, 0])
            V.tensor_scalar(PWF[f, :, 1], Q[f, :, 1], -1.0, None, ALU.mult)
            V.tensor_scalar(PWF[bk, :, 1], Q[bk, ::-1, 1], -1.0, None, ALU.mult)
            co = [AL[:, 2 + r:3 + r].to_broadcast([P, 2 * HC, G]) for r in range(2)]
            V.tensor_tensor(BB.rearrange("p r h g -> p (r h) g"), BT.rearrange("p r h g -> p (r h) g"), co[0], ALU.mult)
            for r in range(2):
                last = V.tensor_tensor(tB[:, r], BT[:, 1 - r], co[1][:, 0:HC], ALU.mult)
            link(last)
            V.tensor_tensor(BB[:, 0], BB[:, 0], tB[:, 0], ALU.subtract)
            link(V.tensor_tensor(BB[:, 1], BB[:, 1], tB[:, 1], ALU.add))
            link(V.tensor_tensor(Dg, ident[0:HC, 0:HC].unsqueeze(1).to_broadcast([HC, G, HC]), dcol.unsqueeze(2).to_broadcast([HC, G, HC]), ALU.mult))
            V.memset(sa[:, 2, 0, 0:1], 0.0).then_inc(sem("s5_tables"), 1)
            dve.wait_ge(*past("s5_tables", 1))
            n0, per = link_n[0], 4
            with dve.Fori(0, NB // 2) as i:
                k = 0
                for s in range(2):
                    b = 2 * i + s
                    gs = bass.ds(GB * b, GB)

                    def pw(r):
                        return PWE[:, :, r, gs].rearrange("p k g -> p g k").unsqueeze(2).to_broadcast([P, GB, HC, T])

                    def bb(r):
                        return BB[:, r, :, gs].rearrange("p h g -> p g h").unsqueeze(3).to_broadcast([P, GB, HC, T])

                    def xo(ap):
                        return ap.rearrange("p (g h k) -> p g h k", g=GB, h=HC)

                    dve.wait_ge(*past(f"x_t{s}", i))
                    x = [X[:, s, r].rearrange("p g c -> p (g c)") for r in range(2)]
                    V.tensor_tensor(xo(x[0]), pw(0), bb(0), ALU.mult)
                    V.tensor_tensor(xo(xt1), pw(1), bb(1), ALU.mult)
                    V.tensor_tensor(xo(x[1]), pw(0), bb(1), ALU.mult)
                    V.tensor_tensor(xo(xt2), pw(1), bb(0), ALU.mult).then_inc(sem("dve_chain"), 1)
                    k += 1
                    dve.wait_ge(*past("dve_chain", per * i + (n0 + k)))
                    V.tensor_tensor(x[0], x[0], xt1, ALU.subtract)
                    V.tensor_tensor(x[1], x[1], xt2, ALU.add).then_inc(sem(f"x_ready{s}"), 1)
                    dve.wait_ge(*past(f"v_mm{s}", i + 1))
                    dve.wait_ge(*past("v_stored", 16 * b))
                    bank = [ps[0:HC, 6 + d].rearrange("p (g k h) -> p g k h", g=GB, h=HC) for d in range(2)]
                    V.tensor_copy(Vs[:, :, 0:T], bank[1])
                    V.tensor_copy(Vs[:, :, T:LAG], bank[0][:, :, 1:T])
                    V.tensor_copy(vtmp, bank[1][:, :, T - 1]).then_inc(sem("dve_chain"), 1)
                    k += 1
                    dve.wait_ge(*past("dve_chain", per * i + (n0 + k)))
                    V.tensor_tensor(Vs[:, :, T - 1], bank[0][:, :, 0], vtmp, ALU.add).then_inc(sem("v_mid"), 1)
                    dve.wait_ge(*past("v_mid", b + 1))
                    V.tensor_tensor(Vs[:, :, T - 1], Vs[:, :, T - 1], Dg[:, gs], ALU.add).then_inc(sem("v_ev"), 1)
                    dve.wait_ge(*past(f"e_mm{s}", i + 1))
                    for o, src in wz_moves(1, b):
                        last = V.tensor_copy(o, src)
                    last.then_inc(sem("wz_v"), 1)
                assert k == per
            link_n[0] = n0 + per * (NB // 2)
            dve.wait_ge(*past("g_stored0", 16 * NB // 2))
            dve.wait_ge(*past("g_stored1", 16 * NB // 2))
            dve.wait_ge(*past("e_mm0", NB // 2))
            dve.wait_ge(*past("e_mm1", NB // 2))
            n0, per = link_n[0], 17
            with dve.Fori(0, RH) as i:
                k = [0]

                def ilink(ins):
                    k[0] += 1
                    ins.then_inc(sem("dve_chain"), 1)
                    dve.wait_ge(*past("dve_chain", per * i + (n0 + k[0])))

                dve.wait_ge(*past("rg_bo", 2 * i))
                for s in range(2):
                    V.memset(xrp[:, s, 0:1], 0.0)
                    V.memset(xrp[:, s, CTX + 1:LOFF + 1], 0.0)
                    last = V.memset(xrp[:, s, PAD - 2:PAD], 0.0)
                ilink(last)
                for s in range(2):
                    def tap(j):
                        return PV[:, bass.ds(2 * i + (C_RCW + 8 * j + s), 1)]

                    dve.wait_ge(*past(f"rg_ev{s}", 6 * i + 1))
                    dve.wait_ge(*past("xc_ready", 2 * i + s))
                    ilink(V.tensor_scalar(TT, xrp[:, s, 0:CV], tap(0), PV[:, bass.ds(2 * i + (C_RCB + s), 1)], ALU.mult, ALU.add))
                    for j in (1, 2):
                        ilink(V.scalar_tensor_tensor(out=TT, in0=xrp[:, s, j:j + CV], scalar=tap(j), in1=TT, op0=ALU.mult, op1=ALU.add))
                    V.scalar_tensor_tensor(out=xcb[:, s, 0:CTX], in0=xrp[:, s, 3:3 + CTX], scalar=tap(3), in1=TT[:, 0:CTX], op0=ALU.mult, op1=ALU.add)
                    V.scalar_tensor_tensor(out=xcb[:, s, CTX:TOK], in0=xrp[:, s, LOFF + 3:PAD], scalar=tap(3), in1=TT[:, LOFF:CV], op0=ALU.mult, op1=ALU.add).then_inc(sem("xc_ready"), 1)
                for s in range(2):
                    dve.wait_ge(*past("rg_sg", 2 * i + s + 1))
                    V.tensor_tensor(SG[:, s], ps3[s], SG[:, s], ALU.mult).then_inc(sem(f"rg_ev{s}"), 1)
                for d in range(2):
                    for s in range(2):
                        dve.wait_ge(*past("rg_at", 8 * i + 4 * d + 2 * s + 2))
                        ilink(V.tensor_tensor(TT[:, 0:TOK], AT[:, s], AT[:, s], ALU.mult))
                        V.scalar_tensor_tensor(out=RT[:, s], in0=TT[:, 0:TOK], scalar=1.0, in1=RT[:, s], op0=ALU.add, op1=ALU.mult).then_inc(sem("rg_om"), 1)
                        dve.wait_ge(*past("rg_om", 4 * i + 2 * d + s + 1))
                    for s in range(2):
                        last = V.tensor_tensor(IT[:, s], IT[:, s], xcb[:, s], ALU.mult)
                    ilink(last)
                    for s in range(2):
                        dve.wait_ge(*past("rg_sq", 4 * i + 2 * d + s + 1))
                        last = V.tensor_tensor(IT[:, s], IT[:, s], RT[:, s], ALU.mult)
                    ilink(last)
                    if d == 0:
                        dve.wait_ge(*past("bo_stored", 16 * i))
                        for s in range(2):
                            last = V.tensor_tensor_scan(HH[:, s], AT[:, s], IT[:, s], 0.0, ALU.mult, ALU.add)
                        last.then_inc(sem("rg_dir"), 1)
                    else:
                        for s in range(2):
                            a, v, o = (z[:, s, 0:CTX][:, ::-1] for z in (AT, IT, RT))
                            last = V.tensor_tensor_scan(o, a, v, 0.0, ALU.mult, ALU.add)
                        ilink(last)
                        for s in range(2):
                            a, v, o = (z[:, s, CTX:TOK][:, ::-1] for z in (AT, IT, RT))
                            last = V.tensor_tensor_scan(o, a, v, RT[:, s, 0:1], ALU.mult, ALU.add)
                        ilink(last)
                        for s in range(2):
                            last = V.tensor_tensor(HH[:, s], HH[:, s], RT[:, s], ALU.add)
                        last.then_inc(sem("rg_dir"), 1)
                        dve.wait_ge(*past("rg_dir", 2 * i + 2))
                        for s in range(2):
                            V.tensor_tensor(HH[:, s], HH[:, s], SG[:, s], ALU.mult).then_inc(sem("rg_bo"), 1)
                assert k[0] == per, k
            link_n[0] = n0 + per * RH
            dve.wait_ge(*past("bo_stored", 16 * RH))
            dve.wait_ge(*past("scan", 4 * NJ))
            with dve.Fori(0, NB // 2) as i:
                for s in range(2):
                    gs = bass.ds(GB * (2 * i + s), GB)
                    dve.wait_ge(*past(f"f_mm{s}", i))

                    def take(rw, steps):
                        return WZ[rw, steps, :, gs].rearrange("p j r g -> p r g j")

                    V.tensor_copy(Zb[f, s], take(f, slice(0, NJ)))
                    V.tensor_copy(Zb[bk, s, :, :, 0:NJC][:, :, :, ::-1], take(bk, slice(0, NJC)))
                    V.tensor_copy(Zb[bk, s, :, :, NJC:NJ][:, :, :, ::-1], take(bk, slice(NJC, NJ))).then_inc(sem(f"z_ready{s}"), 1)
            n0, per = link_n[0], 1
            dve.wait_ge(*past("y_in", 16))
            with dve.Fori(0, DT) as i:
                dve.wait_ge(*past("glu_sg", i + 1))
                V.tensor_tensor(SGs, ps3[1], SGs, ALU.mult).then_inc(sem("glu_ev1"), 1)
                dve.wait_ge(*past("glu_ev0", i + 1))
                V.tensor_tensor(SZ, SZ, YT[:, bass.ds(i, 1)].rearrange("p k t -> p (k t)"), ALU.mult).then_inc(sem("dve_chain"), 1)
                dve.wait_ge(*past("dve_chain", i + (n0 + 1)))
                dve.wait_ge(*past("glu_ev1", i + 1))
                V.tensor_tensor(AO[:, bass.ds(i, 1)].rearrange("p k (j t) -> p (k j) t", t=T), SZ.rearrange("p (t j) -> p j t", t=T),
                                SGs.rearrange("p (j t) -> p j t", t=T), ALU.mult).then_inc(sem("glu_ao"), 1)
            link_n[0] = n0 + DT
            dve.wait_ge(*past("mix_in", 32))

            with dve.Fori(0, 4) as i:
                for s in range(2):
                    dve.wait_ge(*past(f"eo_mm{s}", i + 1))
                    for w, (t0, n) in ((1, (0, CTX)), (0, (CTX, LAT))):
                        x = XT[:, bass.ds(2 * i + s, 1), t0:t0 + n].rearrange("p k t -> p (k t)")
                        V.scalar_tensor_tensor(out=x, in0=ps3[s][:, t0:t0 + n], scalar=MOD[:, bass.ds(4 * i + (2 * (16 + s) + w), 1)],
                                               in1=x, op0=ALU.mult, op1=ALU.add).then_inc(sem(f"eo_ev{s}"), 1)
            modulation(1)
            dve.wait_ge(*past("eo_ev0", 8))
            dve.wait_ge(*past("eo_ev1", 8))
            norm(1)
            with dve.Fori(0, MT) as i:
                dve.wait_ge(*past("fold_mm", i + 1))
                V.tensor_copy(WFc[:, bass.ds(i, 1)].rearrange("p t w n -> p (t w n)"), ps[:, 1, 0:32]).then_inc(sem("fold_ev"), 1)
            for s in range(2):
                V.memset(xmp[:, s, 0:1], 0.0)
                V.memset(xmp[:, s, CTX + 1:LOFF + 1], 0.0)
                last = V.memset(xmp[:, s, PAD - 2:PAD], 0.0)
            link(last)
            n0, per = link_n[0], 6
            with dve.Fori(0, MT // 2) as i:
                k = [0]

                def ilink(ins):
                    k[0] += 1
                    ins.then_inc(sem("dve_chain"), 1)
                    dve.wait_ge(*past("dve_chain", per * i + (n0 + k[0])))

                for s in range(2):
                    m = 2 * i + s

                    def tap(j):
                        return PV[:, bass.ds(2 * i + (C_MCW + MT * j + s), 1)]

                    dve.wait_ge(*past("xm_ev", m + 1))
                    dve.wait_ge(*past("xcv_ready", m))
                    ilink(V.tensor_scalar(mcv, xmp[:, s, 0:CV], tap(0), PV[:, bass.ds(2 * i + (C_MCB + s), 1)], ALU.mult, ALU.add))
                    for j in (1, 2):
                        ilink(V.scalar_tensor_tensor(out=mcv, in0=xmp[:, s, j:j + CV], scalar=tap(j), in1=mcv, op0=ALU.mult, op1=ALU.add))
                    V.scalar_tensor_tensor(out=mcv, in0=xmp[:, s, 3:3 + CV], scalar=tap(3), in1=mcv, op0=ALU.mult, op1=ALU.add).then_inc(sem("mcv_ready"), 1)
                    dve.wait_ge(*past("mcs_ready", m + 1))
                    dve.wait_ge(*past(f"xcv_stored{s}", 16 * i))
                    dve.wait_ge(*past("gates_mm", 2 * i))
                    V.tensor_tensor(xco[:, s, 0:CTX], mcv[:, 0:CTX], mcs[:, 0:CTX], ALU.mult)
                    V.tensor_tensor(xco[:, s, CTX:TOK], mcv[:, LOFF:CV], mcs[:, LOFF:CV], ALU.mult).then_inc(sem("xcv_ready"), 1)
                    dve.wait_ge(*past("zs_ready", m + 1))
                    V.tensor_tensor(zo[:, s], psf[:, 3 * BANK:5 * BANK], zo[:, s], ALU.mult).then_inc(sem("z_ev"), 1)
                assert k[0] == per, k
            link_n[0] = n0 + per * (MT // 2)
            dve.wait_ge(*past("rows_ready", 2))
            link(V.tensor_scalar(rA, rLF, -1.0, None, ALU.mult))
            V.tensor_tensor(rA, rA, rLF, ALU.max).then_inc(sem("lf_abs"), 1)
            link(V.memset(rRes, 1.0))
            link(V.memset(rRes.rearrange("p (b c) -> p b c", c=P)[:, :, 0], 0.0))
            dve.wait_ge(*past("lf_exp", 1))
            log1p(link, rA, rB, rC, rM)
            link(V.tensor_scalar(rLF, rLF, 0.0, None, ALU.min))
            link(V.tensor_tensor(rLF, rLF, rM, ALU.subtract))
            V.memset(TR[:, 0, 0, 0:1], 0.0).then_inc(sem("em_free"), 1)
            link(V.tensor_tensor_scan(rC, rRes, rLF, 0.0, ALU.mult, ALU.add))
            V.tensor_tensor_scan(rM, rLF, rLI, 0.0, ALU.add, ALU.max).then_inc(sem("m_ready"), 1)
            dve.wait_ge(*past("m_ready", 1))
            V.tensor_tensor(rO[0:32, 0:LAT], rC[0:32, CTX:TOK], rM[0:32, CTX:TOK], ALU.subtract)
            V.tensor_tensor(rO[32:64, 0:LAT][:, ::-1], rC[32:64, CTX:TOK], rM[32:64, CTX:TOK], ALU.subtract).then_inc(sem("xr_ready"), 1)
            V.tensor_tensor(rB[0:32], rLI[0:32], rC[0:32], ALU.subtract)
            for o, (t0, n) in zip(natural(rB, slice(32, 64)), ((0, CTX), (CTX, LAT))):
                last = V.tensor_tensor(o, rLI[32:64, t0:t0 + n], rC[32:64, t0:t0 + n], ALU.subtract)
            last.then_inc(sem("yr_ready"), 1)
            idl = ident[0:64, 0:64].rearrange("p (d h) -> p d h", d=2)[:, :, 0:MH].unsqueeze(3).to_broadcast([64, 2, MH, NBLK])
            tbl = rC.rearrange("p (b c) -> p b c", c=P)[:, :, P - 1].unsqueeze(1).unsqueeze(1).to_broadcast([64, 2, MH, NBLK])
            dve.wait_ge(*past("em_free", 1))
            V.tensor_tensor(TR, idl, tbl, ALU.mult).then_inc(sem("tr_ready"), 1)
            dve.wait_ge(*past("rows_t", 1))
            yt = psf[:, 2 * BANK:2 * BANK + 640].rearrange("p (b c) -> p b c", c=64)
            for d in range(2):
                diag = at(K1 + 192 + 400 * d, 400).rearrange("p (j i h) -> p (j i) h", j=NBLK, i=NBLK)[:, 0::NBLK + 1]
                V.tensor_copy(diag, yt[:, :, 32 * d:32 * d + MH])
            V.tensor_copy(TB, ps[:, 4, 0:80].rearrange("p (d h j) -> p d h j", d=2, h=MH))
            link(V.tensor_copy(EMT, ps[:, 5].rearrange("p (j d c) -> p j d c", j=LBLK, d=2)[:, :, :, 0:MH]))
            for q in range(NBLK - 1):
                for d in range(2):
                    t = TB[:, d, :, q]
                    nat_ = {step_of(d, I): I for I in range(NBLK)}
                    J0, J1 = nat_[q], nat_[q + 1]
                    done = sorted(nat_[x] for x in range(q + 1))
                    runs = []
                    for I in done:
                        if runs and runs[-1][-1] == I - 1:
                            runs[-1].append(I)
                        else:
                            runs.append([I])
                    for r in runs:
                        sl = slice(r[0], r[-1] + 1)
                        last = V.tensor_tensor(YB[:, d, J1, sl], YB[:, d, J0, sl], t.unsqueeze(1).to_broadcast([P, len(r), MH]), ALU.add)
                link(last)
            n0, per = link_n[0], 20
            with dve.Fori(0, MH) as i:
                k_ = [0]

                def ilink(ins):
                    k_[0] += 1
                    ins.then_inc(sem("dve_chain"), 1)
                    dve.wait_ge(*past("dve_chain", per * i + (n0 + k_[0])))

                dve.wait_ge(*past("d_ready", 2 * NPI * i))
                V.tensor_copy(EMh, EMT[:, :, :, bass.ds(i, 1)].rearrange("p j d o -> p j (d o)"))
                V.tensor_copy(YBh.rearrange("p d j i -> p (d j i)"), YB[:, :, :, :, bass.ds(i, 1)].rearrange("p d j i o -> p (d j i o)")).then_inc(sem("ybh_ready"), 1)
                for k in range(4):
                    dve.wait_ge(*past(f"v_mmx{k % 2}", 2 * i + k // 2 + 1))
                    if k == 0:
                        dve.wait_ge(*past("pv_mm", 8 * i))
                    V.tensor_copy(Vt[:, :, P * k:P * k + P], ps3[1].rearrange("p (b c) -> p b c", c=P)).then_inc(sem("vt_ev"), 1)

                def weigh(th):
                    for n, (I, d, js) in enumerate(PIECES[th]):
                        u = NPI * th + n
                        if n == 0 or PIECES[th][n - 1][0] != I:
                            dve.wait_ge(*past("s_mm", 20 * i + 10 * th + I + 1))
                        dve.wait_ge(*past("d_ready", 2 * NPI * i + u + 1))
                        if n == 0:
                            dve.wait_ge(*past("pv_mm", 8 * i + 4 * th))
                        w_ = P * len(js)
                        c0 = P * (js[0] - CBLK - HB_ * th)
                        o = POFF[th][I, d]
                        V.scalar_tensor_tensor(out=Pm[:, o:o + w_], in0=ps[:, I % 2, c0:c0 + w_], scalar=MD ** -0.5,
                                               in1=Dt[:, u % 2, 0:w_], op0=ALU.mult, op1=ALU.mult).then_inc(sem("p_ready"), 1)

                def heads_out(th):
                    for j in range(HB_):
                        q = 4 * th + j
                        dve.wait_ge(*past("pv_mm", 8 * i + q + 1))
                        ilink(V.tensor_tensor(rden[:, q], ps[:, 6 + j % 2, 0:2], EMh[:, q], ALU.max))
                        ilink(V.scalar_tensor_tensor(out=rden[:, q], in0=ps[:, 6 + j % 2, 0:2], scalar=-1.0, in1=rden[:, q], op0=ALU.mult, op1=ALU.max))
                        V.reciprocal(rden[:, q], rden[:, q]).then_inc(sem("rd_ready"), 1)
                        dve.wait_ge(*past("hf_ready", 8 * i + q + 1))
                        V.scalar_tensor_tensor(out=Hb[:, j], in0=ps[:, 3 + 2 * (j % 2)], scalar=rden[:, q, 1:2], in1=Hb[:, j],
                                               op0=ALU.mult, op1=ALU.add).then_inc(sem("h_ev"), 1)
                        dve.wait_ge(*past("h_ev", 8 * i + q + 1))
                        last = V.bn_stats(bst[:, q], Hb[:, j])
                        if j == HB_ - 1:
                            ilink(last)
                    V.tensor_copy(lt[:, 0, 0:1], bst[:, 4 * th, 0:1])
                    for j in range(HB_):
                        last = V.bn_aggr(mv[:, 4 * th + j], bst[:, 4 * th + j])
                    last.then_inc(sem("mv_ready"), 1)
                    dve.wait_ge(*past("sd_ready", 2 * i + th + 1))
                    ilink(V.reciprocal(mv[:, 4 * th:4 * th + 4, 1], mv[:, 4 * th:4 * th + 4, 1]))
                    for j in range(HB_):
                        m_ = mv[:, 4 * th + j]
                        V.tensor_scalar(Hb[:, j], Hb[:, j], m_[:, 0:1], m_[:, 1:2], ALU.subtract, ALU.mult).then_inc(sem("hn_ready"), 1)

                def mixed(th):
                    dve.wait_ge(*past("sx_ready", 4 * i + 4))
                    dve.wait_ge(*past("wo_mm0", 8 * i + 4 * th))
                    dve.wait_ge(*past("wo_mm1", 8 * i + 4 * th))
                    for j in range(HB_):
                        dve.wait_ge(*past("h_t", 8 * i + 4 * th + j + 1))
                        for k in range(4):
                            t0 = HALF * th + P * j
                            last = V.scalar_tensor_tensor(out=MX[:, k, P * j:P * j + P], in0=ps[:, 6 + j % 2, P * k:P * k + P],
                                                          scalar=PV[:, bass.ds(4 * i + (C_MG + k), 1)], in1=Xc[:, k, CTX + t0:CTX + t0 + P],
                                                          op0=ALU.mult, op1=ALU.add)
                        last.then_inc(sem("ht_ev"), 1)
                    dve.wait_ge(*past("ht_ev", 8 * i + 4 * th + 4))
                    dve.wait_ge(*past("zt_in", 32 * i + 16 * th + 16))
                    V.tensor_tensor(MX, MX, Zt, ALU.mult).then_inc(sem("mix"), 1)
                    for n in range(DT):
                        dve.wait_ge(*past(f"wo_mm{n % 2}", 8 * i + 4 * th + n // 2 + 1))
                        x = XT[:, n, CTX:TOK].rearrange("p (r c) -> p c r", r=ROWS)[:, 32 * th:32 * th + 32]
                        V.scalar_tensor_tensor(out=x, in0=ps[:, n % 2].rearrange("p (c r) -> p c r", r=ROWS), scalar=gs1[:, n, 0:1],
                                               in1=x, op0=ALU.mult, op1=ALU.add).then_inc(sem("xo"), 1)

                weigh(0)
                heads_out(0)
                weigh(1)
                mixed(0)
                heads_out(1)
                mixed(1)
                assert k_[0] == per
            link_n[0] = n0 + per * MH
            dve.wait_ge(*past("rf_ready", 1))
            link(V.reciprocal(rfin, rfin))
            for k in range(DT):
                V.scalar_tensor_tensor(out=YF[:, k], in0=XT[:, k, CTX:TOK], scalar=PV[:, C_FG + k:C_FG + k + 1], in1=rfin,
                                       op0=ALU.mult, op1=ALU.mult).then_inc(sem("yf_ready"), 1)

        @block.gpsimd
        def _(pool):
            GP = nc.gpsimd
            GP.memset(ident[:, :], 0.0).then_inc(sem("consts"), 1)
            GP.memset(ones[:, :], 1.0).then_inc(sem("consts"), 1)
            GP.memset(cols[:, :], EPS).then_inc(sem("consts"), 1)
            pool.wait_ge(*past("consts", 3))
            GP.affine_select(out=ident[:, :], in_=ident[:, :], compare_op=ALU.not_equal, fill=1.0, base=0,
                             pattern=[[-1, P]], channel_multiplier=1).then_inc(sem("consts"), 1)
            pool.wait_ge(*past("s5_tables", 1))
            with pool.Fori(0, NB // 2) as i:
                for s in range(2):
                    gs = bass.ds(GB * (2 * i + s), GB)

                    def pw(r):
                        return PWF[:, :, r, gs].rearrange("p k g -> p g k").unsqueeze(3).to_broadcast([P, GB, SL, HC])

                    def cc(r):
                        return CT[:, r, :, gs].rearrange("p h g -> p g h").unsqueeze(2).to_broadcast([P, GB, SL, HC])

                    def go(ap):
                        return ap.rearrange("p (g k h) -> p g k h", g=GB, h=HC)

                    pool.wait_ge(*past(f"v_mm{s}", i))
                    pool.wait_ge(*past(f"g_stored{s}", 16 * i))
                    pool.wait_ge(*past(f"g_ready{1 - s}", i + s))
                    pool.wait_ge(*past("s5_tables", 1))
                    GP.tensor_copy(BBv[:, s], BB[:, :, :, gs])
                    GP.tensor_tensor(Gv[s][:, :, 0], pw(0), cc(0), ALU.mult)
                    GP.tensor_tensor(go(pg1), pw(1), cc(1), ALU.mult)
                    GP.tensor_tensor(Gv[s][:, :, 1], pw(1), cc(0), ALU.mult)
                    GP.tensor_tensor(go(pg2), pw(0), cc(1), ALU.mult).then_inc(sem("pool_g"), 1)
                    pool.wait_ge(*past("pool_g", 2 * i + (s + 1)))
                    pool.wait_ge(*past("s5_tables", 1))
                    GP.tensor_tensor(Gv[s][:, :, 0], Gv[s][:, :, 0], go(pg1), ALU.add)
                    GP.tensor_tensor(Gv[s][:, :, 1], Gv[s][:, :, 1], go(pg2), ALU.subtract).then_inc(sem(f"g_ready{s}"), 1)
            pool.wait_ge(*past("wz_a", NB))
            pool.wait_ge(*past("wz_v", NB))
            pool.wait_ge(*past("lam_ready", 1))
            GP.memset(WZ[:, 0], 0.0).then_inc(sem("scan0"), 1)
            pool.wait_ge(*past("scan0", 1))
            with pool.Fori(0, NJ) as i:
                z = WZ[:, bass.ds(i, 1)].rearrange("p j r g -> p (j r) g")
                w = WZ[:, bass.ds(i + 1, 1)].rearrange("p j r g -> p (j r) g")
                pool.wait_ge(*past("scan", 4 * i))
                pool.wait_ge(*past("scan0", 1))
                GP.tensor_tensor(SP1, z, A1, ALU.mult).then_inc(sem("scan"), 1)
                GP.tensor_tensor(SP2[:, ::-1], z, A2, ALU.mult).then_inc(sem("scan"), 1)
                pool.wait_ge(*past("scan", 4 * i + 2))
                GP.tensor_tensor(SP1, SP1, SP2, ALU.add).then_inc(sem("scan"), 1)
                pool.wait_ge(*past("scan", 4 * i + 3))
                pool.wait_ge(*past("scan0", 1))
                GP.tensor_tensor(w, w, SP1, ALU.add).then_inc(sem("scan"), 1)
            pool.wait_ge(*past("bo_stored", 16 * RH))
            with pool.Fori(0, DT) as i:
                for q in range(3):
                    pool.wait_ge(*past(f"mod1_mm{q}", i))
                    pool.dma_start(modw1[:, q], mod_v[1][:, :, bass.ds((3 * i + q) * P, P)]).then_inc(sem(f"mod1_in{q}"), 16)
            pool.wait_ge(*past("glu_ao", DT))
            GP.memset(BI[:, :], 0.0).then_inc(sem("bi_zero"), 1)
            GP.memset(bmask, 1.0).then_inc(sem("bm"), 1)
            pool.wait_ge(*past("bm", 1))
            GP.affine_select(out=bmask, in_=bmask, compare_op=ALU.is_ge, fill=0.0, base=0, pattern=[[-4, 32], [0, 4]], channel_multiplier=1).then_inc(sem("bm"), 1)
            pool.wait_ge(*past("bm", 2))
            GP.affine_select(out=bmask, in_=bmask, compare_op=ALU.is_ge, fill=0.0, base=3, pattern=[[4, 32], [0, 4]], channel_multiplier=-1).then_inc(sem("bm"), 1)
            GP.memset(WFs, 0.0).then_inc(sem("wf_zero"), 1)
            pool.wait_ge(*past("wf_zero", 1))
            pool.wait_ge(*past("bm", 3))
            pool.wait_ge(*past("ml_in", 16 * 13))

            def block_diagonal(o, m, t):
                return GP.tensor_tensor(o.rearrange("p (b o) -> p b o", o=4), bmask, W4[:, m, bass.ds(t, 1)].to_broadcast([P, 32, 4]), ALU.mult)

            with pool.Fori(0, MT) as i:
                pool.wait_ge(*past("bd_t", i))
                pool.wait_ge(*past("bm", 3))
                for m in range(3):
                    last = block_diagonal(BD[:, m], m, i)
                last.then_inc(sem("bd_ready"), 1)
            pool.wait_ge(*past("fold_ev", MT))
            pool.wait_ge(*past("gates_open", 3))
            with pool.Fori(0, MT // 2) as i:
                for s in range(2):
                    if s == 0:
                        pool.wait_ge(*past("gates_mm", 2 * i))
                    pool.wait_ge(*past("bm", 3))
                    for w in range(2):
                        o = WFs[:, s, w].rearrange("p (n d c) -> p n d c", n=2, d=2)[:, :, :, 0:MH]
                        src = WFc[:, bass.ds(2 * i + s, 1), w].rearrange("p t (d n h) -> p (t n) d h", d=2, n=2)
                        last = GP.tensor_copy(o, src)
                    last.then_inc(sem("wf_ready"), 1)
            pool.wait_ge(*past("gates_mm", MT))
            GP.memset(cmask, 0.0).then_inc(sem("cm"), 1)
            pool.wait_ge(*past("cm", 1))
            GP.affine_select(out=cmask[:, 0], in_=cmask[:, 0], compare_op=ALU.is_ge, fill=-1e30, base=0, pattern=[[1, P]], channel_multiplier=-1).then_inc(sem("cm"), 1)
            GP.affine_select(out=cmask[:, 1], in_=cmask[:, 1], compare_op=ALU.is_ge, fill=-1e30, base=0, pattern=[[-1, P]], channel_multiplier=1).then_inc(sem("cm"), 1)
            with pool.Fori(0, MH) as i:
                pool.wait_ge(*past("q_mm", 8 * i))
                pool.wait_ge(*past("cm", 3))
                for k in range(4):
                    block_diagonal(BDq[:, k], 0, 4 * i + k).then_inc(sem("bdq_ready"), 1)
                for k in range(4):
                    pool.wait_ge(*past(f"v_mmx{k % 2}", 2 * i + k // 2))
                    pool.wait_ge(*past("cm", 3))
                    block_diagonal(BDkv[k % 2][:, 0], 1, 4 * i + k)
                    block_diagonal(BDkv[k % 2][:, 1], 2, 4 * i + k).then_inc(sem("bdkv_ready"), 1)
                pool.wait_ge(*past("xb_in", 32 * i + 32))
                for th in range(2):
                    diag = [(n, I, d) for n, (I, d, js) in enumerate(PIECES[th]) if I in js]
                    for x, (n, I, d) in enumerate(diag):
                        u = 8 * th + x
                        used = [NPI * th_ + n_ for th_ in range(2) for n_, (I_, d_, js_) in enumerate(PIECES[th_]) if I_ in js_]
                        pool.wait_ge(*past("d_ready", 2 * NPI * i + (used[u - 2] + 1 if u >= 2 else 0)))
                        GP.tensor_tensor(XM[:, u % 2], Xb[:, d, P * (I - CBLK):P * (I - CBLK) + P], cmask[:, d], ALU.add).then_inc(sem("xmask"), 1)


_OUT = "out_0_dram"


def kernel(**inputs):
    import numpy as np
    import concourse.bacc as bacc
    from concourse import mybir as _mybir
    from concourse.bass_utils import run_bass_kernel_spmd as run

    nc = bacc.Bacc("TRN2", target_bir_lowering=False, num_devices=1)
    arrays, A = {}, {}
    for name, a in inputs.items():
        a = np.ascontiguousarray(a)
        arrays[f"in_{name}"] = a
        A[name] = nc.dram_tensor(f"in_{name}", a.shape, _mybir.dt.from_np(a.dtype), kind="ExternalInput").ap()
    out = nc.dram_tensor(_OUT, inputs["x"].shape, F32, kind="ExternalOutput").ap()
    build(nc, A, out)
    return run(nc, [arrays], core_ids=[0]).results[0][_OUT]
```

```python
import math
from contextlib import ExitStack

import concourse.bass as bass
import concourse.mybir as mybir

F32 = mybir.dt.float32
F32R = mybir.dt.float32r
ALU = mybir.AluOpType
ACT = mybir.ActivationFunctionType
AX = mybir.AxisListType

P = 128
BANK = 512
D = 1024
DT = D // P
CTX, LAT = 256, 1024
TOK = CTX + LAT
SEGS = [(0, 512), (512, 512), (1024, 256)]
GRID_W = 64
ROWS = LAT // GRID_W
EPS = 1e-6

G, ST, HC = 64, 64, 16
T = 8
NJ = TOK // T
NJC = CTX // T
GB = 4
NB = G // GB
SL = T + 2
LAG = 2 * T - 1

PARTS = [(0, 0), (0, 1), (1, 0)]

RH, RD = 4, 256
MW = 2048
MT = MW // P
MH, MD = 4, 512
HT_ = MD // P
NBLK = TOK // P
CBLK = CTX // P
LBLK = LAT // P
PAD = 1 + CTX + 2 + 1 + LAT + 2
LOFF = CTX + 3
CV = LOFF + LAT

C_MODB, C_NG, C_FG, C_GLUB, C_RCW, C_RCB, C_C = 0, 48, 64, 72, 80, 112, 120
C_CC, C_BA, C_BX, C_LAM, C_MCB, C_MG, C_SK = 128, 136, 152, 168, 184, 200, 216
C_MCW = 256

LATE_SIGNALS = ("sums", "ht1_full", "ht1_high", "ht1_low", "w_high", "xm_split", "z_split", "xm_mm0", "xm_mm1",
    "xc_in", "xm_in0", "xm_in1", "xr_stored", "xb_in", "zt_in", "out_stored0", "out_stored1",
    "rows_t", "mix", "v_mmx0", "v_mmx1", "xb_used", "out_ready", "rows_ready", "em_ready", "yr_ready",
    "tr_ready", "xo", "h_ev", "bdkv_ready", "k_ev", "k_mm", "vt_ev", "bdq_ready", "ht_ev", "q_mm", "q_ev", "p_ready",
    "s_mm", "pv_mm", "hn_ready", "h_t", "wo_mm0", "wo_mm1", "sqf_ready", "ssf_mm", "yf_ready", "yf_t", "lf_abs",
    "lf_exp", "m_ready", "em_free", "xr_ready", "ybh_ready", "d_ready", "xmask", "rd_ready", "hf_ready", "mv_ready",
    "sd_ready", "sx_ready", "rf_ready")
DONE_SIGNALS = (("rg_gmm0", 4 * RH), ("e_mm0", NB // 2), ("e_mm1", NB // 2), ("g_ready0", NB // 2), ("g_ready1", NB // 2), ("wz_a", NB),
    ("wz_v", NB), ("rg_pmm0", 2 * RH), ("rg_pmm1", 2 * RH),
    ("u_w0", 64), ("u_w1", 64), ("glu_w0", 16 * DT), ("glu_w1", 16 * DT), ("eo_w0", 64), ("eo_w1", 64),
    ("rows_in", 16 * 15), ("x_in", 16 * 5), ("par_t", 3), ("cs_ready", 1),
    ("csig", 1), ("par_ready", 2), ("s5_nat", 1), ("s5_at", 1), ("s5_bct", 2), ("s5_bt", 16), ("s5_ct", 16),
    ("s5_dt", 1), ("s5_dar", 1), ("s5_mag", 1), ("s5_ang", 1), ("s5_sin", 1), ("lam_abs", 1), ("lam_exp", 1),
    ("lam_ready", 1), ("u_mm0", 4), ("u_mm1", 4), ("u_ev0", 4), ("u_ev1", 4), ("xt_t", 3 * DT), ("xt_ready", 3 * DT),
    ("ss_mm0", DT), ("ht_ready", 2 * DT), ("glu_mm0", DT), ("glu_mm1", DT), ("glu_sg", DT), ("glu_ev0", DT),
    ("glu_ev1", DT), ("eo_mm0", 4), ("eo_mm1", 4), ("mod0_mm0", 3), ("mod0_mm1", 3), ("mod1_mm0", DT + 2), ("mod1_mm1", DT + 2),
    ("mod1_mm2", DT + 2), ("f_mm0", NB // 2), ("f_mm1", NB // 2), ("x_t0", NB // 2), ("x_t1", NB // 2),
    ("x_ready0", NB // 2), ("x_ready1", NB // 2), ("v_mm0", NB // 2), ("v_mm1", NB // 2))


def build(nc, A, out):
    with ExitStack() as ctx:
        sems = {}

        TAKES_OVER = dict(zip(LATE_SIGNALS, DONE_SIGNALS))

        def sem(name):
            name = TAKES_OVER.get(name, (name, 0))[0]
            if name not in sems:
                sems[name] = ctx.enter_context(nc.semaphore(name))
            return sems[name]

        def past(name, n):
            return sem(name), n + TAKES_OVER.get(name, (name, 0))[1]

        def sb(name, n):
            return ctx.enter_context(nc.sbuf_tensor(name, [P, n], F32))

        def dram(name, shape):
            return nc.dram_tensor(name, shape, F32).ap()

        def mm(o, lhsT, rhs, k, n):
            return nc.tensor.matmul(o, lhsT, rhs, start=(k == 0), stop=(k == n - 1))

        AR0 = -(-nc.sbuf_base // 32) * 32
        AR = sb("arena", 47520)
        ps = ctx.enter_context(nc.psum_tensor("ps", [P, 8, BANK], F32))

        psf = ps[:, :, :].rearrange("p b c -> p (b c)")
        ps3 = [psf[:, 3 * s * BANK:3 * s * BANK + TOK] for s in range(2)]

        def at(o, n):
            return AR[:, o:o + n]

        HTo, XTo, WZo, YTo, RB = 0, 10240, 10240, 20480, 30848
        HT = at(HTo, DT * TOK).rearrange("p (k t) -> p k t", k=DT)
        XT = at(XTo, DT * TOK).rearrange("p (k t) -> p k t", k=DT)
        xin = at(HTo, NBLK * D).rearrange("p (b d) -> p b d", b=NBLK)
        WZ = at(WZo, (NJ + 1) * 2 * G).rearrange("p (j r g) -> p j r g", r=2, g=G)
        PV = sb("param_cols", 384)
        MOD = sb("modulation", 2 * 48)
        MODv = MOD[:, :].rearrange("p (l n w) -> p l n w", l=2, w=2)
        ACf = sb("norm_scale", 32)
        ACv = ACf[:, :].rearrange("p (l k w) -> p l k w", l=2, w=2)
        cs = sb("silu_c", 16)
        csv = cs[:, :].rearrange("p (k w) -> p k w", w=2)
        cst = sb("silu_tmp", 16)
        ident = sb("ident", 128)
        ones = sb("ones", 128)
        cols = sb("const_cols", 4)
        lamc = sb("rg_decay", 32)
        W = sb("weights", 2048)
        Wv = W[:, :].rearrange("p (s k n) -> p s k n", s=2, k=DT)
        GW0 = -(-nc.sbuf_base // 32) * 32
        GW = sb("weights2", 2048)

        def over(name, n, offset, dtype=F32R):
            return nc.alloc_sbuf_tensor_at(name, [P, n], dtype, offset=offset)
        sq = [at(RB + 8192, 2 * TOK).rearrange("p (s t) -> p s t", s=2), at(YTo, DT * TOK).rearrange("p (s t) -> p s t", s=DT)]
        SQN = [2, DT]
        rstd = [at(RB + 8192 + 2 * TOK, TOK), at(43968, TOK)]
        ntmp = [[at(RB + 8192 + (3 + q) * TOK, TOK) for q in range(2)],
                [over(f"norm_tmp{q}", TOK, AR0 + 4 * (YTo + 5152 + q * TOK), F32)[:, :] for q in range(2)]]
        modw1 = at(44400, 3 * 1024).rearrange("p (s k n) -> p s k n", s=3, k=DT)
        modw = at(RB, 2 * 3072).rearrange("p (s k n) -> p s k n", s=2, k=DT)
        rows = at(RB + 6144, 384).rearrange("p (v c) -> p v c", v=3)

        xt_d = dram("xt_spill", [P, DT * TOK])
        u_d = dram("u_chunks", [DT, P, TOK])
        y_d = dram("y_chunks", [DT, P, TOK])
        v_d = dram("s5_lags", [G, HC, LAG * HC])
        g_d = dram("s5_out_maps", [NB, P, GB * 2 * SL * HC])
        bo_d = dram("rg_out", [DT, P, TOK])
        xm_d = dram("ml_xm", [MT, P, TOK])
        xc_d = dram("ml_xcv", [MT, P, TOK])
        z_d = dram("ml_z", [MT, P, LAT])
        xr_d = dram("ml_rows", [2 * MH, LAT])

        xr_ = A["x"][0].rearrange("(b p) d -> p b d", p=P)
        cx_ = A["ctx"][0].rearrange("(b p) d -> p b d", p=P)
        rr = lambda ap, pat, **k: ap.rearrange(pat, **k)
        VP = [
            (0, 0, rr(A["mod_b"], "l (n c) -> (l n) c", c=P)),
            (0, 48, rr(A["norm_g"], "l (n c) -> (l n) c", c=P)),
            (0, 64, rr(A["final_g"], "(n c) -> n c", c=P)),
            (0, 72, rr(A["s5_glu_b"], "l (n c) -> (l n) c", c=P)),
            (0, 80, rr(A["rg_conv_w"][0], "j (n c) -> (j n) c", c=P)),
            (0, 112, rr(A["rg_conv_b"], "l (n c) -> (l n) c", c=P)),
            (0, 120, rr(A["c"], "l (n c) -> (l n) c", c=P)),
            (1, 0, rr(A["c_ctx"], "(n c) -> n c", c=P)),
            (1, 8, rr(A["rg_ba"][0], "l (n c) -> (l n) c", c=P)),
            (1, 24, rr(A["rg_bx"][0], "l (n c) -> (l n) c", c=P)),
            (1, 40, rr(A["rg_lam"][0], "l (n c) -> (l n) c", c=P)),
            (1, 56, rr(A["ml_conv_b"], "l (n c) -> (l n) c", c=P)),
            (1, 72, rr(A["ml_norm_g"], "l (n c) -> (l n) c", c=P)),
            (1, 88, rr(A["ml_skip"], "l (n c) -> (l n) c", c=P)),
            (2, 0, rr(A["ml_conv_w"][0], "j (n c) -> (j n) c", c=P)),
        ]
        NVP = len(VP)
        mod_v = [A["mod_w"][l].rearrange("(k p) n -> p k n", p=P) for l in range(2)]
        ew_in = A["e_w_in"][0].rearrange("(k p) (m n) -> m p k n", p=P, n=P)
        glu_v = A["s5_glu_w"][0].rearrange("(k p) (m n) -> m p k n", p=P, n=P)
        ew_out = A["e_w_out"][0].rearrange("(k p) (m n) -> m p k n", p=P, n=P)

        def rb(o, n):
            return at(RB + o, n)

        bn = rb(0, 2048).rearrange("p (r q h) -> p r q h", r=2, h=HC)
        cn = rb(2048, 2048).rearrange("p (h r q) -> p h r q", r=2, h=HC)
        X = rb(0, 2048).rearrange("p (s r g c) -> p s r g c", s=2, r=2, g=GB)
        Gb = [rb(2048, 1280), rb(14336, 1280)]
        Gv = [g.rearrange("p (g r k h) -> p g r k h", g=GB, r=2, h=HC) for g in Gb]
        BT = rb(4096, 2048).rearrange("p (r h g) -> p r h g", r=2, h=HC)
        t1 = rb(4096, 1280)
        CT = rb(6144, 2048).rearrange("p (r h g) -> p r h g", r=2, h=HC)
        BB = rb(8192, 2048).rearrange("p (r h g) -> p r h g", r=2, h=HC)
        Q = rb(10240, 1280).rearrange("p (k r g) -> p k r g", r=2, g=G)
        t2 = rb(10240, 1280)
        PWE = rb(11520, 1024).rearrange("p (k r g) -> p k r g", r=2, g=G)
        PWF = rb(12544, 1280).rearrange("p (k r g) -> p k r g", r=2, g=G)
        AL = rb(13824, 256).rearrange("p (v g) -> p v g", v=4)
        A12 = sb("s5_decay", 256)
        A1 = A12[:, 0:128].rearrange("p (r g) -> p r g", r=2)
        A2 = A12[:, 128:256].rearrange("p (r g) -> p r g", r=2)
        scanP = sb("s5_scan_tmp", 256)
        SP1 = scanP[:, 0:128].rearrange("p (r g) -> p r g", r=2)
        SP2 = scanP[:, 128:256].rearrange("p (r g) -> p r g", r=2)
        nat = rb(14336, 1280).rearrange("p (v q) -> p v q", q=64)
        Eg = rb(15616, 1024).rearrange("p (r g c) -> p r g c", r=2, g=GB)
        Ub = GW[:, 0:1280].rearrange("p (s g j) -> p s g j", s=2, g=GB)
        Vs = W[0:HC, 0:GB * LAG * HC].rearrange("p (g i h) -> p g i h", g=GB, h=HC)
        Dg = W[0:HC, 960:960 + G * HC].rearrange("p (g h) -> p g h", h=HC)
        dcol = W[0:HC, 1984:1984 + G]
        u_b = u_d.rearrange("k (g h) (s j) -> (k g) (h s) j", h=HC, s=T)
        y_b = y_d.rearrange("k (g h) (t j) -> (k g) t h j", h=HC, t=T)
        u_stage = rb(8192, 2 * TOK).rearrange("p (z s j) -> p z s j", z=2, s=T)

        Fg = rb(0, 2560).rearrange("p (s n) -> p s n", s=2)
        Fgv = [Fg[:, s].rearrange("p (g r k h) -> p g r k h", g=GB, r=2, h=HC) for s in range(2)]
        Mb = rb(2560, 1024).rearrange("p (s g c) -> p s g c", s=2, g=GB)
        Fu = rb(3584, 1280).rearrange("p (s g j) -> p s g j", s=2, g=GB)
        Zb = rb(4864, 2560).rearrange("p (s r g j) -> p s r g j", s=2, r=2, g=GB)
        Yb = rb(7424, 1280).rearrange("p (s g j) -> p s g j", s=2, g=GB)

        xrp = rb(0, 2 * PAD).rearrange("p (s t) -> p s t", s=2)
        xcb = rb(2572, 2 * TOK).rearrange("p (s t) -> p s t", s=2)
        RT = rb(5132, 2 * TOK).rearrange("p (s t) -> p s t", s=2)
        IT = rb(7692, 2 * TOK).rearrange("p (s t) -> p s t", s=2)
        AT = rb(10252, 2 * TOK).rearrange("p (s t) -> p s t", s=2)
        TT = rb(12812, CV)
        HH = rb(14095, 2 * TOK).rearrange("p (s t) -> p s t", s=2)
        SG = rb(0, 2 * TOK).rearrange("p (s t) -> p s t", s=2)
        lt = scanP[:, 0:96].rearrange("p (v c) -> p v c", v=6)
        BBs = GW[:, 1280:1536]
        BBv = BBs.rearrange("p (s r h g) -> p s r h g", s=2, r=2, h=HC)
        sa = rb(0, 384).rearrange("p (v r g) -> p v r g", v=3, r=2)
        tB = rb(512, 2048).rearrange("p (r h g) -> p r h g", r=2, h=HC)
        pg1 = rb(4096, 640)
        pg2 = rb(10240, 640)
        xt1 = rb(4096 + 640, 512)
        xt2 = rb(10240 + 640, 512)
        AO = rb(0, DT * TOK).rearrange("p (k t) -> p k t", k=DT)
        YT = at(YTo, DT * TOK).rearrange("p (k t) -> p k t", k=DT)
        SZ = rb(10240, TOK)
        SGs = rb(10240 + TOK, TOK)
        WO = [w[:, :].rearrange("p (k n) -> p k n", k=2 * DT) for w in (W, GW)]
        m_d = bass.AP(v_d.tensor, 0, [[HC * LAG * HC, G], [LAG * HC, HC], [HC, T], [1, P]])
        vtmp = GW[0:HC, 1536:1536 + GB * HC].rearrange("p (g h) -> p g h", g=GB)
        GWv = GW[:, :].rearrange("p (d m k n) -> p d m k n", d=2, m=2, k=2)

        K1 = 41088
        W4 = scanP[:, 0:192].rearrange("p (m t o) -> p m t o", m=3, o=4)
        WIF = [w.rearrange("p (t d n) -> p t d n", t=MT, d=2) for w in (at(43648, 256), at(43904, 256), A12[:, :])]
        WFc = at(K1 + 960, 512).rearrange("p (t w n) -> p t w n", t=MT, w=2)
        WFs = at(K1 + 1472, 512).rearrange("p (s w n) -> p s w n", s=2, w=2)
        bmask = at(K1 + 1984, P).rearrange("p (b o) -> p b o", o=4)
        BD = at(K1 + 2112, 384).rearrange("p (m c) -> p m c", m=3)
        BDT = at(44480, 384).rearrange("p (m c) -> p m c", m=3)
        BI = sb("gate_bias", 1)
        xmp = at(YTo, 2 * PAD).rearrange("p (s t) -> p s t", s=2)
        mcv = at(YTo + 2572, CV)
        mcs = at(YTo + 2572 + CV, CV)
        xco = at(YTo + 5140, 2 * TOK).rearrange("p (s t) -> p s t", s=2)
        zo = at(YTo + 7700, 2 * LAT).rearrange("p (s t) -> p s t", s=2)
        psG = psf[:, 5 * BANK:5 * BANK + TOK]
        HL = over("h_full", DT * TOK, AR0 + 4 * 30720, F32)[:, :].rearrange("p (k t) -> p k t", k=DT)
        HTs = [over(f"h_part{q}", DT * TOK, AR0 + 4 * o)[:, :].rearrange("p (k t) -> p k t", k=DT) for q, o in enumerate((HTo, 30720))]
        WXs = [over(f"in_weight_parts{z}", 2048, o)[:, :].rearrange("p (s k n) -> p s k n", s=2, k=DT) for z, o in enumerate((GW0, AR0 + 4 * 45248))]
        ow_in = A["o_w_in"][0].rearrange("(k p) (m n) -> m p k n", p=P, n=P)
        ow_out = A["o_w_out"][0].rearrange("(h k p) (m n) -> h m p k n", p=P, n=P, h=MH)
        row = [at(1280 * n, TOK)[0:64] for n in range(8)]
        rLI, rLF, rA, rB, rC, rM, rRes, rO = row
        NPC = 52 * P
        Pm = at(0, NPC)
        Xb = at(NPC, 2 * LAT).rearrange("p (d t) -> p d t", d=2)
        Dt = at(8704, 1024).rearrange("p (s t) -> p s t", s=2)
        XM = at(9728, 256).rearrange("p (s t) -> p s t", s=2)
        Xc = at(YTo, 4 * TOK).rearrange("p (k t) -> p k t", k=4)
        Kt = at(YTo + 5120, 4 * TOK).rearrange("p (k t) -> p k t", k=4)
        Vt = at(YTo + 10240, 4 * TOK).rearrange("p (b e) -> p b e", b=NBLK)
        Qt = at(YTo + 15360, 2048).rearrange("p (k t) -> p k t", k=4)
        MX = at(YTo + 17408, 2048).rearrange("p (k t) -> p k t", k=4)
        WOo = at(YTo + 19456, 1024).rearrange("p (s k n) -> p s k n", s=2, k=4)
        Xm = at(43968, 2 * TOK).rearrange("p (s t) -> p s t", s=2)
        Sp = at(43968, 2 * BANK).rearrange("p (d t) -> p d t", d=2)
        BDq = at(46528, 512).rearrange("p (k c) -> p k c", k=4)
        BDkv = [at(47040, 256).rearrange("p (m c) -> p m c", m=2), A12[:, :].rearrange("p (m c) -> p m c", m=2)]
        Zt = W[:, :].rearrange("p (k t) -> p k t", k=4)
        Hb = GW[:, :].rearrange("p (j e) -> p j e", j=4)
        YB = at(K1 + 192, 800).rearrange("p (d j i h) -> p d j i h", d=2, j=NBLK, i=NBLK)
        TB = at(K1 + 992, 80).rearrange("p (d h j) -> p d h j", d=2, h=4)
        TR = at(K1 + 1072, 80)[0:64].rearrange("p (d h j) -> p d h j", d=2, h=4)
        EMT = at(K1 + 1152, 64).rearrange("p (j d h) -> p j d h", j=LBLK, d=2)
        cmask = at(K1 + 1216, 256).rearrange("p (d c) -> p d c", d=2)
        YBh = at(K1 + 1472, 200).rearrange("p (d j i) -> p d j i", d=2, j=NBLK)
        EMh = at(K1 + 1672, 16).rearrange("p (j d) -> p j d", d=2)
        rden = at(K1 + 1688, 16).rearrange("p (j d) -> p j d", d=2)
        bst = at(K1 + 1704, 48).rearrange("p (s n) -> p s n", s=8)
        mv = at(K1 + 1752, 16).rearrange("p (s n) -> p s n", n=2)
        gs1 = MODv[:, 1, 16:24]
        HALF = LAT // 2
        HB_ = HALF // P

        def blocks_of(d, I, th):
            js = range(CBLK + HB_ * th, CBLK + HB_ * (th + 1))
            return [J for J in js if I < CBLK or (J >= I if d == 0 else J <= I)]

        PIECES = [[(I, d, blocks_of(d, I, th)) for I in range(NBLK) for d in range(2) if blocks_of(d, I, th)] for th in range(2)]
        NPI = len(PIECES[0])
        NSUM = NPI - 2
        assert len(PIECES[1]) == NPI
        POFF = [{}, {}]
        for th in range(2):
            o = 0
            for I, d, js in PIECES[th]:
                POFF[th][I, d] = o
                o += P * len(js)
            assert o <= NPC

        def p_of(th, I, d, J):
            js = blocks_of(d, I, th)
            o = POFF[th][I, d] + P * (J - js[0])
            return Pm[:, o:o + P]

        def pieces_before(th, I):
            return sum(1 for x in PIECES[th] if x[0] < I)

        def step_of(d, I):
            return I if d == 0 else (CBLK - 1 - I if I < CBLK else NBLK + CBLK - 1 - I)

        xr_rows = bass.AP(xr_d.tensor, 0, [[0, P], [LAT, 2 * MH], [1, LAT]])

        def bcast_row(n):
            return xr_rows[:, bass.ds(n, 1)].rearrange("p o t -> p (o t)")

        SQf = at(0, DT * LAT).rearrange("p (k t) -> p k t", k=DT)
        YF = at(YTo, DT * LAT).rearrange("p (k t) -> p k t", k=DT)
        rfin = at(8192, LAT)
        YO = at(30720, 2 * D).rearrange("p (s c) -> p s c", s=2)

        def natural(ap, rw):
            return [ap[rw, 0:CTX][:, ::-1], ap[rw, CTX:TOK][:, ::-1]]

        block = ctx.enter_context(nc.Block())
        MAGIC = 12582912.0
        TWO_PI = (6.28125, 0.0019350051879882812, 3.019916050561733e-07)

        def wz_moves(r, b):
            src = ps[:, 2 + 2 * r:4 + 2 * r, 0:2 * NJ].rearrange("p a (g j) -> p a g j", g=2)

            def put(rw, steps):
                w = WZ[rw, steps, r, bass.ds(GB * b, GB)]
                return w.rearrange("p j (a g) -> p a g j", a=2)

            f, bk = slice(0, 64), slice(64, 128)
            return [
                (put(f, slice(1, NJ + 1)), src[f]),
                (put(bk, slice(1, NJC + 1)), src[bk, :, :, 0:NJC][:, :, :, ::-1]),
                (put(bk, slice(NJC + 1, NJ + 1)), src[bk, :, :, NJC:NJ][:, :, :, ::-1]),
            ]

        def log1p(link, y, z, z2, o, n=9):
            V = nc.vector
            link(V.tensor_scalar(z, y, 2.0, None, ALU.add))
            link(V.reciprocal(z, z))
            link(V.tensor_tensor(z, z, y, ALU.mult))
            link(V.tensor_tensor(z2, z, z, ALU.mult))
            link(V.tensor_scalar(o, z2, 1.0 / (2 * n - 1), None, ALU.mult))
            for c in range(n - 2, 0, -1):
                link(V.scalar_tensor_tensor(out=o, in0=o, scalar=1.0 / (2 * c + 1), in1=z2, op0=ALU.add, op1=ALU.mult))
            link(V.scalar_tensor_tensor(out=o, in0=o, scalar=1.0, in1=z, op0=ALU.add, op1=ALU.mult))
            link(V.tensor_scalar(o, o, 2.0, None, ALU.mult))

        @block.sync
        def _(sp):
            for v, r, src in VP:
                sp.dma_start(rows[r:r + src.shape[0], v, :], src).then_inc(sem("rows_in"), 16)
            sp.dma_start(xin[:, 0:CBLK, :], cx_).then_inc(sem("x_in"), 16)
            for b in range(0, LBLK, 2):
                sp.dma_start(xin[:, CBLK + b:CBLK + b + 2, :], xr_[:, b:b + 2, :]).then_inc(sem("x_in"), 16)
            with sp.Fori(0, 3) as i:
                for s in range(2):
                    sp.wait_ge(*past(f"mod0_mm{s}", i))
                    sp.dma_start(modw[:, s], mod_v[0][:, :, bass.ds((2 * i + s) * 384, 384)]).then_inc(sem(f"mod0_in{s}"), 16)
            sp.wait_ge(*past("xt_ready", 24))
            sp.dma_start(xt_d, at(XTo, DT * TOK)).then_inc(sem("xt_spilled"), 16)
            with sp.Fori(0, 4) as i:
                for s in range(2):
                    sp.wait_ge(*past(f"u_mm{s}", i))
                    sp.dma_start(Wv[:, s], ew_in[bass.ds(2 * i + s, 1)].rearrange("m p k n -> p (m k) n")).then_inc(sem(f"u_w{s}"), 16)
            for s in range(2):
                sp.wait_ge(*past(f"u_mm{s}", 4))
            with nc.allow_non_contiguous_dma(reason="a thousand skip coefficients"):
                sp.dma_start(dcol, A["s5_d"][0].rearrange("(g h) -> h g", h=HC)).then_inc(sem("s5_in"), 16)
            for s in range(2):
                sp.wait_ge(*past(f"u_stored{s}", 64))
            with sp.Fori(0, NB // 2) as i:
                for s in range(2):
                    sp.wait_ge(*past(f"e_mm{s}", i))
                    sp.dma_start(Ub[:, s], u_b[bass.ds(GB * (2 * i + s), GB)].rearrange("g q j -> q g j")).then_inc(sem(f"ub_in{s}"), 16)
            sp.wait_ge(*past("v_stored", 16 * NB))
            sp.wait_ge(*past("e_mm0", NB // 2))
            sp.wait_ge(*past("e_mm1", NB // 2))
            with sp.Fori(0, RH) as i:
                for s in range(2):
                    sp.wait_ge(*past(f"rg_pmm{s}", 2 * i))
                    sp.dma_start(Wv[:, s], ew_in[bass.ds(2 * i + 16 + s, 1)].rearrange("m p k n -> p (m k) n")).then_inc(sem(f"rg_w{s}"), 16)
                for s in range(2):
                    sp.wait_ge(*past(f"rg_gmm{s}", 4 * i))
                for d in range(2):
                    for m, name in enumerate(("rg_wa", "rg_wx")):
                        sp.dma_start(GWv[:, d, m], A[name][0, d, bass.ds(i, 1)].rearrange("o (k p) n -> p (o k) n", p=P)).then_inc(sem("rg_gw"), 16)
                for s in range(2):
                    sp.wait_ge(*past(f"rg_pmm{s}", 2 * i + 1))
                    sp.dma_start(Wv[:, s], ew_in[bass.ds(2 * i + 24 + s, 1)].rearrange("m p k n -> p (m k) n")).then_inc(sem(f"rg_w{s}"), 16)
            sp.wait_ge(*past("bo_stored", 16 * RH))
            sp.wait_ge(*past("g_stored0", 16 * NB // 2))
            sp.wait_ge(*past("g_stored1", 16 * NB // 2))
            with sp.Fori(0, NB // 2) as i:
                for s in range(2):
                    sp.wait_ge(*past(f"f_mm{s}", i))
                    sp.dma_start(Fg[:, s], g_d[bass.ds(2 * i + s, 1)].rearrange("b p n -> p (b n)")).then_inc(sem(f"f_in{s}"), 16)
                    sp.dma_start(Fu[:, s], u_b[bass.ds(GB * (2 * i + s), GB)].rearrange("g q j -> q g j")).then_inc(sem(f"f_in{s}"), 16)
                    for g in range(GB):
                        sp.dma_start(Mb[:, s, g], m_d[bass.ds(GB * (2 * i + s) + g, 1)]).then_inc(sem(f"f_in{s}"), 16)
            sp.wait_ge(*past("y_stored0", 16 * GB * (NB // 2)))
            sp.wait_ge(*past("y_stored1", 16 * GB * (NB // 2)))

            def glu_weights(i):
                for s, src in ((1, ew_in[bass.ds(i + 8, 1)]), (0, glu_v[bass.ds(i, 1)])):
                    sp.wait_ge(*past(f"glu_mm{s}", i))
                    sp.dma_start(Wv[:, s], src.rearrange("m p k n -> p (m k) n")).then_inc(sem(f"glu_w{s}"), 16)

            glu_weights(0)
            sp.dma_start(YT, y_d.rearrange("k p t -> p k t")).then_inc(sem("y_in"), 16)
            glu_weights(1)
            sp.dma_start(XT, xt_d.rearrange("p (k t) -> p k t", k=DT)).then_inc(sem("mix_in"), 16)
            with sp.Fori(2, DT) as i:
                glu_weights(i)
            sp.wait_ge(*past("glu_mm0", DT))
            sp.wait_ge(*past("glu_mm1", DT))

            def mix_weights(i):
                for s in range(2):
                    sp.wait_ge(*past(f"eo_mm{s}", i))
                    sp.dma_start(WO[s], ew_out[bass.ds(2 * i + s, 1)].rearrange("m p k n -> p (m k) n")).then_inc(sem(f"eo_w{s}"), 16)

            mix_weights(0)
            sp.dma_start(HT, bo_d.rearrange("k p t -> p k t")).then_inc(sem("mix_in"), 16)
            with sp.Fori(1, 4) as i:
                mix_weights(i)
            sp.wait_ge(*past("eo_mm0", 4))
            sp.wait_ge(*past("eo_mm1", 4))
            with sp.Fori(0, MT) as i:
                for z, kind in enumerate(("xm", "z")):
                    sp.wait_ge(*past(f"{kind}_split", i))
                    sp.dma_start(Wv[:, z], ow_in[bass.ds(i + MT * z, 1)].rearrange("m p k n -> p (m k) n")).then_inc(sem(f"{kind}_w"), 16)
            for s in range(2):
                sp.wait_ge(*past(f"xm_mm{s}", MT // 2))
                sp.wait_ge(*past(f"z_mm{s}", MT // 2))
                for nm, n in (("xm", 32), ("xcv", 16), ("z", 16)):
                    sp.wait_ge(*past(f"{nm}_stored{s}", n * MT // 2))
            sp.wait_ge(*past("gates_mm", MT))

            def key_value_rows(i):
                sp.wait_ge(*past("sx_ready", 8 * i))
                sp.dma_start(Xc, xc_d[bass.ds(4 * i, 4)].rearrange("k p t -> p k t")).then_inc(sem("xc_in"), 16)
                sp.wait_ge(*past("pv_mm", 8 * i))
                for k in range(4):
                    s = k % 2
                    sp.wait_ge(*past(f"v_mmx{s}", 2 * i + k // 2))
                    sp.dma_start(Xm[:, s], xm_d[bass.ds(4 * i + k, 1)].rearrange("k p t -> p (k t)")).then_inc(sem(f"xm_in{s}"), 16)

            def decay_rows(i):
                sp.wait_ge(*past("xb_used", i))
                for d in range(2):
                    sp.dma_start(Xb[:, d], bcast_row(i + MH * d)).then_inc(sem("xb_in"), 16)

            def output_weights(i, th, n):
                sp.wait_ge(*past(f"wo_mm{n % 2}", 8 * i + 4 * th + n // 2))
                sp.dma_start(WOo[:, n % 2], ow_out[bass.ds(i, 1), n].rearrange("o p k n -> p (o k) n")).then_inc(sem(f"wo_in{n % 2}"), 16)

            def head(i, last):
                for th in range(2):
                    sp.wait_ge(*past("mix", 2 * i + th))
                    sp.dma_start(Zt, z_d[bass.ds(4 * i, 4), :, HALF * th:HALF * th + HALF].rearrange("k p t -> p k t")).then_inc(sem("zt_in"), 16)
                    for n in range(DT):
                        if th == 1 and n == 2 and not last:
                            key_value_rows(i + 1)
                            decay_rows(i + 1)
                        output_weights(i, th, n)

            key_value_rows(0)
            sp.wait_ge(*past("rows_t", 1))
            sp.wait_ge(*past("xr_stored", 32))
            decay_rows(0)
            with sp.Fori(0, MH - 1) as i:
                head(i, False)
            head(MH - 1, True)
            for b in range(LBLK):
                sp.wait_ge(*past("out_ready", b + 1))
                sp.dma_start(out[0, P * b:P * b + P, :], YO[:, b % 2]).then_inc(sem(f"out_stored{b % 2}"), 16)
            for s in range(2):
                sp.wait_ge(*past(f"out_stored{s}", 16 * LBLK // 2))

        @block.tensor
        def _(pe):
            pe.wait_ge(*past("rows_in", 16 * NVP))
            pe.wait_ge(*past("consts", 4))
            for v, n in enumerate((128, 104, 64)):
                nc.tensor.transpose(ps[:, 7, P * v:P * v + n], rows[0:n, v, :], ident[0:n, 0:n]).then_inc(sem("par_t"), 1)

            def square_sums(l, k):
                pe.wait_ge(*past(f"sq_ready{l}", k + 1))
                for j, (t0, n) in enumerate(SEGS):
                    last = mm(ps[:, 4 + j, 0:n], ones[:, :], sq[l][:, k % SQN[l], t0:t0 + n], k, DT)
                last.then_inc(sem(f"ss_mm{l}"), 1)

            pe.wait_ge(*past("x_in", 16 * 5))
            for k in range(DT):
                for j, (t0, n) in enumerate(SEGS):
                    q = 3 * k + j
                    if q >= 4:
                        pe.wait_ge(*past("xt_ready", q - 3))
                    for b in range(n // P):
                        last = nc.tensor.transpose(ps[:, q % 4, P * b:P * b + P], xin[:, t0 // P + b, P * k:P * k + P], ident[:, :])
                    last.then_inc(sem("xt_t"), 1)
                if k:
                    square_sums(0, k - 1)
            square_sums(0, DT - 1)

            def modulate(l):
                pe.wait_ge(*past("cs_ready", 1))
                with pe.Fori(0, 3) as i:
                    for s in range(2):
                        pe.wait_ge(*past(f"mod{l}_in{s}", 16 * i + 16))
                        for n in range(3):
                            for k in range(DT):
                                last = mm(ps[:, 7, bass.ds(12 * i + 6 * s + 2 * n, 2)], modw[:, s, k, P * n:P * n + P], csv[:, k, :], k, DT)
                        last.then_inc(sem(f"mod{l}_mm{s}"), 1)

            modulate(0)
            with pe.Fori(0, 4) as i:
                for s in range(2):
                    pe.wait_ge(*past(f"u_w{s}", 16 * i + 16))
                    pe.wait_ge(*past(f"u_ev{s}", i))
                    for t0, n in SEGS:
                        for k in range(DT):
                            if t0 == 0 and s == 0:
                                pe.wait_ge(*past("ht_ready", 2 * k + 2))
                            last = mm(ps3[s][:, t0:t0 + n], Wv[:, s, k], HT[:, k, t0:t0 + n], k, DT)
                    last.then_inc(sem(f"u_mm{s}"), 1)
            pe.wait_ge(*past("s5_nat", 1))
            pe.wait_ge(*past("u_ev0", 4))
            pe.wait_ge(*past("u_ev1", 4))
            nc.tensor.transpose(ps[:, 6, 0:P], nat[:, 11:13].rearrange("p v q -> p (v q)"), ident[:, :])
            nc.tensor.transpose(ps[:, 6, P:2 * P], nat[:, 17:19].rearrange("p v q -> p (v q)"), ident[:, :]).then_inc(sem("s5_at"), 1)
            for w in range(2):
                if w == 1:
                    pe.wait_ge(*past("s5_bt", 16))
                for h in range(HC):
                    src = (bn.rearrange("p r q h -> p h (r q)") if w == 0 else cn.rearrange("p h r q -> p h (r q)"))[:, h]
                    last = nc.tensor.transpose(ps[:, h // 4, P * (h % 4):P * (h % 4) + P], src, ident[:, :])
                last.then_inc(sem("s5_bct"), 1)
            pe.wait_ge(*past("s5_ct", 16))
            with pe.Fori(0, NB // 2) as i:
                for s in range(2):
                    b = 2 * i + s
                    pe.wait_ge(*past(f"x_ready{s}", i + 1))
                    pe.wait_ge(*past("eg_ready", 2 * b))
                    for r in range(2):
                        for g in range(GB):
                            if r == 1 and g == GB - 1:
                                pe.wait_ge(*past(f"g_ready{s}", i + 1))
                                pe.wait_ge(*past("v_ev", b))
                            last = nc.tensor.transpose(ps[:, r, P * g:P * g + P], X[:, s, r, g], ident[:, :])
                    last.then_inc(sem(f"x_t{s}"), 1)
                    for g in range(GB):
                        for d in range(2):
                            rw = slice(64 * d, 64 * d + 64)
                            for r in range(2):
                                last = mm(ps[0:HC, 6 + d, P * g:P * g + P], BBv[rw, s, r, :, g],
                                          Gv[s][rw, g, r, 2 * d:2 * d + T, :], r, 2)
                    last.then_inc(sem(f"v_mm{s}"), 1)
                    pe.wait_ge(*past("eg_ready", 2 * b + 2))
                    pe.wait_ge(*past(f"ub_in{s}", 16 * i + 16))
                    pe.wait_ge(*past("wz_a", b))
                    pe.wait_ge(*past("wz_v", b))
                    for r in range(2):
                        for g in range(GB):
                            last = mm(ps[:, 2 + 2 * r + g // 2, NJ * (g % 2):NJ * (g % 2) + NJ], Eg[:, r, g], Ub[:, s, g], 0, 1)
                    last.then_inc(sem(f"e_mm{s}"), 1)
            pe.wait_ge(*past("wz_a", NB))
            pe.wait_ge(*past("wz_v", NB))
            pe.wait_ge(*past("v_ev", NB))
            with pe.Fori(0, RH) as i:
                for kind in range(2):
                    for s in range(2):
                        pe.wait_ge(*past(f"rg_w{s}", 32 * i + 16 * kind + 16))
                        pe.wait_ge(*past(f"rg_ev{s}", 6 * i + kind))
                        for t0, n in SEGS:
                            for k in range(DT):
                                last = mm(ps3[s][:, t0:t0 + n], Wv[:, s, k], HT[:, k, t0:t0 + n], k, DT)
                        last.then_inc(sem(f"rg_pmm{s}"), 1)
                pe.wait_ge(*past("rg_gw", 64 * i + 64))
                pe.wait_ge(*past("xc_ready", 2 * i + 2))
                for d in range(2):
                    for m in range(2):
                        for s in range(2):
                            pe.wait_ge(*past(f"rg_ev{s}", 6 * i + 2 + 2 * d + m))
                            for t0, n in SEGS:
                                for k in range(2):
                                    last = mm(ps3[s][:, t0:t0 + n], GWv[:, d, m, k, P * s:P * s + P], xcb[:, k, t0:t0 + n], k, 2)
                            last.then_inc(sem(f"rg_gmm{s}"), 1)
            pe.wait_ge(*past("rg_ev0", 6 * RH))
            pe.wait_ge(*past("rg_ev1", 6 * RH))
            with pe.Fori(0, NB // 2) as i:
                for s in range(2):
                    pe.wait_ge(*past(f"f_in{s}", 96 * i + 96))
                    pe.wait_ge(*past(f"z_ready{s}", i + 1))
                    pe.wait_ge(*past(f"y_ev{s}", i))
                    for g in range(GB):
                        o = ps[:, 2 * s + g // 2, NJ * (g % 2):NJ * (g % 2) + NJ]
                        mm(o, Mb[:, s, g], Fu[:, s, g], 0, 3)
                        for r in range(2):
                            last = mm(o, Fgv[s][:, g, r, 1:1 + T, :].rearrange("p k h -> p (k h)"), Zb[:, s, r, g], 1 + r, 3)
                    last.then_inc(sem(f"f_mm{s}"), 1)
            for q in range(6):
                pe.wait_ge(*past(f"mod1_in{q % 3}", 16 * (q // 3) + 16))
                for k in range(DT):
                    last = mm(ps[:, 7, 64 + 2 * q:66 + 2 * q], modw1[:, q % 3, k], csv[:, k, :], k, DT)
                last.then_inc(sem(f"mod1_mm{q % 3}"), 1)
            pe.wait_ge(*past("y_ev0", NB // 2))
            pe.wait_ge(*past("y_ev1", NB // 2))
            with pe.Fori(0, DT) as i:
                for s, src in ((1, HT), (0, YT)):
                    if s == 0:
                        pe.wait_ge(*past("y_in", 16))
                    pe.wait_ge(*past(f"glu_w{s}", 16 * i + 16))
                    pe.wait_ge(*past(f"glu_ev{s}", i))
                    for t0, n in SEGS:
                        for k in range(DT):
                            last = mm(ps3[s][:, t0:t0 + n], Wv[:, s, k], src[:, k, t0:t0 + n], k, DT)
                    last.then_inc(sem(f"glu_mm{s}"), 1)
                for q in range(3):
                    pe.wait_ge(*past(f"mod1_in{q}", 16 * i + 48))
                    for k in range(DT):
                        last = mm(ps[:, 7, bass.ds(6 * i + 2 * q, 2)], modw1[:, q, k], csv[:, k, :], k, DT)
                    last.then_inc(sem(f"mod1_mm{q}"), 1)
            pe.wait_ge(*past("glu_ao", DT))
            with pe.Fori(0, 4) as i:
                for s in range(2):
                    pe.wait_ge(*past(f"eo_w{s}", 16 * i + 16))
                    pe.wait_ge(*past(f"eo_ev{s}", 2 * i))
                    for half, (j, (t0, n)) in [(h, x) for h in range(2) for x in enumerate(SEGS)]:
                        t = 4 * i + (2 * s + j - 1)
                        folds = half == 0 and j > 0
                        if folds:
                            if s == 0 and j == 1:
                                pe.wait_ge(*past("ml_in", 16 * 13))
                            pe.wait_ge(*past("bd_ready", t + 1))
                            pe.wait_ge(*past("fold_ev", t))
                            for m in range(3):
                                last = nc.tensor.transpose(ps[:, 6, P * m:P * m + P], BD[:, m], ident[:, :])
                            last.then_inc(sem("bd_t"), 1)
                        if half == 1 and s == 0 and j == 0:
                            pe.wait_ge(*past("mix_in", 32))
                        for k in range(DT):
                            last = mm(ps3[s][:, t0:t0 + n], WO[s][:, DT * half + k], (AO, HT)[half][:, k, t0:t0 + n], DT * half + k, 2 * DT)
                        if folds:
                            pe.wait_ge(*past("bdt_ready", t + 1))
                            for m in range(3):
                                c = 3 * P + 16 * (m // 2)
                                fold = mm(ps[:, 6, c:c + 16], BDT[:, m], WIF[m][:, bass.ds(t, 1)].rearrange("p o d n -> p (o d n)"), m % 2, 2 - m // 2)
                            fold.then_inc(sem("fold_mm"), 1)
                    last.then_inc(sem(f"eo_mm{s}"), 1)
            for s in range(2):
                pe.wait_ge(*past(f"eo_ev{s}", 8))
            for k in range(DT):
                square_sums(1, k)
            pe.wait_ge(*past("fold_ev", MT))
            pe.wait_ge(*past("ht1_full", 1))
            pe.wait_ge(*past("wf_zero", 1))
            for t0, n in SEGS:
                nc.tensor.matmul(psG[:, t0:t0 + n], WFs[:, 0, 0], XT[:, 0, t0:t0 + n], start=True, stop=False, skip_group_check=True).then_inc(sem("gates_open"), 1)
            with pe.Fori(0, MT // 2) as i:
                for s in range(2):
                    m = 2 * i + s
                    pe.wait_ge(*past("xm_split", m + 1))
                    pe.wait_ge(*past("xm_ev", m))
                    for t0, n in SEGS:
                        for k in range(DT):
                            if t0 == 0:
                                pe.wait_ge(*past("ht1_low", k + 1))
                            for q, (a, b) in enumerate(PARTS):
                                last = mm(ps3[0][:, t0:t0 + n], WXs[0][:, a, k], HTs[b][:, k, t0:t0 + n], 3 * k + q, 3 * DT)
                    last.then_inc(sem(f"xm_mm{s}"), 1)
                    pe.wait_ge(*past("z_split", m + 1))
                    pe.wait_ge(*past("z_ev", m))
                    for t0 in (0, BANK):
                        for k in range(DT):
                            for q, (a, b) in enumerate(PARTS):
                                last = mm(psf[:, 3 * BANK + t0:4 * BANK + t0], WXs[1][:, a, k], HTs[b][:, k, CTX + t0:CTX + t0 + BANK], 3 * k + q, 3 * DT)
                    last.then_inc(sem(f"z_mm{s}"), 1)
                    pe.wait_ge(*past("wf_ready", m + 1))
                    pe.wait_ge(*past("xcv_ready", m + 1))
                    for t0, n in SEGS:
                        nc.tensor.matmul(psG[:, t0:t0 + n], WFs[:, s, 0], xco[:, s, t0:t0 + n], start=False, stop=False, skip_group_check=True)
                        if t0 == 0:
                            x = [(xmp[:, s, 1:1 + CTX], 0), (xmp[:, s, LOFF + 1:LOFF + 1 + CTX], CTX)]
                        else:
                            x = [(xmp[:, s, LOFF + 1 + t0 - CTX:LOFF + 1 + t0 - CTX + n], 0)]
                        for r, o in x:
                            last = nc.tensor.matmul(psG[:, t0 + o:t0 + o + r.shape[1]], WFs[:, s, 1], r, start=False, stop=False, skip_group_check=True)
                    last.then_inc(sem("gates_mm"), 1)
            def keys_values(i):
                pe.wait_ge(*past("xc_in", 16 * i + 16))
                for k in range(4):
                    pe.wait_ge(*past("bdkv_ready", 4 * i + k + 1))
                    pe.wait_ge(*past("k_ev", 4 * i + k))
                    for t0, n in SEGS:
                        last = mm(ps3[0][:, t0:t0 + n], BDkv[k % 2][:, 0], Xc[:, k, t0:t0 + n], 0, 1)
                    last.then_inc(sem("k_mm"), 1)
                    pe.wait_ge(*past(f"xm_in{k % 2}", 32 * i + 16 * (k // 2) + 16))
                    pe.wait_ge(*past("vt_ev", 4 * i + k))
                    for b in range(NBLK):
                        last = mm(ps3[1][:, P * b:P * b + P], Xm[:, k % 2, P * b:P * b + P], BDkv[k % 2][:, 1], 0, 1)
                    last.then_inc(sem(f"v_mmx{k % 2}"), 1)

            def head(i, last_head):
                def queries(th):
                    for k in range(4):
                        if k == 0:
                            pe.wait_ge(*past("ht_ev", 8 * i))
                            pe.wait_ge(*past("h_ev", 8 * i))
                        else:
                            pe.wait_ge(*past("q_ev", 8 * i + 4 * th + k - 1))
                        mm(ps[:, 6 + k % 2], BDq[:, k], Xc[:, k, CTX + HALF * th:CTX + HALF * th + HALF], 0, 1).then_inc(sem("q_mm"), 1)

                def scores(th):
                    if th == 0:
                        pe.wait_ge(*past("xo", 16 * i))
                    pe.wait_ge(*past("q_ev", 8 * i + 4 * th + 4))
                    pe.wait_ge(*past("k_ev", 4 * i + 4))
                    for I in range(NBLK):
                        done = pieces_before(th, max(I - 1, 0))
                        pe.wait_ge(*past("p_ready", 2 * NPI * i + (NPI * th + done)))
                        for k in range(4):
                            last = mm(ps[:, I % 2], Kt[:, k, P * I:P * I + P], Qt[:, k, :], k, 4)
                        last.then_inc(sem("s_mm"), 1)

                def values(th):
                    pe.wait_ge(*past("p_ready", 2 * NPI * i + NPI * (th + 1)))
                    pe.wait_ge(*past("vt_ev", 4 * i + 4))
                    for j in range(HB_):
                        J = CBLK + HB_ * th + j
                        b0 = 2 + 2 * (j % 2)
                        pe.wait_ge(*past("h_ev", 8 * i + 4 * th + max(j - 1, 0)))
                        if j == 0:
                            pe.wait_ge(*past("q_ev", 8 * i + 8))
                        for d in range(2):
                            Is = [I for I in range(NBLK) if J in blocks_of(d, I, th)]
                            for n, I in enumerate(Is):
                                p = p_of(th, I, d, J)
                                mm(ps[:, b0 + d], p, Vt[:, I], n, len(Is))
                        if j == 0:
                            pe.wait_ge(*past("sums", 2 * NSUM * i + NSUM * (th + 1)))
                        for d in range(2):
                            last = mm(ps[:, 6 + j % 2, d:d + 1], Sp[:, d, P * j:P * j + P], ones[:, 0:1], 0, 1)
                        last.then_inc(sem("pv_mm"), 1)

                def outputs(th):
                    for j in range(HB_):
                        pe.wait_ge(*past("hn_ready", 8 * i + 4 * th + j + 1))
                        pe.wait_ge(*past("ht_ev", 8 * i + 4 * th + max(j - 1, 0)))
                        for k in range(4):
                            last = nc.tensor.transpose(ps[:, 6 + j % 2, P * k:P * k + P], Hb[:, j, P * k:P * k + P], ident[:, :])
                        last.then_inc(sem("h_t"), 1)
                    pe.wait_ge(*past("mix", 2 * i + th + 1))
                    if th == 1 and not last_head:
                        pe.wait_ge(*past("k_ev", 4 * i + 8))
                    for n in range(DT):
                        pe.wait_ge(*past(f"wo_in{n % 2}", 16 * (8 * i + 4 * th + n // 2 + 1)))
                        pe.wait_ge(*past("xo", 16 * i + 8 * th + max(n - 1, 0)))
                        for k in range(4):
                            last = mm(ps[:, n % 2], WOo[:, n % 2, k], MX[:, k, :], k, 4)
                        last.then_inc(sem(f"wo_mm{n % 2}"), 1)

                pe.wait_ge(*past("bdq_ready", 4 * i + 4))
                queries(0)
                scores(0)
                queries(1)
                values(0)
                scores(1)
                outputs(0)
                values(1)
                if not last_head:
                    pe.wait_ge(*past("xo", 16 * i + 8))
                    pe.wait_ge(*past("h_ev", 8 * i + 8))
                    keys_values(i + 1)
                outputs(1)

            pe.wait_ge(*past("rows_ready", 2))
            pe.wait_ge(*past("z_ev", MT))
            pe.wait_ge(*past("xm_ev", MT))
            keys_values(0)
            pe.wait_ge(*past("k_ev", 4))
            pe.wait_ge(*past("vt_ev", 4))
            pe.wait_ge(*past("em_ready", 1))
            for j in range(LBLK):
                nc.tensor.transpose(ps[:, 5, 64 * j:64 * j + 64], rA[0:64, P * j:P * j + P], ident[0:64, 0:64])
            pe.wait_ge(*past("yr_ready", 1))
            for b in range(NBLK):
                nc.tensor.transpose(psf[:, 2 * BANK + 64 * b:2 * BANK + 64 * b + 64], rB[0:64, P * b:P * b + P], ident[0:64, 0:64])
            pe.wait_ge(*past("tr_ready", 1))
            mm(ps[:, 4, 0:80], ones[0:64, :], TR.rearrange("p d h j -> p (d h j)"), 0, 1).then_inc(sem("rows_t"), 1)
            with pe.Fori(0, MH - 1) as i:
                head(i, False)
            head(MH - 1, True)
            for k in range(DT):
                pe.wait_ge(*past("sqf_ready", k + 1))
                for t in range(2):
                    last = mm(ps[:, 2 + t], ones[:, :], SQf[:, k, BANK * t:BANK * t + BANK], k, DT)
            last.then_inc(sem("ssf_mm"), 1)
            for b in range(LBLK):
                pe.wait_ge(*past("yf_ready", DT * (1 + b // 4)))
                if b >= 2:
                    pe.wait_ge(*past("out_ready", b - 1))
                for k in range(DT):
                    o = 4 + 2 * (b % 2) + k // 4
                    last = nc.tensor.transpose(ps[:, o, P * (k % 4):P * (k % 4) + P], YF[:, k, P * b:P * b + P], ident[:, :])
                last.then_inc(sem("yf_t"), 1)

        @block.scalar
        def _(act):
            act.wait_ge(*past("par_ready", 2))
            nc.scalar.activation(cst[:, :], PV[:, C_C:C_C + 16], ACT.Sigmoid).then_inc(sem("csig"), 1)

            def square(l, k):
                if k >= SQN[l]:
                    act.wait_ge(*past(f"ss_mm{l}", k + 1 - SQN[l]))
                nc.scalar.activation(sq[l][:, k % SQN[l]], XT[:, k], ACT.Square).then_inc(sem(f"sq_ready{l}"), 1)

            def norm(l):
                act.wait_ge(*past(f"ss_mm{l}", DT))
                for j, (t0, n) in enumerate(SEGS):
                    nc.scalar.activation(rstd[l][:, t0:t0 + n], ps[:, 4 + j, 0:n], ACT.Sqrt, bias=cols[:, 0:1], scale=1.0 / D).then_inc(sem(f"rms{l}"), 1)
                for k in range(DT):
                    for w, (t0, n) in ((1, (0, CTX)), (0, (CTX, LAT))):
                        act.wait_ge(*past(f"nt_ready{l}", 2 * k + 2 - w))
                        o, i_ = (HT, HL)[l][:, k, t0:t0 + n], ntmp[l][k % 2][:, t0:t0 + n]
                        if l == 1 and w == 0:
                            o = o.rearrange("p (c r) -> p r c", r=ROWS)
                            i_ = i_.rearrange("p (r c) -> p r c", r=ROWS)
                        nc.scalar.activation(o, i_, ACT.Identity, bias=MODv[:, l, k, w:w + 1]).then_inc(sem(["ht_ready", "ht1_full"][l]), 1)
                    if l == 1:
                        act.wait_ge(*past("ht1_full", 2 * k + 2))
                        nc.scalar.activation(HTs[0][:, k], HL[:, k], ACT.Copy).then_inc(sem("ht1_high"), 1)

            for k in range(DT):
                act.wait_ge(*past("xt_ready", 3 * k + 3))
                square(0, k)
            norm(0)
            act.wait_ge(*past("ht_ready", 16))
            act.wait_ge(*past("mod0_mm0", 3))
            act.wait_ge(*past("mod0_mm1", 3))
            for dst, src in (
                (nat[:, 0], A["s5_a_re"][0].rearrange("d g q -> (d g) q")),
                (nat[:, 1], A["s5_a_im"][0].rearrange("d g q -> (d g) q")),
                (nat[:, 2, 0:1], A["s5_log_dt"][0].rearrange("d (g o) -> (d g) o", o=1)),
                (bn[:, 0], A["s5_b_re"][0].rearrange("d g q h -> (d g) q h")),
                (bn[:, 1], A["s5_b_im"][0].rearrange("d g q h -> (d g) q h")),
                (cn[:, :, 0], A["s5_c_re"][0].rearrange("d g h q -> (d g) h q")),
                (cn[:, :, 1], A["s5_c_im"][0].rearrange("d g h q -> (d g) h q")),
            ):
                act.dma_start(dst, src).then_inc(sem("s5_in"), 16)
            act.wait_ge(*past("s5_in", 16 * 7))
            nc.scalar.activation(nat[:, 2, 1:2], nat[:, 2, 0:1], ACT.Exp).then_inc(sem("s5_dt"), 1)
            act.wait_ge(*past("s5_dar", 1))
            nc.scalar.activation(nat[:, 5], nat[:, 3], ACT.Exp).then_inc(sem("s5_mag"), 1)
            act.wait_ge(*past("s5_ang", 1))
            nc.scalar.activation(nat[:, 8], nat[:, 7], ACT.Sin)
            nc.scalar.activation(nat[:, 9], nat[:, 7], ACT.Sin, scale=0.5).then_inc(sem("s5_sin"), 1)
            act.wait_ge(*past("lam_abs", 1))
            nc.scalar.activation(lt[:, 1], lt[:, 0], ACT.Exp, scale=-1.0).then_inc(sem("lam_exp"), 1)
            with act.Fori(0, 4) as i:
                for s in range(2):
                    act.wait_ge(*past(f"u_mm{s}", i + 1))
                    act.wait_ge(*past(f"u_stored{s}", 16 * i))
                    nc.scalar.activation(u_stage[:, s, ::-1, :].rearrange("p s j -> p j s"),
                                         ps3[s].rearrange("p (j s) -> p j s", s=T), ACT.Copy).then_inc(sem(f"u_ev{s}"), 1)
                    act.wait_ge(*past(f"u_ev{s}", i + 1))
                    act.dma_start(u_d[bass.ds(2 * i + s, 1)].rearrange("o p t -> p (o t)"),
                                  u_stage[:, s].rearrange("p s j -> p (s j)")).then_inc(sem(f"u_stored{s}"), 16)
            with act.Fori(0, NB // 2) as i:
                for s in range(2):
                    b = 2 * i + s
                    act.wait_ge(*past(f"x_t{s}", i + 1))
                    act.wait_ge(*past(f"e_mm{1 - s}", i + s))
                    for r in range(2):
                        nc.scalar.activation(Eg[:, r].rearrange("p g c -> p (g c)"), ps[:, r], ACT.Copy).then_inc(sem("eg_ready"), 1)
                    act.wait_ge(*past(f"g_ready{s}", i + 1))
                    act.dma_start(g_d[bass.ds(b, 1)].rearrange("b p n -> p (b n)"), Gb[s]).then_inc(sem(f"g_stored{s}"), 16)
                    act.wait_ge(*past(f"e_mm{s}", i + 1))
                    for o, src in wz_moves(0, b):
                        last = nc.scalar.activation(o, src, ACT.Copy)
                    last.then_inc(sem("wz_a"), 1)
                    act.wait_ge(*past("v_ev", b + 1))
                    act.dma_start(v_d[bass.ds(GB * b, GB)].rearrange("g h c -> h g c"),
                                  Vs.rearrange("p g i h -> p g (i h)")).then_inc(sem("v_stored"), 16)
            act.wait_ge(*past("g_stored0", 16 * NB // 2))
            act.wait_ge(*past("g_stored1", 16 * NB // 2))
            act.wait_ge(*past("lam_ready", 1))
            with act.Fori(0, RH) as i:
                act.wait_ge(*past("rg_bo", 2 * i))
                for s in range(2):
                    act.wait_ge(*past(f"rg_pmm{s}", 2 * i + 1))
                    nc.scalar.activation(xrp[:, s, 1:1 + CTX], ps3[s][:, 0:CTX], ACT.Copy)
                    nc.scalar.activation(xrp[:, s, LOFF + 1:LOFF + 1 + LAT], ps3[s][:, CTX:TOK], ACT.Copy).then_inc(sem(f"rg_ev{s}"), 1)
                act.wait_ge(*past("xc_ready", 2 * i + 2))
                for s in range(2):
                    act.wait_ge(*past(f"rg_pmm{s}", 2 * i + 2))
                    nc.scalar.activation(SG[:, s], ps3[s], ACT.Sigmoid).then_inc(sem("rg_sg"), 1)
                for d in range(2):
                    act.wait_ge(*past("rg_dir", 2 * i + d))
                    for m, (dst, c0) in enumerate(((RT, C_BA), (IT, C_BX))):
                        for s in range(2):
                            act.wait_ge(*past(f"rg_gmm{s}", 4 * i + 2 * d + m + 1))
                            nc.scalar.activation(dst[:, s], ps3[s], ACT.Sigmoid, bias=PV[:, bass.ds(2 * i + (c0 + 8 * d + s), 1)]).then_inc(sem(f"rg_ev{s}"), 1)
                    for s in range(2):
                        act.wait_ge(*past(f"rg_ev{s}", 6 * i + 4 + 2 * d))
                        nc.scalar.activation(AT[:, s], RT[:, s], ACT.Exp, scale=lamc[:, bass.ds(2 * i + (8 * d + s), 1)]).then_inc(sem("rg_at"), 1)
                        act.wait_ge(*past("rg_at", 8 * i + 4 * d + 2 * s + 1))
                        nc.scalar.activation(RT[:, s], RT[:, s], ACT.Tanh, scale=lamc[:, bass.ds(2 * i + (16 + 8 * d + s), 1)]).then_inc(sem("rg_at"), 1)
                    for s in range(2):
                        act.wait_ge(*past("rg_om", 4 * i + 2 * d + s + 1))
                        nc.scalar.activation(RT[:, s], RT[:, s], ACT.Sqrt).then_inc(sem("rg_sq"), 1)
                act.wait_ge(*past("rg_bo", 2 * i + 2))
                act.dma_start(bo_d[bass.ds(2 * i, 2)].rearrange("s p t -> p s t"), HH).then_inc(sem("bo_stored"), 16)
            act.wait_ge(*past("bo_stored", 16 * RH))
            with act.Fori(0, NB // 2) as i:
                for s in range(2):
                    act.wait_ge(*past(f"f_mm{s}", i + 1))
                    act.wait_ge(*past(f"y_stored{s}", 16 * GB * i))
                    nc.scalar.activation(Yb[:, s].rearrange("p (a b) j -> p a (b j)", a=2),
                                         ps[:, 2 * s:2 * s + 2, 0:2 * NJ], ACT.Gelu_apprx_tanh).then_inc(sem(f"y_ev{s}"), 1)
                    act.wait_ge(*past(f"y_ev{s}", i + 1))
                    for g in range(GB):
                        act.dma_start(y_b[bass.ds(GB * (2 * i + s) + g, 1)].rearrange("o t h j -> (o t) h j"), Yb[:, s, g]).then_inc(sem(f"y_stored{s}"), 16)
            act.wait_ge(*past("bo_stored", 16 * RH))
            act.wait_ge(*past("scan", 4 * NJ))
            for m, name in enumerate(("ml_wq", "ml_wk", "ml_wv")):
                act.dma_start(W4[:, m], A[name][0].rearrange("(t b) i o -> (b i) t o", b=32)).then_inc(sem("ml_in"), 16)
            for m in range(3):
                for d in range(2):
                    act.dma_start(WIF[m][:, :, d], A["ml_w_if"][0, d, m].rearrange("(t p) n -> p t n", p=P)).then_inc(sem("ml_in"), 16)
            act.wait_ge(*past("bi_zero", 1))
            for d in range(2):
                for n in range(2):
                    act.dma_start(BI[64 * n + 32 * d:64 * n + 32 * d + MH, :], A["ml_b_if"][0, d, MH * n:MH * n + MH].rearrange("(h o) -> h o", o=1)).then_inc(sem("ml_in"), 16)
            with act.Fori(0, DT) as i:
                act.wait_ge(*past("glu_mm1", i + 1))
                act.wait_ge(*past("glu_ao", i))
                nc.scalar.activation(SGs, ps3[1], ACT.Sigmoid).then_inc(sem("glu_sg"), 1)
                act.wait_ge(*past("glu_mm0", i + 1))
                nc.scalar.activation(SZ, ps3[0], ACT.Sigmoid, bias=PV[:, bass.ds(i + C_GLUB, 1)]).then_inc(sem("glu_ev0"), 1)
            with act.Fori(0, 4) as i:
                for s in range(2):
                    for j in range(2):
                        act.wait_ge(*past("bd_t", 4 * i + (2 * s + j) + 1))
                        nc.scalar.activation(BDT.rearrange("p m c -> p (m c)"), ps[:, 6, 0:3 * P], ACT.Copy).then_inc(sem("bdt_ready"), 1)
                    act.wait_ge(*past(f"eo_ev{s}", 2 * i + 2))
                    nc.scalar.activation(sq[1][:, bass.ds(2 * i + s, 1)].rearrange("p k t -> p (k t)"),
                                         XT[:, bass.ds(2 * i + s, 1)].rearrange("p k t -> p (k t)"), ACT.Square).then_inc(sem("sq_ready1"), 1)
            norm(1)
            with act.Fori(0, MT // 2) as i:
                for s in range(2):
                    m = 2 * i + s
                    act.wait_ge(*past(f"xm_mm{s}", i + 1))
                    act.wait_ge(*past(f"xm_stored{s}", 32 * i))
                    act.wait_ge(*past("gates_mm", 2 * i))
                    nc.scalar.activation(xmp[:, s, 1:1 + CTX], ps3[0][:, 0:CTX], ACT.Copy)
                    nc.scalar.activation(xmp[:, s, LOFF + 1:LOFF + 1 + LAT], ps3[0][:, CTX:TOK], ACT.Copy).then_inc(sem("xm_ev"), 1)
                    act.wait_ge(*past("mcv_ready", m + 1))
                    nc.scalar.activation(mcs, mcv, ACT.Sigmoid).then_inc(sem("mcs_ready"), 1)
                    act.wait_ge(*past(f"z_mm{s}", i + 1))
                    act.wait_ge(*past(f"z_stored{s}", 16 * i))
                    nc.scalar.activation(zo[:, s], psf[:, 3 * BANK:5 * BANK], ACT.Sigmoid).then_inc(sem("zs_ready"), 1)
                    act.wait_ge(*past("xm_ev", m + 1))
                    act.dma_start(xm_d[bass.ds(m, 1), :, 0:CTX].rearrange("o p t -> p (o t)"), xmp[:, s, 1:1 + CTX]).then_inc(sem(f"xm_stored{s}"), 16)
                    act.dma_start(xm_d[bass.ds(m, 1), :, CTX:TOK].rearrange("o p t -> p (o t)"), xmp[:, s, LOFF + 1:LOFF + 1 + LAT]).then_inc(sem(f"xm_stored{s}"), 16)
                    act.wait_ge(*past("xcv_ready", m + 1))
                    act.dma_start(xc_d[bass.ds(m, 1)].rearrange("o p t -> p (o t)"), xco[:, s]).then_inc(sem(f"xcv_stored{s}"), 16)
                    act.wait_ge(*past("z_ev", m + 1))
                    act.dma_start(z_d[bass.ds(m, 1)].rearrange("o p t -> p (o t)"), zo[:, s]).then_inc(sem(f"z_stored{s}"), 16)
            act.wait_ge(*past("gates_mm", MT))
            act.wait_ge(*past("ml_in", 16 * 13))
            for n, r in enumerate((rLI, rLF)):
                nc.scalar.activation(r[0:32], psG[64 * n:64 * n + 32], ACT.Identity, bias=BI[64 * n:64 * n + 32, :])
                for o, src in zip(natural(r, slice(32, 64)), (psG[64 * n + 32:64 * n + 64, 0:CTX], psG[64 * n + 32:64 * n + 64, CTX:TOK])):
                    last = nc.scalar.activation(o, src, ACT.Identity, bias=BI[64 * n + 32:64 * n + 64, :])
                last.then_inc(sem("rows_ready"), 1)
            act.wait_ge(*past("lf_abs", 1))
            nc.scalar.activation(rA, rA, ACT.Exp, scale=-1.0).then_inc(sem("lf_exp"), 1)

            def keys_out(i, ks):
                for k in ks:
                    act.wait_ge(*past("k_mm", 4 * i + k + 1))
                    if k == 0:
                        act.wait_ge(*past("s_mm", 20 * i))
                    nc.scalar.activation(Kt[:, k], ps3[0], ACT.Copy).then_inc(sem("k_ev"), 1)

            for k in range(4):
                keys_out(0, [k])
                act.wait_ge(*past(f"v_mmx{k % 2}", k // 2 + 1))
                nc.scalar.activation(Vt[:, :, P * k:P * k + P], ps3[1].rearrange("p (b c) -> p b c", c=P), ACT.Copy).then_inc(sem("vt_ev"), 1)
            act.wait_ge(*past("m_ready", 1))
            act.wait_ge(*past("em_free", 1))
            nc.scalar.activation(rA[0:32, 0:LAT], rM[0:32, CTX:TOK], ACT.Exp, scale=-1.0)
            nc.scalar.activation(rA[32:64, 0:LAT][:, ::-1], rM[32:64, CTX:TOK], ACT.Exp, scale=-1.0).then_inc(sem("em_ready"), 1)
            act.wait_ge(*past("xr_ready", 1))
            for d in range(2):
                act.dma_start(xr_d[MH * d:MH * d + MH, :], rO[32 * d:32 * d + MH, 0:LAT]).then_inc(sem("xr_stored"), 16)
            act.wait_ge(*past("xr_stored", 32))

            def head(i, last_head):
                def queries(th):
                    for k in range(4):
                        act.wait_ge(*past("q_mm", 8 * i + 4 * th + k + 1))
                        if k == 0:
                            act.wait_ge(*past("s_mm", 20 * i + 10 * th))
                        nc.scalar.activation(Qt[:, k], ps[:, 6 + k % 2], ACT.Copy).then_inc(sem("q_ev"), 1)

                def decays(th):
                    for n, (I, d, js) in enumerate(PIECES[th]):
                        u = NPI * th + n
                        act.wait_ge(*past("p_ready", 2 * NPI * i + max(u - 1, 0)))
                        for J in js:
                            if J == I:
                                x = 8 * th + sum(1 for q in PIECES[th][:n] if q[0] in q[2])
                                act.wait_ge(*past("xmask", 16 * i + x + 1))
                                src = XM[:, x % 2]
                            else:
                                src = Xb[:, d, P * (J - CBLK):P * (J - CBLK) + P]
                            last = nc.scalar.activation(Dt[:, u % 2, P * (J - js[0]):P * (J - js[0]) + P], src, ACT.Exp, bias=YBh[:, d, J, I:I + 1])
                        last.then_inc(sem("d_ready"), 1)

                def heads_out(th):
                    act.wait_ge(*past("h_t", 8 * i + 4 * th))
                    for j in range(HB_):
                        act.wait_ge(*past("rd_ready", 8 * i + 4 * th + j + 1))
                        nc.scalar.activation(Hb[:, j], ps[:, 2 + 2 * (j % 2)], ACT.Copy, scale=rden[:, 4 * th + j, 0:1]).then_inc(sem("hf_ready"), 1)

                def deviations(th):
                    act.wait_ge(*past("mv_ready", 2 * i + th + 1))
                    nc.scalar.activation(mv[:, 4 * th:4 * th + 4, 1], mv[:, 4 * th:4 * th + 4, 1], ACT.Sqrt, bias=cols[:, 0:1]).then_inc(sem("sd_ready"), 1)

                def skip(th):
                    act.wait_ge(*past("wo_mm0", 8 * i + 4 * th))
                    act.wait_ge(*past("wo_mm1", 8 * i + 4 * th))
                    nc.scalar.activation(cst[:, 1 + th:2 + th], cols[:, 0:1], ACT.Copy)
                    for k in range(4):
                        nc.scalar.activation(MX[:, k], Xc[:, k, CTX + HALF * th:CTX + HALF * th + HALF], ACT.Copy,
                                             scale=PV[:, bass.ds(4 * i + (C_SK + k), 1)]).then_inc(sem("sx_ready"), 1)

                act.wait_ge(*past("xb_in", 32 * i + 32))
                act.wait_ge(*past("ybh_ready", i + 1))
                queries(0)
                decays(0)
                queries(1)
                heads_out(0)
                deviations(0)
                skip(0)
                decays(1)
                nc.scalar.activation(cst[:, 0:1], cols[:, 0:1], ACT.Copy).then_inc(sem("xb_used"), 1)
                skip(1)
                heads_out(1)
                if not last_head:
                    keys_out(i + 1, [0, 1])
                deviations(1)
                if not last_head:
                    keys_out(i + 1, [2, 3])

            with act.Fori(0, MH - 1) as i:
                head(i, False)
            head(MH - 1, True)
            for k in range(DT):
                act.wait_ge(*past("xo", 16 * MH - DT + k + 1))
                nc.scalar.activation(SQf[:, k], XT[:, k, CTX:TOK], ACT.Square).then_inc(sem("sqf_ready"), 1)
            act.wait_ge(*past("ssf_mm", 1))
            nc.scalar.activation(rfin, psf[:, 2 * BANK:4 * BANK], ACT.Sqrt, bias=cols[:, 0:1], scale=1.0 / D).then_inc(sem("rf_ready"), 1)
            for b in range(LBLK):
                act.wait_ge(*past("yf_t", b + 1))
                if b >= 2:
                    act.wait_ge(*past(f"out_stored{b % 2}", 16 * (b // 2)))
                nc.scalar.activation(YO[:, b % 2], psf[:, (4 + 2 * (b % 2)) * BANK:(6 + 2 * (b % 2)) * BANK], ACT.Copy).then_inc(sem("out_ready"), 1)

        @block.vector
        def _(dve):
            V = nc.vector
            link_n = [0]

            def link(ins):
                link_n[0] += 1
                ins.then_inc(sem("dve_chain"), 1)
                dve.wait_ge(*past("dve_chain", link_n[0]))

            dve.wait_ge(*past("par_t", 3))
            V.tensor_copy(PV[:, 0:232], ps[:, 7, 0:232]).then_inc(sem("par_ready"), 1)
            V.tensor_copy(PV[:, 256:320], ps[:, 7, 256:320]).then_inc(sem("par_ready"), 1)
            dve.wait_ge(*past("csig", 1))
            V.tensor_tensor(csv.rearrange("p k w -> p w k"), cst[:, :].rearrange("p (w k) -> p w k", w=2),
                            PV[:, C_C:C_C + 16].rearrange("p (w k) -> p w k", w=2), ALU.mult).then_inc(sem("cs_ready"), 1)
            for q in range(24):
                t0, n = SEGS[q % 3]
                dve.wait_ge(*past("xt_t", q + 1))
                V.tensor_copy(XT[:, q // 3, t0:t0 + n], ps[:, q % 4, 0:n]).then_inc(sem("xt_ready"), 1)

            def modulation(l):
                for s in range(2 + l):
                    dve.wait_ge(*past(f"mod{l}_mm{s}", (3, DT + 2)[l]))
                if l == 1:
                    link(V.tensor_tensor(MODv[:, 0, 18:24], ps[:, 7, 64:76].rearrange("p (n w) -> p n w", w=2),
                                         PV[:, C_MODB + 18:C_MODB + 24].unsqueeze(2).to_broadcast([P, 6, 2]), ALU.add))
                nt = (18, 24)[l]
                link(V.tensor_tensor(MODv[:, l, 0:nt], ps[:, 7, 0:2 * nt].rearrange("p (n w) -> p n w", w=2),
                                     PV[:, C_MODB + 24 * l:C_MODB + 24 * l + nt].unsqueeze(2).to_broadcast([P, nt, 2]), ALU.add))
                link(V.scalar_tensor_tensor(out=ACv[:, l], in0=MODv[:, l, DT:2 * DT], scalar=1.0,
                                            in1=PV[:, C_NG + 8 * l:C_NG + 8 * l + 8].unsqueeze(2).to_broadcast([P, DT, 2]),
                                            op0=ALU.add, op1=ALU.mult))

            def low_part(k):
                dve.wait_ge(*past("ht1_high", k + 1))
                V.tensor_tensor(HTs[1][:, k], HL[:, k], HTs[0][:, k].bitcast(F32), ALU.subtract).then_inc(sem("ht1_low"), 1)

            def norm(l):
                dve.wait_ge(*past(f"rms{l}", 3))
                link(V.reciprocal(rstd[l], rstd[l]))
                if l == 0:
                    modulation(0)
                for k in range(DT):
                    if k >= 2:
                        dve.wait_ge(*past(["ht_ready", "ht1_full"][l], 2 * k - 2))
                    for w, (t0, n) in ((1, (0, CTX)), (0, (CTX, LAT))):
                        V.scalar_tensor_tensor(out=ntmp[l][k % 2][:, t0:t0 + n], in0=XT[:, k, t0:t0 + n], scalar=ACv[:, l, k, w:w + 1],
                                               in1=rstd[l][:, t0:t0 + n], op0=ALU.mult, op1=ALU.mult).then_inc(sem(f"nt_ready{l}"), 1)
                    if l == 1 and k:
                        low_part(k - 1)

            norm(0)
            dve.wait_ge(*past("s5_dt", 1))
            V.tensor_scalar(nat[:, 3], nat[:, 0], nat[:, 2, 1:2], None, ALU.mult).then_inc(sem("s5_dar"), 1)
            link(V.tensor_scalar(nat[:, 4], nat[:, 1], nat[:, 2, 1:2], None, ALU.mult))
            link(V.tensor_scalar(nat[:, 6], nat[:, 4], 1.0 / (2 * math.pi), MAGIC, ALU.mult, ALU.add))
            link(V.tensor_scalar(nat[:, 6], nat[:, 6], MAGIC, None, ALU.subtract))
            src = 4
            for c in TWO_PI:
                link(V.scalar_tensor_tensor(out=nat[:, 7], in0=nat[:, 6], scalar=-c, in1=nat[:, src], op0=ALU.mult, op1=ALU.add))
                src = 7
            V.tensor_scalar(nat[:, 7], nat[:, 7], 3.1415925, -3.1415925, ALU.min, ALU.max).then_inc(sem("s5_ang"), 1)
            link(V.tensor_tensor(nat[:, 13], nat[:, 0], nat[:, 0], ALU.mult))
            link(V.tensor_tensor(nat[:, 14], nat[:, 1], nat[:, 1], ALU.mult))
            link(V.tensor_tensor(nat[:, 13], nat[:, 13], nat[:, 14], ALU.add))
            link(V.reciprocal(nat[:, 13], nat[:, 13]))
            dve.wait_ge(*past("s5_mag", 1))
            dve.wait_ge(*past("s5_sin", 1))
            link(V.tensor_tensor(nat[:, 10], nat[:, 9], nat[:, 9], ALU.mult))
            link(V.tensor_scalar(nat[:, 10], nat[:, 10], -2.0, 1.0, ALU.mult, ALU.add))
            link(V.tensor_tensor(nat[:, 11], nat[:, 5], nat[:, 10], ALU.mult))
            link(V.tensor_tensor(nat[:, 12], nat[:, 5], nat[:, 8], ALU.mult))
            link(V.tensor_scalar(nat[:, 15], nat[:, 11], 1.0, None, ALU.subtract))
            link(V.tensor_tensor(nat[:, 14], nat[:, 15], nat[:, 0], ALU.mult))
            link(V.tensor_tensor(nat[:, 16], nat[:, 12], nat[:, 1], ALU.mult))
            link(V.tensor_tensor(nat[:, 14], nat[:, 14], nat[:, 16], ALU.add))
            link(V.tensor_tensor(nat[:, 17], nat[:, 14], nat[:, 13], ALU.mult))
            link(V.tensor_tensor(nat[:, 16], nat[:, 12], nat[:, 0], ALU.mult))
            link(V.tensor_tensor(nat[:, 19], nat[:, 15], nat[:, 1], ALU.mult))
            link(V.tensor_tensor(nat[:, 16], nat[:, 16], nat[:, 19], ALU.subtract))
            V.tensor_tensor(nat[:, 18], nat[:, 16], nat[:, 13], ALU.mult).then_inc(sem("s5_nat"), 1)
            link(V.tensor_scalar(lt[:, 0], PV[:, C_LAM:C_LAM + 16], -1.0, None, ALU.mult))
            link(V.tensor_scalar(lt[:, 4], lt[:, 0], 0.0, None, ALU.max))
            V.tensor_tensor(lt[:, 0], lt[:, 0], PV[:, C_LAM:C_LAM + 16], ALU.max).then_inc(sem("lam_abs"), 1)
            dve.wait_ge(*past("lam_exp", 1))
            log1p(link, lt[:, 1], lt[:, 2], lt[:, 3], lt[:, 5])
            link(V.tensor_tensor(lt[:, 4], lt[:, 4], lt[:, 5], ALU.add))
            link(V.tensor_scalar(lamc[:, 0:16], lt[:, 4], -8.0, None, ALU.mult))
            V.tensor_scalar(lamc[:, 16:32], lt[:, 4], 8.0, None, ALU.mult).then_inc(sem("lam_ready"), 1)
            dve.wait_ge(*past("s5_at", 1))
            for v in range(4):
                for d in range(2):
                    last = V.tensor_copy(AL[64 * d:64 * d + 64, v], ps[64 * (v % 2):64 * (v % 2) + 64, 6, P * (v // 2) + 64 * d:P * (v // 2) + 64 * d + 64])
            link(last)
            for w, dst in enumerate((BT, CT)):
                dve.wait_ge(*past("s5_bct", w + 1))
                for q in range(4):
                    for r in range(2):
                        for d in range(2):
                            V.tensor_copy(dst[64 * d:64 * d + 64, r, 4 * q:4 * q + 4, :],
                                          ps[64 * r:64 * r + 64, q].rearrange("p (h c) -> p h c", h=4)[:, :, 64 * d:64 * d + 64]).then_inc(sem(("s5_bt", "s5_ct")[w]), 1)
            dve.wait_ge(*past("s5_ct", 16))
            dve.wait_ge(*past("u_stored0", 64))
            dve.wait_ge(*past("u_stored1", 64))
            dve.wait_ge(*past("s5_in", 128))
            V.tensor_copy(sa[:, 0, 0], AL[:, 0])
            V.tensor_copy(sa[:, 0, 1], AL[:, 0])
            V.tensor_scalar(sa[:, 1, 0], AL[:, 1], -1.0, None, ALU.mult)
            V.tensor_copy(sa[:, 1, 1], AL[:, 1])
            V.memset(Q[:, 0, 0], 1.0)
            V.memset(Q[:, 0, 1], 0.0)
            link(V.tensor_copy(Q[:, 1], AL[:, 0:2]))
            for k in range(2, SL):
                V.tensor_tensor(Q[:, k], Q[:, k - 1], sa[:, 0], ALU.mult)
                link(V.tensor_tensor(sa[:, 2], Q[:, k - 1, ::-1], sa[:, 1], ALU.mult))
                link(V.tensor_tensor(Q[:, k], Q[:, k], sa[:, 2], ALU.add))
            V.tensor_copy(A1[:, 0], Q[:, T, 0])
            V.tensor_copy(A1[:, 1], Q[:, T, 0])
            V.tensor_scalar(A2[:, 1], Q[:, T, 1], -1.0, None, ALU.mult)
            V.tensor_copy(A2[:, 0], Q[:, T, 1])
            f, bk = slice(0, 64), slice(64, 128)
            V.tensor_copy(PWE[f], Q[f, 0:T])
            V.tensor_copy(PWE[bk], Q[bk, T - 1::-1])
            V.tensor_copy(PWF[f, :, 0], Q[f, :, 0])
            V.tensor_copy(PWF[bk, :, 0], Q[bk, ::-1, 0])
            V.tensor_scalar(PWF[f, :, 1], Q[f, :, 1], -1.0, None, ALU.mult)
            V.tensor_scalar(PWF[bk, :, 1], Q[bk, ::-1, 1], -1.0, None, ALU.mult)
            co = [AL[:, 2 + r:3 + r].to_broadcast([P, 2 * HC, G]) for r in range(2)]
            V.tensor_tensor(BB.rearrange("p r h g -> p (r h) g"), BT.rearrange("p r h g -> p (r h) g"), co[0], ALU.mult)
            for r in range(2):
                last = V.tensor_tensor(tB[:, r], BT[:, 1 - r], co[1][:, 0:HC], ALU.mult)
            link(last)
            V.tensor_tensor(BB[:, 0], BB[:, 0], tB[:, 0], ALU.subtract)
            link(V.tensor_tensor(BB[:, 1], BB[:, 1], tB[:, 1], ALU.add))
            link(V.tensor_tensor(Dg, ident[0:HC, 0:HC].unsqueeze(1).to_broadcast([HC, G, HC]), dcol.unsqueeze(2).to_broadcast([HC, G, HC]), ALU.mult))
            V.memset(sa[:, 2, 0, 0:1], 0.0).then_inc(sem("s5_tables"), 1)
            dve.wait_ge(*past("s5_tables", 1))
            n0 = link_n[0]

            def chained(n):
                dve.wait_ge(*past("dve_chain", n0 + n))

            def state_maps(i, s, n):
                b = 2 * i + s
                gs = bass.ds(GB * b, GB)

                def pw(r):
                    return PWE[:, :, r, gs].rearrange("p k g -> p g k").unsqueeze(2).to_broadcast([P, GB, HC, T])

                def bb(r):
                    return BB[:, r, :, gs].rearrange("p h g -> p g h").unsqueeze(3).to_broadcast([P, GB, HC, T])

                def xo(ap):
                    return ap.rearrange("p (g h k) -> p g h k", g=GB, h=HC)

                dve.wait_ge(*past(f"x_t{s}", i))
                dve.wait_ge(*past(f"x_ready{1 - s}", i + s))
                x = [X[:, s, r].rearrange("p g c -> p (g c)") for r in range(2)]
                V.tensor_tensor(xo(x[0]), pw(0), bb(0), ALU.mult)
                V.tensor_tensor(xo(xt1), pw(1), bb(1), ALU.mult)
                V.tensor_tensor(xo(x[1]), pw(0), bb(1), ALU.mult)
                V.tensor_tensor(xo(xt2), pw(1), bb(0), ALU.mult).then_inc(sem("dve_chain"), 1)
                chained(n)
                V.tensor_tensor(x[0], x[0], xt1, ALU.subtract)
                V.tensor_tensor(x[1], x[1], xt2, ALU.add).then_inc(sem(f"x_ready{s}"), 1)

            def lag_matrices(i, s, n):
                b = 2 * i + s
                gs = bass.ds(GB * b, GB)
                dve.wait_ge(*past(f"v_mm{s}", i + 1))
                dve.wait_ge(*past("v_stored", 16 * b))
                bank = [ps[0:HC, 6 + d].rearrange("p (g k h) -> p g k h", g=GB, h=HC) for d in range(2)]
                V.tensor_copy(Vs[:, :, 0:T], bank[1])
                V.tensor_copy(Vs[:, :, T:LAG], bank[0][:, :, 1:T])
                V.tensor_copy(vtmp, bank[1][:, :, T - 1]).then_inc(sem("dve_chain"), 1)
                chained(n)
                V.tensor_tensor(Vs[:, :, T - 1], bank[0][:, :, 0], vtmp, ALU.add).then_inc(sem("v_mid"), 1)
                dve.wait_ge(*past("v_mid", b + 1))
                V.tensor_tensor(Vs[:, :, T - 1], Vs[:, :, T - 1], Dg[:, gs], ALU.add).then_inc(sem("v_ev"), 1)
                dve.wait_ge(*past(f"e_mm{s}", i + 1))
                for o, src in wz_moves(1, b):
                    last = V.tensor_copy(o, src)
                last.then_inc(sem("wz_v"), 1)

            state_maps(0, 0, 1)
            with dve.Fori(0, NB // 2 - 1) as i:
                state_maps(i, 1, 4 * i + 2)
                lag_matrices(i, 0, 4 * i + 3)
                state_maps(i + 1, 0, 4 * i + 4)
                lag_matrices(i, 1, 4 * i + 5)
            state_maps(NB // 2 - 1, 1, 2 * NB - 2)
            lag_matrices(NB // 2 - 1, 0, 2 * NB - 1)
            lag_matrices(NB // 2 - 1, 1, 2 * NB)
            link_n[0] = n0 + 2 * NB
            dve.wait_ge(*past("g_stored0", 16 * NB // 2))
            dve.wait_ge(*past("g_stored1", 16 * NB // 2))
            dve.wait_ge(*past("e_mm0", NB // 2))
            dve.wait_ge(*past("e_mm1", NB // 2))
            n0, per = link_n[0], 17
            with dve.Fori(0, RH) as i:
                k = [0]

                def ilink(ins):
                    k[0] += 1
                    ins.then_inc(sem("dve_chain"), 1)
                    dve.wait_ge(*past("dve_chain", per * i + (n0 + k[0])))

                dve.wait_ge(*past("rg_bo", 2 * i))
                for s in range(2):
                    V.memset(xrp[:, s, 0:1], 0.0)
                    V.memset(xrp[:, s, CTX + 1:LOFF + 1], 0.0)
                    last = V.memset(xrp[:, s, PAD - 2:PAD], 0.0)
                ilink(last)
                for s in range(2):
                    def tap(j):
                        return PV[:, bass.ds(2 * i + (C_RCW + 8 * j + s), 1)]

                    dve.wait_ge(*past(f"rg_ev{s}", 6 * i + 1))
                    dve.wait_ge(*past("xc_ready", 2 * i + s))
                    ilink(V.tensor_scalar(TT, xrp[:, s, 0:CV], tap(0), PV[:, bass.ds(2 * i + (C_RCB + s), 1)], ALU.mult, ALU.add))
                    for j in (1, 2):
                        ilink(V.scalar_tensor_tensor(out=TT, in0=xrp[:, s, j:j + CV], scalar=tap(j), in1=TT, op0=ALU.mult, op1=ALU.add))
                    V.scalar_tensor_tensor(out=xcb[:, s, 0:CTX], in0=xrp[:, s, 3:3 + CTX], scalar=tap(3), in1=TT[:, 0:CTX], op0=ALU.mult, op1=ALU.add)
                    V.scalar_tensor_tensor(out=xcb[:, s, CTX:TOK], in0=xrp[:, s, LOFF + 3:PAD], scalar=tap(3), in1=TT[:, LOFF:CV], op0=ALU.mult, op1=ALU.add).then_inc(sem("xc_ready"), 1)
                for s in range(2):
                    dve.wait_ge(*past("rg_sg", 2 * i + s + 1))
                    V.tensor_tensor(SG[:, s], ps3[s], SG[:, s], ALU.mult).then_inc(sem(f"rg_ev{s}"), 1)
                for d in range(2):
                    for s in range(2):
                        dve.wait_ge(*past(f"rg_ev{s}", 6 * i + 4 + 2 * d))
                        last = V.tensor_tensor(IT[:, s], IT[:, s], xcb[:, s], ALU.mult)
                    ilink(last)
                    for s in range(2):
                        dve.wait_ge(*past("rg_at", 8 * i + 4 * d + 2 * s + 2))
                        ilink(V.tensor_tensor(TT[:, 0:TOK], AT[:, s], AT[:, s], ALU.mult))
                        V.scalar_tensor_tensor(out=RT[:, s], in0=TT[:, 0:TOK], scalar=1.0, in1=RT[:, s], op0=ALU.add, op1=ALU.mult).then_inc(sem("rg_om"), 1)
                        dve.wait_ge(*past("rg_om", 4 * i + 2 * d + s + 1))
                    for s in range(2):
                        dve.wait_ge(*past("rg_sq", 4 * i + 2 * d + s + 1))
                        last = V.tensor_tensor(IT[:, s], IT[:, s], RT[:, s], ALU.mult)
                    ilink(last)
                    if d == 0:
                        dve.wait_ge(*past("bo_stored", 16 * i))
                        for s in range(2):
                            last = V.tensor_tensor_scan(HH[:, s], AT[:, s], IT[:, s], 0.0, ALU.mult, ALU.add)
                        last.then_inc(sem("rg_dir"), 1)
                    else:
                        for s in range(2):
                            a, v, o = (z[:, s, 0:CTX][:, ::-1] for z in (AT, IT, RT))
                            last = V.tensor_tensor_scan(o, a, v, 0.0, ALU.mult, ALU.add)
                        ilink(last)
                        for s in range(2):
                            a, v, o = (z[:, s, CTX:TOK][:, ::-1] for z in (AT, IT, RT))
                            last = V.tensor_tensor_scan(o, a, v, RT[:, s, 0:1], ALU.mult, ALU.add)
                        ilink(last)
                        for s in range(2):
                            last = V.tensor_tensor(HH[:, s], HH[:, s], RT[:, s], ALU.add)
                        last.then_inc(sem("rg_dir"), 1)
                        dve.wait_ge(*past("rg_dir", 2 * i + 2))
                        for s in range(2):
                            V.tensor_tensor(HH[:, s], HH[:, s], SG[:, s], ALU.mult).then_inc(sem("rg_bo"), 1)
                assert k[0] == per, k
            link_n[0] = n0 + per * RH
            dve.wait_ge(*past("bo_stored", 16 * RH))
            dve.wait_ge(*past("scan", 4 * NJ))
            with dve.Fori(0, NB // 2) as i:
                for s in range(2):
                    gs = bass.ds(GB * (2 * i + s), GB)
                    dve.wait_ge(*past(f"f_mm{s}", i))

                    def take(rw, steps):
                        return WZ[rw, steps, :, gs].rearrange("p j r g -> p r g j")

                    V.tensor_copy(Zb[f, s], take(f, slice(0, NJ)))
                    V.tensor_copy(Zb[bk, s, :, :, 0:NJC][:, :, :, ::-1], take(bk, slice(0, NJC)))
                    V.tensor_copy(Zb[bk, s, :, :, NJC:NJ][:, :, :, ::-1], take(bk, slice(NJC, NJ))).then_inc(sem(f"z_ready{s}"), 1)
            n0, per = link_n[0], 1
            dve.wait_ge(*past("y_in", 16))
            with dve.Fori(0, DT) as i:
                dve.wait_ge(*past("glu_sg", i + 1))
                V.tensor_tensor(SGs, ps3[1], SGs, ALU.mult).then_inc(sem("glu_ev1"), 1)
                dve.wait_ge(*past("glu_ev0", i + 1))
                V.tensor_tensor(SZ, SZ, YT[:, bass.ds(i, 1)].rearrange("p k t -> p (k t)"), ALU.mult).then_inc(sem("dve_chain"), 1)
                dve.wait_ge(*past("dve_chain", i + (n0 + 1)))
                dve.wait_ge(*past("glu_ev1", i + 1))
                V.tensor_tensor(AO[:, bass.ds(i, 1)].rearrange("p k (j t) -> p (k j) t", t=T), SZ.rearrange("p (t j) -> p j t", t=T),
                                SGs.rearrange("p (j t) -> p j t", t=T), ALU.mult).then_inc(sem("glu_ao"), 1)
            link_n[0] = n0 + DT
            modulation(1)
            dve.wait_ge(*past("mix_in", 32))

            with dve.Fori(0, 4) as i:
                for s in range(2):
                    for j in range(2):
                        t = 4 * i + (2 * s + j)
                        dve.wait_ge(*past("fold_mm", t + 1))
                        V.tensor_copy(WFc[:, bass.ds(t, 1)].rearrange("p t w n -> p (t w n)"), ps[:, 6, 3 * P:3 * P + 32]).then_inc(sem("fold_ev"), 1)
                    dve.wait_ge(*past(f"eo_mm{s}", i + 1))
                    for w, (t0, n) in ((1, (0, CTX)), (0, (CTX, LAT))):
                        x = XT[:, bass.ds(2 * i + s, 1), t0:t0 + n].rearrange("p k t -> p (k t)")
                        V.scalar_tensor_tensor(out=x, in0=ps3[s][:, t0:t0 + n], scalar=MOD[:, bass.ds(4 * i + (2 * (16 + s) + w), 1)],
                                               in1=x, op0=ALU.mult, op1=ALU.add).then_inc(sem(f"eo_ev{s}"), 1)
            dve.wait_ge(*past("eo_ev0", 8))
            dve.wait_ge(*past("eo_ev1", 8))
            norm(1)
            low_part(DT - 1)
            for s in range(2):
                V.memset(xmp[:, s, 0:1], 0.0)
                V.memset(xmp[:, s, CTX + 1:LOFF + 1], 0.0)
                last = V.memset(xmp[:, s, PAD - 2:PAD], 0.0)
            link(last)
            n0, per = link_n[0], 6
            with dve.Fori(0, MT // 2) as i:
                k = [0]

                def ilink(ins):
                    k[0] += 1
                    ins.then_inc(sem("dve_chain"), 1)
                    dve.wait_ge(*past("dve_chain", per * i + (n0 + k[0])))

                for s in range(2):
                    m = 2 * i + s

                    def tap(j):
                        return PV[:, bass.ds(2 * i + (C_MCW + MT * j + s), 1)]

                    dve.wait_ge(*past("xm_ev", m + 1))
                    dve.wait_ge(*past("xcv_ready", m))
                    ilink(V.tensor_scalar(mcv, xmp[:, s, 0:CV], tap(0), PV[:, bass.ds(2 * i + (C_MCB + s), 1)], ALU.mult, ALU.add))
                    for j in (1, 2):
                        ilink(V.scalar_tensor_tensor(out=mcv, in0=xmp[:, s, j:j + CV], scalar=tap(j), in1=mcv, op0=ALU.mult, op1=ALU.add))
                    V.scalar_tensor_tensor(out=mcv, in0=xmp[:, s, 3:3 + CV], scalar=tap(3), in1=mcv, op0=ALU.mult, op1=ALU.add).then_inc(sem("mcv_ready"), 1)
                    dve.wait_ge(*past("mcs_ready", m + 1))
                    dve.wait_ge(*past(f"xcv_stored{s}", 16 * i))
                    dve.wait_ge(*past("gates_mm", 2 * i))
                    V.tensor_tensor(xco[:, s, 0:CTX], mcv[:, 0:CTX], mcs[:, 0:CTX], ALU.mult)
                    V.tensor_tensor(xco[:, s, CTX:TOK], mcv[:, LOFF:CV], mcs[:, LOFF:CV], ALU.mult).then_inc(sem("xcv_ready"), 1)
                    dve.wait_ge(*past("zs_ready", m + 1))
                    V.tensor_tensor(zo[:, s], psf[:, 3 * BANK:5 * BANK], zo[:, s], ALU.mult).then_inc(sem("z_ev"), 1)
                assert k[0] == per, k
            link_n[0] = n0 + per * (MT // 2)
            dve.wait_ge(*past("rows_ready", 2))
            link(V.tensor_scalar(rA, rLF, -1.0, None, ALU.mult))
            V.tensor_tensor(rA, rA, rLF, ALU.max).then_inc(sem("lf_abs"), 1)
            link(V.memset(rRes, 1.0))
            link(V.memset(rRes.rearrange("p (b c) -> p b c", c=P)[:, :, 0], 0.0))
            dve.wait_ge(*past("lf_exp", 1))
            log1p(link, rA, rB, rC, rM)
            link(V.tensor_scalar(rLF, rLF, 0.0, None, ALU.min))
            link(V.tensor_tensor(rLF, rLF, rM, ALU.subtract))
            V.memset(TR[:, 0, 0, 0:1], 0.0).then_inc(sem("em_free"), 1)
            link(V.tensor_tensor_scan(rC, rRes, rLF, 0.0, ALU.mult, ALU.add))
            V.tensor_tensor_scan(rM, rLF, rLI, 0.0, ALU.add, ALU.max).then_inc(sem("m_ready"), 1)
            dve.wait_ge(*past("m_ready", 1))
            V.tensor_tensor(rO[0:32, 0:LAT], rC[0:32, CTX:TOK], rM[0:32, CTX:TOK], ALU.subtract)
            V.tensor_tensor(rO[32:64, 0:LAT][:, ::-1], rC[32:64, CTX:TOK], rM[32:64, CTX:TOK], ALU.subtract).then_inc(sem("xr_ready"), 1)
            V.tensor_tensor(rB[0:32], rLI[0:32], rC[0:32], ALU.subtract)
            for o, (t0, n) in zip(natural(rB, slice(32, 64)), ((0, CTX), (CTX, LAT))):
                last = V.tensor_tensor(o, rLI[32:64, t0:t0 + n], rC[32:64, t0:t0 + n], ALU.subtract)
            last.then_inc(sem("yr_ready"), 1)
            idl = ident[0:64, 0:64].rearrange("p (d h) -> p d h", d=2)[:, :, 0:MH].unsqueeze(3).to_broadcast([64, 2, MH, NBLK])
            tbl = rC.rearrange("p (b c) -> p b c", c=P)[:, :, P - 1].unsqueeze(1).unsqueeze(1).to_broadcast([64, 2, MH, NBLK])
            dve.wait_ge(*past("em_free", 1))
            V.tensor_tensor(TR, idl, tbl, ALU.mult).then_inc(sem("tr_ready"), 1)
            dve.wait_ge(*past("rows_t", 1))
            yt = psf[:, 2 * BANK:2 * BANK + 640].rearrange("p (b c) -> p b c", c=64)
            for d in range(2):
                diag = at(K1 + 192 + 400 * d, 400).rearrange("p (j i h) -> p (j i) h", j=NBLK, i=NBLK)[:, 0::NBLK + 1]
                V.tensor_copy(diag, yt[:, :, 32 * d:32 * d + MH])
            V.tensor_copy(TB, ps[:, 4, 0:80].rearrange("p (d h j) -> p d h j", d=2, h=MH))
            link(V.tensor_copy(EMT, ps[:, 5].rearrange("p (j d c) -> p j d c", j=LBLK, d=2)[:, :, :, 0:MH]))
            for q in range(NBLK - 1):
                for d in range(2):
                    t = TB[:, d, :, q]
                    nat_ = {step_of(d, I): I for I in range(NBLK)}
                    J0, J1 = nat_[q], nat_[q + 1]
                    done = sorted(nat_[x] for x in range(q + 1))
                    runs = []
                    for I in done:
                        if runs and runs[-1][-1] == I - 1:
                            runs[-1].append(I)
                        else:
                            runs.append([I])
                    for r in runs:
                        sl = slice(r[0], r[-1] + 1)
                        last = V.tensor_tensor(YB[:, d, J1, sl], YB[:, d, J0, sl], t.unsqueeze(1).to_broadcast([P, len(r), MH]), ALU.add)
                link(last)
            n0, per = link_n[0], 20

            def values_out(i, ks):
                for k in ks:
                    dve.wait_ge(*past(f"v_mmx{k % 2}", 2 * i + k // 2 + 1))
                    if k == 0:
                        dve.wait_ge(*past("pv_mm", 8 * i))
                    V.tensor_copy(Vt[:, :, P * k:P * k + P], ps3[1].rearrange("p (b c) -> p b c", c=P)).then_inc(sem("vt_ev"), 1)

            def head(i, last_head):
                k_ = [0]

                def ilink(ins):
                    k_[0] += 1
                    ins.then_inc(sem("dve_chain"), 1)
                    dve.wait_ge(*past("dve_chain", per * i + (n0 + k_[0])))

                dve.wait_ge(*past("d_ready", 2 * NPI * i))
                V.tensor_copy(EMh, EMT[:, :, :, bass.ds(i, 1)].rearrange("p j d o -> p j (d o)"))
                V.tensor_copy(YBh.rearrange("p d j i -> p (d j i)"), YB[:, :, :, :, bass.ds(i, 1)].rearrange("p d j i o -> p (d j i o)")).then_inc(sem("ybh_ready"), 1)

                def weigh(th):
                    for n, (I, d, js) in enumerate(PIECES[th]):
                        u = NPI * th + n
                        if n == 0 or PIECES[th][n - 1][0] != I:
                            dve.wait_ge(*past("s_mm", 20 * i + 10 * th + I + 1))
                        dve.wait_ge(*past("d_ready", 2 * NPI * i + u + 1))
                        if n == 0:
                            dve.wait_ge(*past("pv_mm", 8 * i + 4 * th))
                        w_ = P * len(js)
                        c0 = P * (js[0] - CBLK - HB_ * th)
                        o = POFF[th][I, d]
                        V.scalar_tensor_tensor(out=Pm[:, o:o + w_], in0=ps[:, I % 2, c0:c0 + w_], scalar=MD ** -0.5,
                                               in1=Dt[:, u % 2, 0:w_], op0=ALU.mult, op1=ALU.mult).then_inc(sem("p_ready"), 1)

                def heads_out(th):
                    for j in range(HB_):
                        q = 4 * th + j
                        dve.wait_ge(*past("pv_mm", 8 * i + q + 1))
                        ilink(V.tensor_tensor(rden[:, q], ps[:, 6 + j % 2, 0:2], EMh[:, q], ALU.max))
                        ilink(V.scalar_tensor_tensor(out=rden[:, q], in0=ps[:, 6 + j % 2, 0:2], scalar=-1.0, in1=rden[:, q], op0=ALU.mult, op1=ALU.max))
                        V.reciprocal(rden[:, q], rden[:, q]).then_inc(sem("rd_ready"), 1)
                        dve.wait_ge(*past("hf_ready", 8 * i + q + 1))
                        V.scalar_tensor_tensor(out=Hb[:, j], in0=ps[:, 3 + 2 * (j % 2)], scalar=rden[:, q, 1:2], in1=Hb[:, j],
                                               op0=ALU.mult, op1=ALU.add).then_inc(sem("h_ev"), 1)
                        dve.wait_ge(*past("h_ev", 8 * i + q + 1))
                        last = V.bn_stats(bst[:, q], Hb[:, j])
                        if j == HB_ - 1:
                            ilink(last)
                    V.tensor_copy(scanP[:, 200:201], bst[:, 4 * th, 0:1])
                    for j in range(HB_):
                        last = V.bn_aggr(mv[:, 4 * th + j], bst[:, 4 * th + j])
                    last.then_inc(sem("mv_ready"), 1)

                def normed(th):
                    dve.wait_ge(*past("sd_ready", 2 * i + th + 1))
                    ilink(V.reciprocal(mv[:, 4 * th:4 * th + 4, 1], mv[:, 4 * th:4 * th + 4, 1]))
                    for j in range(HB_):
                        m_ = mv[:, 4 * th + j]
                        V.tensor_scalar(Hb[:, j], Hb[:, j], m_[:, 0:1], m_[:, 1:2], ALU.subtract, ALU.mult).then_inc(sem("hn_ready"), 1)

                def mixed(th):
                    dve.wait_ge(*past("sx_ready", 8 * i + 4 * th + 4))
                    for j in range(HB_):
                        dve.wait_ge(*past("h_t", 8 * i + 4 * th + j + 1))
                        for k in range(4):
                            last = V.scalar_tensor_tensor(out=MX[:, k, P * j:P * j + P], in0=ps[:, 6 + j % 2, P * k:P * k + P],
                                                          scalar=PV[:, bass.ds(4 * i + (C_MG + k), 1)], in1=MX[:, k, P * j:P * j + P],
                                                          op0=ALU.mult, op1=ALU.add)
                        last.then_inc(sem("ht_ev"), 1)
                    dve.wait_ge(*past("ht_ev", 8 * i + 4 * th + 4))
                    dve.wait_ge(*past("zt_in", 32 * i + 16 * th + 16))
                    V.tensor_tensor(MX, MX, Zt, ALU.mult).then_inc(sem("mix"), 1)
                    for n in range(DT):
                        dve.wait_ge(*past(f"wo_mm{n % 2}", 8 * i + 4 * th + n // 2 + 1))
                        x = XT[:, n, CTX:TOK].rearrange("p (r c) -> p c r", r=ROWS)[:, 32 * th:32 * th + 32]
                        V.scalar_tensor_tensor(out=x, in0=ps[:, n % 2].rearrange("p (c r) -> p c r", r=ROWS), scalar=gs1[:, n, 0:1],
                                               in1=x, op0=ALU.mult, op1=ALU.add).then_inc(sem("xo"), 1)

                weigh(0)
                heads_out(0)
                normed(0)
                weigh(1)
                mixed(0)
                heads_out(1)
                if not last_head:
                    values_out(i + 1, [0])
                normed(1)
                if not last_head:
                    values_out(i + 1, [1, 2, 3])
                mixed(1)
                assert k_[0] == per

            with dve.Fori(0, MH - 1) as i:
                head(i, False)
            head(MH - 1, True)
            link_n[0] = n0 + per * MH
            dve.wait_ge(*past("rf_ready", 1))
            for t in range(2):
                h = slice(BANK * t, BANK * t + BANK)
                link(V.reciprocal(rfin[:, h], rfin[:, h]))
                for k in range(DT):
                    V.scalar_tensor_tensor(out=YF[:, k, h], in0=XT[:, k, CTX + BANK * t:CTX + BANK * t + BANK], scalar=PV[:, C_FG + k:C_FG + k + 1],
                                           in1=rfin[:, h], op0=ALU.mult, op1=ALU.mult).then_inc(sem("yf_ready"), 1)

        @block.gpsimd
        def _(pool):
            GP = nc.gpsimd
            GP.memset(ident[:, :], 0.0).then_inc(sem("consts"), 1)
            GP.memset(ones[:, :], 1.0).then_inc(sem("consts"), 1)
            GP.memset(cols[:, :], EPS).then_inc(sem("consts"), 1)
            pool.wait_ge(*past("consts", 3))
            GP.affine_select(out=ident[:, :], in_=ident[:, :], compare_op=ALU.not_equal, fill=1.0, base=0,
                             pattern=[[-1, P]], channel_multiplier=1).then_inc(sem("consts"), 1)
            pool.wait_ge(*past("s5_tables", 1))
            with pool.Fori(0, NB // 2) as i:
                for s in range(2):
                    gs = bass.ds(GB * (2 * i + s), GB)

                    def pw(r):
                        return PWF[:, :, r, gs].rearrange("p k g -> p g k").unsqueeze(3).to_broadcast([P, GB, SL, HC])

                    def cc(r):
                        return CT[:, r, :, gs].rearrange("p h g -> p g h").unsqueeze(2).to_broadcast([P, GB, SL, HC])

                    def go(ap):
                        return ap.rearrange("p (g k h) -> p g k h", g=GB, h=HC)

                    pool.wait_ge(*past(f"v_mm{s}", i))
                    pool.wait_ge(*past(f"g_stored{s}", 16 * i))
                    pool.wait_ge(*past(f"g_ready{1 - s}", i + s))
                    pool.wait_ge(*past("s5_tables", 1))
                    GP.tensor_copy(BBv[:, s], BB[:, :, :, gs])
                    GP.tensor_tensor(Gv[s][:, :, 0], pw(0), cc(0), ALU.mult)
                    GP.tensor_tensor(go(pg1), pw(1), cc(1), ALU.mult)
                    GP.tensor_tensor(Gv[s][:, :, 1], pw(1), cc(0), ALU.mult)
                    GP.tensor_tensor(go(pg2), pw(0), cc(1), ALU.mult).then_inc(sem("pool_g"), 1)
                    pool.wait_ge(*past("pool_g", 2 * i + (s + 1)))
                    pool.wait_ge(*past("s5_tables", 1))
                    GP.tensor_tensor(Gv[s][:, :, 0], Gv[s][:, :, 0], go(pg1), ALU.add)
                    GP.tensor_tensor(Gv[s][:, :, 1], Gv[s][:, :, 1], go(pg2), ALU.subtract).then_inc(sem(f"g_ready{s}"), 1)
            pool.wait_ge(*past("wz_a", NB))
            pool.wait_ge(*past("wz_v", NB))
            pool.wait_ge(*past("lam_ready", 1))
            GP.memset(WZ[:, 0], 0.0).then_inc(sem("scan0"), 1)
            pool.wait_ge(*past("scan0", 1))
            with pool.Fori(0, NJ) as i:
                z = WZ[:, bass.ds(i, 1)].rearrange("p j r g -> p (j r) g")
                w = WZ[:, bass.ds(i + 1, 1)].rearrange("p j r g -> p (j r) g")
                pool.wait_ge(*past("scan", 4 * i))
                pool.wait_ge(*past("scan0", 1))
                GP.tensor_tensor(SP1, z, A1, ALU.mult).then_inc(sem("scan"), 1)
                GP.tensor_tensor(SP2[:, ::-1], z, A2, ALU.mult).then_inc(sem("scan"), 1)
                pool.wait_ge(*past("scan", 4 * i + 2))
                GP.tensor_tensor(SP1, SP1, SP2, ALU.add).then_inc(sem("scan"), 1)
                pool.wait_ge(*past("scan", 4 * i + 3))
                pool.wait_ge(*past("scan0", 1))
                GP.tensor_tensor(w, w, SP1, ALU.add).then_inc(sem("scan"), 1)
            pool.wait_ge(*past("bo_stored", 16 * RH))
            GP.memset(BI[:, :], 0.0).then_inc(sem("bi_zero"), 1)
            for q in range(6):
                if q >= 3:
                    pool.wait_ge(*past(f"mod1_mm{q - 3}", 1))
                pool.dma_start(modw1[:, q % 3], mod_v[0][:, :, (18 + q) * P:(19 + q) * P]).then_inc(sem(f"mod1_in{q % 3}"), 16)
            with pool.Fori(0, DT) as i:
                for q in range(3):
                    pool.wait_ge(*past(f"mod1_mm{q}", i + 2))
                    pool.dma_start(modw1[:, q], mod_v[1][:, :, bass.ds((3 * i + q) * P, P)]).then_inc(sem(f"mod1_in{q}"), 16)
            pool.wait_ge(*past("glu_ao", DT))
            GP.memset(bmask, 1.0).then_inc(sem("bm"), 1)
            pool.wait_ge(*past("bm", 1))
            GP.affine_select(out=bmask, in_=bmask, compare_op=ALU.is_ge, fill=0.0, base=0, pattern=[[-4, 32], [0, 4]], channel_multiplier=1).then_inc(sem("bm"), 1)
            pool.wait_ge(*past("bm", 2))
            GP.affine_select(out=bmask, in_=bmask, compare_op=ALU.is_ge, fill=0.0, base=3, pattern=[[4, 32], [0, 4]], channel_multiplier=-1).then_inc(sem("bm"), 1)
            GP.memset(WFs, 0.0).then_inc(sem("wf_zero"), 1)
            pool.wait_ge(*past("wf_zero", 1))
            pool.wait_ge(*past("bm", 3))
            pool.wait_ge(*past("ml_in", 16 * 13))

            def block_diagonal(o, m, t):
                return GP.tensor_tensor(o.rearrange("p (b o) -> p b o", o=4), bmask, W4[:, m, bass.ds(t, 1)].to_broadcast([P, 32, 4]), ALU.mult)

            with pool.Fori(0, MT) as i:
                pool.wait_ge(*past("bd_t", i))
                pool.wait_ge(*past("bm", 3))
                for m in range(3):
                    last = block_diagonal(BD[:, m], m, i)
                last.then_inc(sem("bd_ready"), 1)
            pool.wait_ge(*past("fold_ev", MT))
            pool.wait_ge(*past("gates_open", 3))
            with pool.Fori(0, MT // 2) as i:
                for s in range(2):
                    for z, kind in enumerate(("xm", "z")):
                        pool.wait_ge(*past(f"{kind}_w", 16 * (2 * i + s) + 16))
                        pool.wait_ge(*past(f"{kind}_mm{1 - s}", i + s))
                        pool.wait_ge(*past("bm", 3))
                        GP.tensor_tensor(WXs[z][:, 0], Wv[:, z], ones[:, :].unsqueeze(1).to_broadcast([P, DT, P]), ALU.mult).then_inc(sem("w_high"), 1)
                        pool.wait_ge(*past("w_high", 4 * i + (2 * s + z + 1)))
                        pool.wait_ge(*past("bm", 3))
                        GP.tensor_tensor(WXs[z][:, 1], Wv[:, z], WXs[z][:, 0].bitcast(F32), ALU.subtract).then_inc(sem(f"{kind}_split"), 1)
                    if s == 0:
                        pool.wait_ge(*past("gates_mm", 2 * i))
                    pool.wait_ge(*past("bm", 3))
                    for w in range(2):
                        o = WFs[:, s, w].rearrange("p (n d c) -> p n d c", n=2, d=2)[:, :, :, 0:MH]
                        src = WFc[:, bass.ds(2 * i + s, 1), w].rearrange("p t (d n h) -> p (t n) d h", d=2, n=2)
                        last = GP.tensor_copy(o, src)
                    last.then_inc(sem("wf_ready"), 1)
            pool.wait_ge(*past("gates_mm", MT))
            GP.memset(cmask, 0.0).then_inc(sem("cm"), 1)
            pool.wait_ge(*past("cm", 1))
            GP.affine_select(out=cmask[:, 0], in_=cmask[:, 0], compare_op=ALU.is_ge, fill=-1e30, base=0, pattern=[[1, P]], channel_multiplier=-1).then_inc(sem("cm"), 1)
            GP.affine_select(out=cmask[:, 1], in_=cmask[:, 1], compare_op=ALU.is_ge, fill=-1e30, base=0, pattern=[[-1, P]], channel_multiplier=1).then_inc(sem("cm"), 1)
            def key_value_weights(i):
                for k in range(4):
                    pool.wait_ge(*past(f"v_mmx{k % 2}", 2 * i + k // 2))
                    pool.wait_ge(*past("cm", 3))
                    block_diagonal(BDkv[k % 2][:, 0], 1, 4 * i + k)
                    block_diagonal(BDkv[k % 2][:, 1], 2, 4 * i + k).then_inc(sem("bdkv_ready"), 1)

            def head(i, last_head):
                pool.wait_ge(*past("q_mm", 8 * i))
                pool.wait_ge(*past("cm", 3))
                for k in range(4):
                    block_diagonal(BDq[:, k], 0, 4 * i + k).then_inc(sem("bdq_ready"), 1)
                pool.wait_ge(*past("xb_in", 32 * i + 32))
                for th in range(2):
                    diag = [(n, I, d) for n, (I, d, js) in enumerate(PIECES[th]) if I in js]
                    m = [0]

                    def sum_up(th, x):
                        end = diag[x][0] if x < len(diag) else NPI
                        while todo[0] < end:
                            n, todo[0] = todo[0], todo[0] + 1
                            I, d, js = PIECES[th][n]
                            if I == 0:
                                continue
                            c = slice(P * (js[0] - CBLK - HB_ * th), P * (js[-1] + 1 - CBLK - HB_ * th))
                            o = POFF[th][I, d]
                            a = Sp[:, d, c] if I > 1 else Pm[:, POFF[th][0, d]:POFF[th][0, d] + HALF]
                            pool.wait_ge(*past("p_ready", 2 * NPI * i + (NPI * th + n + 1)))
                            if I == 1:
                                pool.wait_ge(*past("pv_mm", 8 * i + 4 * th))
                                if th == 0:
                                    for q in range(2):
                                        pool.wait_ge(*past(f"v_mmx{q}", 2 * i + 2))
                            else:
                                pool.wait_ge(*past("sums", 2 * NSUM * i + (NSUM * th + m[0])))
                            GP.tensor_tensor(Sp[:, d, c], a, Pm[:, o:o + P * len(js)], ALU.add).then_inc(sem("sums"), 1)
                            m[0] += 1

                    todo = [0]
                    for x, (n, I, d) in enumerate(diag):
                        u = 8 * th + x
                        used = [NPI * th_ + n_ for th_ in range(2) for n_, (I_, d_, js_) in enumerate(PIECES[th_]) if I_ in js_]
                        pool.wait_ge(*past("d_ready", 2 * NPI * i + (used[u - 2] + 1 if u >= 2 else 0)))
                        GP.tensor_tensor(XM[:, u % 2], Xb[:, d, P * (I - CBLK):P * (I - CBLK) + P], cmask[:, d], ALU.add).then_inc(sem("xmask"), 1)
                        sum_up(th, x)
                    sum_up(th, len(diag))
                if not last_head:
                    key_value_weights(i + 1)

            key_value_weights(0)
            with pool.Fori(0, MH - 1) as i:
                head(i, False)
            head(MH - 1, True)


_OUT = "out_0_dram"


def kernel(**inputs):
    import numpy as np
    import concourse.bacc as bacc
    from concourse import mybir as _mybir
    from concourse.bass_utils import run_bass_kernel_spmd as run

    nc = bacc.Bacc("TRN2", target_bir_lowering=False, num_devices=1)
    arrays, A = {}, {}
    for name, a in inputs.items():
        a = np.ascontiguousarray(a)
        arrays[f"in_{name}"] = a
        A[name] = nc.dram_tensor(f"in_{name}", a.shape, _mybir.dt.from_np(a.dtype), kind="ExternalInput").ap()
    out = nc.dram_tensor(_OUT, inputs["x"].shape, F32, kind="ExternalOutput").ap()
    build(nc, A, out)
    return run(nc, [arrays], core_ids=[0]).results[0][_OUT]
```
